# Optimizing a Trainium2 kernel written in Bass

```python
import jax, jax.numpy as jnp
from jax import lax
import numpy as np

D_MODEL = 1024
BATCH = 1
SEQ = 1024
DEPTH = 1
DEC_BATCH = 1
DEC_SEQ = 2048
PAST_LEN = 128

D_MIX = D_MODEL
D_ATT = D_MIX // 2
D_POOL = D_MIX - D_ATT
N_HEADS = 8
QK_NOPE = 64
QK_ROPE = 32
V_DIM = D_ATT // N_HEADS
Q_LORA = 384
KV_LORA = 256
ROPE_THETA = 10000.0
Q_BLOCK = 128
POOL_WINDOWS = (2, 4, 8, 16)
N_POOL_GROUPS = len(POOL_WINDOWS)
POOL_GROUP = D_POOL // N_POOL_GROUPS
N_EXPERTS = 16
CAPACITY_FACTOR = 2
EXPERT_FF = 1024
D_IN = Q_LORA + KV_LORA + QK_ROPE + D_POOL
N_MOD = 6
EPS = 1e-6

kernel_name = "hymba_mla_pool_ec_moe_adaln_encoder"

def rmsnorm(x, gain=None):
    x32 = x.astype(jnp.float32)
    y = (x32 * lax.rsqrt(jnp.mean(x32 * x32, axis=-1, keepdims=True) + EPS)).astype(x.dtype)
    return y if gain is None else y * gain

def rope_tables(s, dtype):
    inv = ROPE_THETA ** (-jnp.arange(0, QK_ROPE, 2, dtype=jnp.float32) / QK_ROPE)
    ang = jnp.arange(s, dtype=jnp.float32)[:, None] * inv[None, :]
    return jnp.cos(ang)[:, None, :].astype(dtype), jnp.sin(ang)[:, None, :].astype(dtype)

def apply_rope(x, cos, sin):
    x1, x2 = jnp.split(x, 2, axis=-1)
    return jnp.concatenate([x1 * cos - x2 * sin, x2 * cos + x1 * sin], axis=-1)

def latent_attention(c_q, c_kv, k_pe, q_norm_g, kv_norm_g, w_uq, w_ukv):
    b, s, _ = c_q.shape
    q = (rmsnorm(c_q, q_norm_g) @ w_uq).reshape(b, s, N_HEADS, QK_NOPE + QK_ROPE)
    kv = (rmsnorm(c_kv, kv_norm_g) @ w_ukv).reshape(b, s, N_HEADS, QK_NOPE + V_DIM)
    cos, sin = rope_tables(s, c_q.dtype)
    q = jnp.concatenate([q[..., :QK_NOPE], apply_rope(q[..., QK_NOPE:], cos, sin)], axis=-1)
    k_pe = apply_rope(k_pe[:, :, None, :], cos, sin)
    k = jnp.concatenate([kv[..., :QK_NOPE],
                         jnp.broadcast_to(k_pe, (b, s, N_HEADS, QK_ROPE))], axis=-1)
    v = kv[..., QK_NOPE:]
    scale = (QK_NOPE + QK_ROPE) ** -0.5
    n_blk = s // Q_BLOCK
    q_blocks = (q * scale).reshape(b, n_blk, Q_BLOCK, N_HEADS, QK_NOPE + QK_ROPE).transpose(1, 0, 2, 3, 4)

    def attend(qb):
        scores = jnp.einsum('bqhd,bkhd->bhqk', qb, k, preferred_element_type=jnp.float32)
        p = jax.nn.softmax(scores, axis=-1).astype(v.dtype)
        return jnp.einsum('bhqk,bkhd->bqhd', p, v)

    o = lax.map(attend, q_blocks)
    return o.transpose(1, 0, 2, 3, 4).reshape(b, s, N_HEADS * V_DIM)

def multiscale_pool(u, w_pool, pool_scale):
    b, s, _ = u.shape
    ug = u.reshape(b, s, N_POOL_GROUPS, POOL_GROUP)
    cs = jnp.pad(jnp.cumsum(ug.astype(jnp.float32), axis=1), ((0, 0), (1, 0), (0, 0), (0, 0)))
    t = jnp.arange(s)
    means = []
    for g, w in enumerate(POOL_WINDOWS):
        lo = jnp.clip(t - w // 2, 0, s)
        hi = jnp.clip(t + (w - w // 2), 0, s)
        cs_g = cs[:, :, g, :]
        count = (hi - lo).astype(jnp.float32)[None, :, None]
        means.append((cs_g[:, hi] - cs_g[:, lo]) / count)
    mean = jnp.stack(means, axis=2)
    d = (mean - ug.astype(jnp.float32)).astype(u.dtype)
    y = jnp.einsum('bsgc,gcd->bsgd', d, w_pool).reshape(b, s, D_POOL)
    return y * pool_scale

def expert_choice_ffn(h, w_router, w_gate, w_up, w_down):
    b, s, d = h.shape
    n = b * s
    cap = CAPACITY_FACTOR * n // N_EXPERTS
    xf = h.reshape(n, d)
    logits = jnp.einsum('nd,de->ne', xf, w_router, preferred_element_type=jnp.float32)
    aff = jax.nn.softmax(logits, axis=-1)
    gates, idx = lax.top_k(aff.T, cap)
    xe = xf[idx]
    a = jnp.einsum('ecd,edf->ecf', xe, w_gate)
    u = jnp.einsum('ecd,edf->ecf', xe, w_up)
    ye = jnp.einsum('ecf,efd->ecd', jax.nn.silu(a) * u, w_down) * gates[..., None].astype(h.dtype)
    out = jnp.zeros_like(xf).at[idx.reshape(-1)].add(ye.reshape(-1, d))
    return out.reshape(b, s, d)

def encoder_layer(x, c, w_ada, b_ada, w_in, q_norm_g, kv_norm_g, w_uq, w_ukv,
                  w_pool, pool_scale, w_out, w_router, w_gate, w_up, w_down):
    mod = jax.nn.silu(c) @ w_ada + b_ada
    sh1, sc1, g1, sh2, sc2, g2 = jnp.split(mod[:, None, :], N_MOD, axis=-1)
    h = rmsnorm(x) * (1 + sc1) + sh1
    z = h @ w_in
    c_q, c_kv, k_pe, u = jnp.split(z, [Q_LORA, Q_LORA + KV_LORA, Q_LORA + KV_LORA + QK_ROPE], axis=-1)
    att = latent_attention(c_q, c_kv, k_pe, q_norm_g, kv_norm_g, w_uq, w_ukv)
    pool = multiscale_pool(u, w_pool, pool_scale)
    x = x + g1 * (jnp.concatenate([att, pool], axis=-1) @ w_out)
    h = rmsnorm(x) * (1 + sc2) + sh2
    return x + g2 * expert_choice_ffn(h, w_router, w_gate, w_up, w_down)

def setup_inputs(seed: int = 0) -> dict:
    key = jax.random.key(seed)
    ks = jax.random.split(key, 20)
    f32 = jnp.float32
    L = DEPTH

    def nrm(k, shape, scale):
        return jax.random.normal(k, shape, f32) * scale

    mod_offset = jnp.array([0.0, 0.0, 1.0, 0.0, 0.0, 1.0], f32)[None, :, None]
    b_ada = (nrm(ks[5], (L, N_MOD, D_MODEL), 0.02) + mod_offset).reshape(L, N_MOD * D_MODEL)
    return {
        "x_prompt": nrm(ks[0], (BATCH, SEQ, D_MODEL), 1.0),
        "x_sample": nrm(ks[1], (DEC_BATCH, DEC_SEQ, D_MODEL), 1.0),
        "c_prompt": nrm(ks[2], (BATCH, D_MODEL), 1.0),
        "c_sample": nrm(ks[3], (DEC_BATCH, D_MODEL), 1.0),
        "w_ada": nrm(ks[4], (L, D_MODEL, N_MOD * D_MODEL), 0.1 * D_MODEL ** -0.5),
        "b_ada": b_ada,
        "w_in": nrm(ks[6], (L, D_MODEL, D_IN), D_MODEL ** -0.5),
        "q_norm_g": 1.0 + nrm(ks[7], (L, Q_LORA), 0.02),
        "kv_norm_g": 1.0 + nrm(ks[8], (L, KV_LORA), 0.02),
        "w_uq": nrm(ks[9], (L, Q_LORA, N_HEADS * (QK_NOPE + QK_ROPE)), Q_LORA ** -0.5),
        "w_ukv": nrm(ks[10], (L, KV_LORA, N_HEADS * (QK_NOPE + V_DIM)), KV_LORA ** -0.5),
        "w_pool": nrm(ks[11], (L, N_POOL_GROUPS, POOL_GROUP, POOL_GROUP), POOL_GROUP ** -0.5),
        "pool_scale": 1.0 + nrm(ks[12], (L, D_POOL), 0.1),
        "w_out": nrm(ks[13], (L, D_MIX, D_MODEL), D_MIX ** -0.5),
        "w_router": nrm(ks[14], (L, D_MODEL, N_EXPERTS), D_MODEL ** -0.5),
        "w_gate": nrm(ks[15], (L, N_EXPERTS, D_MODEL, EXPERT_FF), D_MODEL ** -0.5),
        "w_up": nrm(ks[16], (L, N_EXPERTS, D_MODEL, EXPERT_FF), D_MODEL ** -0.5),
        "w_down": nrm(ks[17], (L, N_EXPERTS, EXPERT_FF, D_MODEL), EXPERT_FF ** -0.5),
        "final_norm_g": 1.0 + nrm(ks[18], (D_MODEL,), 0.02),
    }

def reference(x_prompt, x_sample, c_prompt, c_sample, w_ada, b_ada, w_in, q_norm_g, kv_norm_g,
              w_uq, w_ukv, w_pool, pool_scale, w_out, w_router, w_gate, w_up, w_down, final_norm_g):
    def trunk(x, c):
        for l in range(DEPTH):
            x = encoder_layer(x, c, w_ada[l], b_ada[l], w_in[l], q_norm_g[l], kv_norm_g[l],
                              w_uq[l], w_ukv[l], w_pool[l], pool_scale[l], w_out[l],
                              w_router[l], w_gate[l], w_up[l], w_down[l])
        return rmsnorm(x, final_norm_g)

    y_prompt = trunk(x_prompt, c_prompt)
    y_sample = trunk(x_sample, c_sample)
    return (y_prompt, y_sample)


_drawn_inputs = setup_inputs


def setup_inputs(seed=0):
    import zlib

    import numpy as np

    out = dict(_drawn_inputs(seed))
    spreads = {}
    factors = {'q_norm_g': 8.0, 'kv_norm_g': 8.0, 'final_norm_g': 8.386, 'pool_scale': 5.114}
    for name, (base, spread) in spreads.items():
        noise = np.random.default_rng([zlib.crc32(name.encode()), seed]).standard_normal(out[name].shape)
        drawn = base * np.exp(spread * noise) if base else spread * noise
        out[name] = __import__('jax').numpy.asarray(drawn.astype(out[name].dtype))
    for name, factor in factors.items():
        out[name] = (out[name] * factor).astype(out[name].dtype)
    return out
```

```python
from contextlib import ExitStack

import numpy as np

import concourse.bass as bass
from concourse import mybir

F32 = mybir.dt.float32
F32R = mybir.dt.float32r
BF16 = mybir.dt.bfloat16
I32 = mybir.dt.int32
ALU = mybir.AluOpType
ACT = mybir.ActivationFunctionType
AX = mybir.AxisListType.X

P = 128
BANK = 512
D = 1024
KD = D // P
SEQS = (1024, 2048)
STARTS = (0, 1024)
TOKENS = sum(SEQS)
TILES = TOKENS // P
TILE0 = (0, SEQS[0] // P)
QL, KVL, ROPE, DP = 384, 256, 32, 512
D_IN = QL + KVL + ROPE + DP
HEADS, NOPE, VD = 8, 64, 64
QK = NOPE + ROPE
KQ, KKV = QL // P, KVL // P
KC = KQ + KKV
E = 16
FF = 1024
KF = FF // P
CAPS = tuple(2 * s // E for s in SEQS)
CT = tuple(c // P for c in CAPS)
EPS = 1e-6
WINDOWS = (2, 4, 8, 16)


def sequence(sem, start=0):
    count = [start]

    def step(instruction):
        count[0] += 1
        instruction.then_inc(sem, 1)
        return count[0]

    return step


class Pools:

    before, used = [], []

    def __init__(self, nc, ctx, stage):
        self.nc, self.ctx, self.stage = nc, ctx, stage
        Pools.before, Pools.used = Pools.used, []

    def sb(self, name, shape, dt=F32):
        return self.ctx.enter_context(self.nc.sbuf_tensor(f"{self.stage}_{name}", shape, dt))

    def ps(self, name, shape=(P, BANK), dt=F32):
        return self.ctx.enter_context(self.nc.psum_tensor(f"{self.stage}_{name}", list(shape), dt))

    def sem(self, name):
        s = self.ctx.enter_context(self.nc.semaphore(f"{self.stage}_{name}"))
        Pools.used.append(s.num)
        return s

    def clear_last(self, pool):
        nums = sorted(Pools.before)
        while nums:
            n = 1
            while n < len(nums) and nums[n] == nums[0] + n:
                n += 1
            pool.sem_clear(range(nums[0], nums[0] + n))
            nums = nums[n:]


def modulation(nc, w, keep):
    CH = 4
    J = 6 * KD
    NCH = J // CH
    with ExitStack() as ctx:
        m = Pools(nc, ctx, "ada")
        ct = m.sb("ct", [P, 2, KD])
        cs = m.sb("cs", [P, 2, KD])
        wa = m.sb("wa", [P, 3, KD, CH * P])
        brow = m.sb("brow", [J, P])
        ones = m.sb("ones", [P, P])
        diag = m.sb("diag", [P, 2, P])
        gates = m.sb("gates", [P, 2, 2, D])
        mod_ps = m.ps("mod_ps", [P, J, 2])
        b_ps = m.ps("b_ps", [P, J])
        row_ps = [m.ps(f"row_ps{i}") for i in range(2)]
        small_in = m.sem("small_in")
        w_in = [m.sem(f"w_in{i}") for i in range(3)]
        silu_done = m.sem("silu_done")
        ones_set = m.sem("ones_set")
        b_ready = m.sem("b_ready")
        chunk_done = m.sem("chunk_done")
        cols_done = m.sem("cols_done")
        diag_ready = m.sem("diag_ready")
        row_ready = m.sem("row_ready")
        row_copied = m.sem("row_copied")
        gates_stored = m.sem("gates_stored")
        block = ctx.enter_context(nc.Block())
        w_ada = w["w_ada"][0].rearrange("(p k) n -> p k n", k=KD)

        @block.sync
        def _(sp):
            for g, name in enumerate(("c_prompt", "c_sample")):
                sp.dma_start(ct[:, g, :], w[name][0].rearrange("(p k) -> p k", k=KD)).then_inc(small_in, 16)
            sp.dma_start(brow[:, :], w["b_ada"][0].rearrange("(j p) -> j p", p=P)).then_inc(small_in, 16)
            sp.dma_start(keep["ident"][:, :], w["k_ident"]).then_inc(small_in, 16)
            for n in range(NCH):
                if n >= 3:
                    sp.wait_ge(chunk_done, n - 2)
                sp.dma_start(wa[:, n % 3], w_ada[:, :, n * CH * P:(n + 1) * CH * P]).then_inc(w_in[n % 3], 16)
            sp.wait_ge(row_copied, KD)
            sp.dma_start(w["s_gates"], gates[0:1].rearrange("p a g d -> p (a g d)")).then_inc(gates_stored, 16)
            sp.wait_ge(gates_stored, 16)

        @block.gpsimd
        def _(pool):
            m.clear_last(pool)

        @block.scalar
        def _(act):
            act.wait_ge(small_in, 64)
            nc.scalar.activation(cs[:], ct[:], ACT.Silu).then_inc(silu_done, 1)

        @block.tensor
        def _(pe):
            pe.wait_ge(small_in, 64)
            nc.tensor.transpose(b_ps[:, :], brow[:, :], keep["ident"][0:J, 0:J]).then_inc(b_ready, 1)
            pe.wait_ge(silu_done, 1)
            for n in range(NCH):
                pe.wait_ge(w_in[n % 3], 16 * (n // 3 + 1))
                for j in range(CH):
                    for k in range(KD):
                        mm = nc.tensor.matmul(mod_ps[:, n * CH + j, :], wa[:, n % 3, k, j * P:(j + 1) * P],
                                              cs[:, :, k], start=(k == 0), stop=(k == KD - 1))
                mm.then_inc(chunk_done, 1)
            for n in range(4 * KD):
                pe.wait_ge(diag_ready, n + 1)
                bank = n // 4
                if n % 4 == 0 and bank >= 2:
                    pe.wait_ge(row_copied, bank - 1)
                mm = nc.tensor.matmul(row_ps[bank % 2][:, (n % 4) * P:(n % 4 + 1) * P], ones[:, :],
                                      diag[:, n % 2, :], start=True, stop=True)
                mm.then_inc(row_ready, 1)

        @block.vector
        def _(dve):
            nc.vector.memset(ones[:], 1.0).then_inc(ones_set, 1)
            dve.wait_ge(b_ready, 1)
            nc.vector.tensor_copy(keep["modc"][:, 2, :], b_ps[:, :]).then_inc(cols_done, 1)
            dve.wait_ge(chunk_done, NCH)
            dve.wait_ge(cols_done, 1)
            for g in range(2):
                nc.vector.tensor_tensor(keep["modc"][:, g, :], mod_ps[:, :, g], keep["modc"][:, 2, :],
                                        ALU.add).then_inc(cols_done, 1)
            dve.wait_ge(cols_done, 3)
            for g in range(2):
                for c in (KD, 4 * KD):
                    nc.vector.tensor_scalar(keep["modc"][:, g, c:c + KD], keep["modc"][:, g, c:c + KD], 1.0,
                                            None, ALU.add).then_inc(cols_done, 1)
            dve.wait_ge(small_in, 64)
            dve.wait_ge(ones_set, 1)
            for n in range(4 * KD):
                g, which, k = n // (2 * KD), n // KD % 2, n % KD
                col = (2 * KD, 5 * KD)[which] + k
                if n >= 2:
                    dve.wait_ge(row_ready, n - 1)
                nc.vector.tensor_scalar(diag[:, n % 2, :], keep["ident"][:, :], keep["modc"][:, g, col:col + 1],
                                        None, ALU.mult).then_inc(diag_ready, 1)
                if n % 4 == 3:
                    dve.wait_ge(row_ready, n + 1)
                    dst = gates[:, which, g, (k - 3) * P:(k + 1) * P]
                    nc.vector.tensor_copy(dst, row_ps[n // 4 % 2][:, :]).then_inc(row_copied, 1)


def in_proj(nc, w, keep):
    TB = 4
    NB = TILES // TB
    T = TB * P
    with ExitStack() as ctx:
        m = Pools(nc, ctx, "inp")
        wi = m.sb("wi", [P, KD, D_IN])
        x = m.sb("x", [P, 2, TB, D])
        junk = m.sb("junk", [P, 2, D])
        zjunk = m.sb("zjunk", [P, QL + KVL])
        ht = m.sb("ht", [P, 2, KD, T])
        rope = m.sb("rope", [P, TILES, 2, ROPE])
        ms = m.sb("ms", [P, NB, TB])
        zr = m.sb("zr", [P, 2, QL + KVL])
        zms = m.sb("zms", [P, TILES, 2])
        kr = m.sb("kr", [P, TILES, ROPE])
        tmp = m.sb("tmp", [P, 2, ROPE])
        ut = m.sb("ut", [P, 2, T])
        ct = m.sb("ct", [P, 2, KC * P])
        krt = m.sb("krt", [ROPE, TOKENS])
        gain = m.sb("gain", [P, KC])
        eps = m.sb("eps", [P, 1])
        t_ps = [m.ps(f"t_ps{i}") for i in range(2)]
        q_ps, kv_ps = m.ps("q_ps"), m.ps("kv_ps")
        u_ps = [m.ps(f"u_ps{i}") for i in range(2)]
        c_ps = [m.ps(f"c_ps{i}") for i in range(2)]
        w_loaded = [m.sem(f"w_loaded{k}") for k in range(KD)]
        x_loaded = [m.sem(f"x_loaded{i}") for i in range(2)]
        rope_loaded = m.sem("rope_loaded")
        eps_set = m.sem("eps_set")
        x_squared = m.sem("x_squared")
        x_std = m.sem("x_std")
        x_rstd = m.sem("x_rstd")
        x_normed = m.sem("x_normed")
        xt_ready = m.sem("xt_ready")
        ht_ready = m.sem("ht_ready")
        z_ready = m.sem("z_ready")
        z_squared = m.sem("z_squared")
        z_std = m.sem("z_std")
        z_rstd = m.sem("z_rstd")
        z_normed = m.sem("z_normed")
        roped = m.sem("roped")
        u_ready = m.sem("u_ready")
        u_copied = m.sem("u_copied")
        u_stored = [m.sem(f"u_stored{i}") for i in range(2)]
        ct_ready = m.sem("ct_ready")
        ct_copied = m.sem("ct_copied")
        ct_stored = [m.sem(f"ct_stored{i}") for i in range(2)]
        kr_stored = m.sem("kr_stored")
        block = ctx.enter_context(nc.Block())

        def group(b):
            return 0 if b * TB < TILE0[1] else 1

        @block.sync
        def _(sp):
            def load(b):
                g = group(b)
                row = b * T - STARTS[g]
                src = w[("x_prompt", "x_sample")[g]][0][row:row + T, :]
                sp.dma_start(x[:, b % 2], src.rearrange("(j p) d -> p j d", p=P)).then_inc(x_loaded[b % 2], 16)

            load(0)
            for name, k0, ks in (("q_norm_g", 0, KQ), ("kv_norm_g", KQ, KKV)):
                sp.dma_start(gain[:, k0:k0 + ks], w[name][0].rearrange("(k p) -> p k", p=P),
                             allow_slow_non_contiguous=True).then_inc(rope_loaded, 16)
            sp.dma_start(rope[:], w["k_rope"].rearrange("t p a c -> p t a c")).then_inc(rope_loaded, 16)
            for k in range(KD):
                sp.dma_start(wi[:, k, :], w["w_in"][0][k * P:(k + 1) * P, :]).then_inc(w_loaded[k], 16)
            load(1)
            for n in range(TILES):
                b = n // TB
                if n % TB == 0 and b + 2 < NB:
                    sp.wait_ge(xt_ready, KD * (b + 1))
                    load(b + 2)
                sp.wait_ge(u_copied, n + 1)
                sp.dma_start(w["s_ut"][n % TB, :, b * T:(b + 1) * T], ut[:, n % 2]).then_inc(u_stored[n % 2], 16)
                sp.wait_ge(ct_copied, n + 1)
                sp.dma_start(w["s_ct"][n], ct[:, n % 2]).then_inc(ct_stored[n % 2], 16)
            sp.dma_start(w["s_krt"], krt[:, :]).then_inc(kr_stored, 16)
            for i in range(2):
                sp.wait_ge(u_stored[i], 16 * TILES // 2)
                sp.wait_ge(ct_stored[i], 16 * TILES // 2)
            sp.wait_ge(kr_stored, 16)

        @block.gpsimd
        def _(pool):
            m.clear_last(pool)

        @block.scalar
        def _(act):
            def stats(b):
                act.wait_ge(x_loaded[b % 2], 16 * (b // 2 + 1))
                for j in range(TB):
                    if TB * b + j >= 2:
                        act.wait_ge(x_squared, TB * b + j - 1)
                    sq = nc.scalar.activation(junk[:, j % 2], x[:, b % 2, j, :], ACT.Square, scale=float(D) ** -0.5,
                                              accum_out=ms[:, b, j:j + 1])
                    sq.then_inc(x_squared, 1)
                act.wait_ge(x_squared, TB * (b + 1))
                nc.scalar.activation(ms[:, b, :], ms[:, b, :], ACT.Sqrt, bias=eps[:, 0:1]).then_inc(x_std, 1)

            def evacuate(b, k):
                act.wait_ge(xt_ready, KD * b + k + 1)
                if k == 0 and b >= 2:
                    act.wait_ge(u_ready, TB * (b - 1))
                g = group(b)
                nc.scalar.activation(ht[:, b % 2, k, :], t_ps[k % 2][:, :], ACT.Identity,
                                     bias=keep["modc"][:, g, k:k + 1],
                                     scale=keep["modc"][:, g, KD + k:KD + k + 1]).then_inc(ht_ready, 1)

            def latent_stats(n):
                act.wait_ge(z_ready, n + 1)
                if n:
                    act.wait_ge(z_squared, 2 * n)
                sq = nc.scalar.activation(zjunk[:, 0:QL], q_ps[:, 0:QL], ACT.Square, scale=float(QL) ** -0.5,
                                          accum_out=zms[:, n, 0:1])
                sq.then_inc(z_squared, 1)
                sq = nc.scalar.activation(zjunk[:, QL:QL + KVL], kv_ps[:, 0:KVL], ACT.Square,
                                          scale=float(KVL) ** -0.5, accum_out=zms[:, n, 1:2])
                sq.then_inc(z_squared, 1)
                act.wait_ge(z_squared, 2 * (n + 1))
                nc.scalar.activation(zms[:, n, :], zms[:, n, :], ACT.Sqrt, bias=eps[:, 0:1]).then_inc(z_std, 1)

            def latent_copy(n):
                act.wait_ge(ct_ready, n + 1)
                if n >= 2:
                    act.wait_ge(ct_stored[n % 2], 16 * (n // 2))
                for k in range(KC):
                    nc.scalar.activation(ct[:, n % 2, k * P:(k + 1) * P], c_ps[k // 4][:, k % 4 * P:(k % 4 + 1) * P],
                                         ACT.Copy, scale=gain[:, k:k + 1])
                nc.scalar.activation(krt[:, n * P:(n + 1) * P], c_ps[1][0:ROPE, P:2 * P],
                                     ACT.Copy).then_inc(ct_copied, 1)

            act.wait_ge(eps_set, 1)
            act.wait_ge(rope_loaded, 48)
            stats(0)
            for k in range(KD):
                evacuate(0, k)
            for b in range(NB):
                if b + 1 < NB:
                    stats(b + 1)
                for j in range(TB):
                    latent_stats(TB * b + j)
                    latent_copy(TB * b + j)
                    if b + 1 < NB:
                        evacuate(b + 1, 2 * j)
                        evacuate(b + 1, 2 * j + 1)

        @block.vector
        def _(dve):
            nc.vector.memset(eps[:], EPS).then_inc(eps_set, 1)
            dve.wait_ge(rope_loaded, 48)

            def norm(b):
                dve.wait_ge(x_std, b + 1)
                nc.vector.reciprocal(ms[:, b, :], ms[:, b, :]).then_inc(x_rstd, 1)
                dve.wait_ge(x_rstd, b + 1)
                for j in range(TB):
                    nc.vector.tensor_scalar(x[:, b % 2, j, :], x[:, b % 2, j, :], ms[:, b, j:j + 1], None,
                                            ALU.mult).then_inc(x_normed, 1)

            norm(0)
            for b in range(NB):
                if b + 1 < NB:
                    norm(b + 1)
                for j in range(TB):
                    n = TB * b + j
                    dve.wait_ge(z_squared, 2 * (n + 1))
                    if n:
                        dve.wait_ge(roped, 2 * n)
                    for a in range(2):
                        nc.vector.tensor_tensor(tmp[:, a, :], kv_ps[:, KVL:KVL + ROPE], rope[:, n, a, :],
                                                ALU.mult).then_inc(z_rstd, 1)
                    dve.wait_ge(z_rstd, 3 * n + 2)
                    H = ROPE // 2
                    nc.vector.tensor_tensor(kr[:, n, 0:H], tmp[:, 0, 0:H], tmp[:, 1, H:ROPE],
                                            ALU.subtract).then_inc(roped, 1)
                    nc.vector.tensor_tensor(kr[:, n, H:ROPE], tmp[:, 0, H:ROPE], tmp[:, 1, 0:H],
                                            ALU.add).then_inc(roped, 1)
                    dve.wait_ge(z_std, n + 1)
                    nc.vector.reciprocal(zms[:, n, :], zms[:, n, :]).then_inc(z_rstd, 1)
                    dve.wait_ge(z_rstd, 3 * n + 3)
                    if n >= 2:
                        dve.wait_ge(ct_ready, n - 1)
                    nc.vector.tensor_scalar(zr[:, n % 2, 0:QL], q_ps[:, 0:QL], zms[:, n, 0:1], None,
                                            ALU.mult).then_inc(z_normed, 1)
                    nc.vector.tensor_scalar(zr[:, n % 2, QL:QL + KVL], kv_ps[:, 0:KVL], zms[:, n, 1:2], None,
                                            ALU.mult).then_inc(z_normed, 1)
                    dve.wait_ge(u_ready, n + 1)
                    if n >= 2:
                        dve.wait_ge(u_stored[n % 2], 16 * (n // 2))
                    nc.vector.tensor_copy(ut[:, n % 2, :], u_ps[n % 2][:, :]).then_inc(u_copied, 1)

        @block.tensor
        def _(pe):
            def turn(b, k):
                if k == 0:
                    pe.wait_ge(x_normed, TB * (b + 1))
                if KD * b + k >= 2:
                    pe.wait_ge(ht_ready, KD * b + k - 1)
                for j in range(TB):
                    mm = nc.tensor.transpose(t_ps[k % 2][:, j * P:(j + 1) * P], x[:, b % 2, j, k * P:(k + 1) * P],
                                             keep["ident"][:, :])
                mm.then_inc(xt_ready, 1)

            for k in range(KD):
                turn(0, k)
            for b in range(NB):
                pe.wait_ge(ht_ready, KD * (b + 1))
                for j in range(TB):
                    n = TB * b + j
                    if n:
                        pe.wait_ge(z_normed, 2 * n)
                        pe.wait_ge(roped, 2 * n)
                        pe.wait_ge(z_squared, 2 * n)
                    for ps, c0, cols in ((q_ps, 0, QL), (kv_ps, QL, KVL + ROPE)):
                        for k in range(KD):
                            if n == 0 and c0 == 0:
                                pe.wait_ge(w_loaded[k], 16)
                            mm = nc.tensor.matmul(ps[:, 0:cols], ht[:, b % 2, k, j * P:(j + 1) * P],
                                                  wi[:, k, c0:c0 + cols], start=(k == 0), stop=(k == KD - 1))
                    mm.then_inc(z_ready, 1)
                    if n >= 2:
                        pe.wait_ge(u_copied, n - 1)
                    c0 = QL + KVL + ROPE + j * P
                    for k in range(KD):
                        mm = nc.tensor.matmul(u_ps[n % 2][:, :], wi[:, k, c0:c0 + P], ht[:, b % 2, k, :],
                                              start=(k == 0), stop=(k == KD - 1))
                    mm.then_inc(u_ready, 1)
                    pe.wait_ge(z_normed, 2 * (n + 1))
                    if n:
                        pe.wait_ge(ct_copied, n)
                    for c in range(KC):
                        mm = nc.tensor.transpose(c_ps[c // 4][:, c % 4 * P:(c % 4 + 1) * P],
                                                 zr[:, n % 2, c * P:(c + 1) * P], keep["ident"][:, :])
                    pe.wait_ge(roped, 2 * (n + 1))
                    mm = nc.tensor.transpose(c_ps[1][0:ROPE, P:2 * P], kr[:, n, :], keep["ident"][:, :])
                    mm.then_inc(ct_ready, 1)
                    if b + 1 < NB:
                        turn(b + 1, 2 * j)
                        turn(b + 1, 2 * j + 1)


def attention(nc, w, keep, g):
    S = SEQS[g]
    NT = S // P
    NQB = S // BANK
    CB = BANK // P
    NG = 2 * NQB
    PER = NG * NT
    PAIRS = HEADS // 2
    RING = 4
    MB = 3
    LAG = 3
    QSTEP = NT // 2 + 1
    UNITS = [[u for u in range(NT) if 2 + u * (NT - 4) // NT == kt] for kt in range(NT)]
    WQ_IN = 3 * 16
    SCALE = float(QK) ** -0.5
    t0 = TILE0[g]
    with ExitStack() as ctx:
        m = Pools(nc, ctx, f"att{g}")
        ct = m.sb("ct", [P, NT, KC * P])
        wkv = m.sb("wkv", [P, KKV, HEADS * (NOPE + VD)])
        v_all = m.sb("v_all", [P, NT, HEADS * VD])
        v = m.sb("v", [P, 2, NT, 2 * VD], F32R)
        wq = m.sb("wq", [P, 2, KQ, P])
        wk = m.sb("wk", [P, 2, KKV, NOPE])
        lower = m.sb("lower", [P, max(SEQS) // BANK, BANK])
        rope = lower[:].rearrange("p r n -> p (r n)")
        olo, osum, rden = (lower[0:VD, i, :] for i in range(3))
        qh = m.sb("qh", [P, 2, S], F32R)
        ql = m.sb("ql", [P, 2, S], F32R)
        kh = m.sb("kh", [P, 2, S], F32R)
        kl = m.sb("kl", [P, 2, S], F32R)
        qf = m.sb("qf", [P, BANK])
        upper = m.sb("upper", [P, 2, BANK])
        att, prod = upper[0:VD], upper[NOPE:QK]
        e = m.sb("e", [P, RING, BANK])
        pr = m.sb("pr", [P, RING, 2, BANK], F32R)
        acc = m.sb("acc", [P, 2, BANK])
        ones = m.sb("ones", [P, VD])
        mx = m.sb("mx", [P, CB, NQB])
        nmx = m.sb("nmx", [P, CB])
        s_ps = [m.ps(f"s_ps{i}") for i in range(2)]
        m_ps = [m.ps(f"m_ps{i}") for i in range(MB)]
        o_ps = [m.ps(f"o_ps{i}") for i in range(2)]
        x_ps = m.ps("x_ps")
        ct_in = [m.sem(f"ct_in{i}") for i in range(2)]
        wkv_in = m.sem("wkv_in")
        tabs_in = m.sem("tabs_in")
        kpe_in = m.sem("kpe_in")
        wq_in = [m.sem(f"wq_in{i}") for i in range(2)]
        wk_done = m.sem("wk_done")
        rows_set = m.sem("rows_set")
        v_ready = m.sem("v_ready")
        v_even_copied = m.sem("v_even_copied")
        v_odd_copied = m.sem("v_odd_copied")
        v_hi_done = m.sem("v_hi_done")
        v_lo_done = m.sem("v_lo_done")
        kpe_hi_done = m.sem("kpe_hi_done")
        kpe_lo_done = m.sem("kpe_lo_done")
        k_ready = m.sem("k_ready")
        k_hi_done = m.sem("k_hi_done")
        k_lo_done = m.sem("k_lo_done")
        q_ready = m.sem("q_ready")
        q_nope_copied = m.sem("q_nope_copied")
        q_prod_done = m.sem("q_prod_done")
        q_added = m.sem("q_added")
        q_hi_done = m.sem("q_hi_done")
        q_lo_done = m.sem("q_lo_done")
        unit_ready = m.sem("unit_ready")
        max_part = m.sem("max_part")
        nmx_ready = m.sem("nmx_ready")
        nmx_turned = m.sem("nmx_turned")
        row_done = m.sem("row_done")
        scores_ready = m.sem("scores_ready")
        exp_done = m.sem("exp_done")
        hi_done = m.sem("hi_done")
        lo_done = m.sem("lo_done")
        sum_done = m.sem("sum_done")
        values_done = m.sem("values_done")
        olo_done = m.sem("olo_done")
        den_ready = m.sem("den_ready")
        rden_done = m.sem("rden_done")
        osum_done = m.sem("osum_done")
        att_done = m.sem("att_done")
        att_stored = [m.sem(f"att_stored{i}") for i in range(2)]
        block = ctx.enter_context(nc.Block())

        def over_pairs(eng, body):
            body(0, False)
            with eng.Fori(1, PAIRS - 1) as hp:
                body(hp, False)
            body(PAIRS - 1, True)

        def is_first(hp):
            return isinstance(hp, int) and hp == 0

        def after(b):
            return (b + 1) // NQB % 2, (b + 1) % NQB

        def cols(j):
            return slice(j * BANK, (j + 1) * BANK)

        @block.sync
        def _(sp):
            def load_weights(n, par):
                H = ROPE // 2
                src = w["w_uq"][0].rearrange("(k p) n -> p k n", p=P)
                for dst, at, width in ((0, 0, QK), (QK, QK - H, H), (QK + H, NOPE, H)):
                    sp.dma_start(wq[:, par, :, dst:dst + width], src[:, :, bass.ds(n * QK + at, width)],
                                 ).then_inc(wq_in[par], 16)

            sp.dma_start(wkv[:], w["w_ukv"][0].rearrange("(k p) n -> p k n", p=P)).then_inc(wkv_in, 16)
            for i in range(2):
                half = slice(i * NT // 2, (i + 1) * NT // 2)
                sp.dma_start(ct[:, half], w["s_ct"][t0:t0 + NT][half].rearrange("t p c -> p t c")).then_inc(ct_in[i], 16)
            load_weights(0, 0)
            sp.dma_start(rope[NOPE:P, 0:S], w["k_rope_t"][:, 0:S]).then_inc(tabs_in, 16)
            sp.dma_start(e[NOPE:QK].rearrange("p r n -> p (r n)")[:, 0:S],
                         w["s_krt"][:, STARTS[g]:STARTS[g] + S]).then_inc(kpe_in, 16)
            load_weights(1, 1)

            def body(hp, last):
                for b in range(NG):
                    h, j = b // NQB, b % NQB
                    if j == 0 and not last:
                        sp.wait_ge(q_ready, hp * NG + (h + 1) * NQB)
                        load_weights(hp * 2 + h + 2, h)
                    sp.wait_ge(att_done, hp * NG + b + 1)
                    sp.dma_start(w["s_att"][bass.ds(hp * 2 * VD + h * VD, VD),
                                            STARTS[g] + j * BANK:STARTS[g] + (j + 1) * BANK],
                                 att[:, b % 2, :]).then_inc(att_stored[b % 2], 16)

            over_pairs(sp, body)
            for i in range(2):
                sp.wait_ge(att_stored[i], 16 * PAIRS * NQB)

        @block.tensor
        def _(pe):
            def project_k(out, j, k0):
                for k in range(KKV):
                    mm = nc.tensor.matmul(out[0:NOPE, :], wk[:, k0, k, :], ct_cols(KQ + k, j),
                                          start=(k == 0), stop=(k == KKV - 1))
                mm.then_inc(k_ready, 1)

            def ct_cols(k, j):
                return ct[:, j * CB:(j + 1) * CB, k * P:(k + 1) * P]

            def project_q(par, j):
                for k in range(KQ):
                    mm = nc.tensor.matmul(x_ps[:, :], wq[:, par, k, :], ct_cols(k, j),
                                          start=(k == 0), stop=(k == KQ - 1))
                mm.then_inc(q_ready, 1)

            def unit(par, j, u):
                kb, c = u // CB, u % CB
                at = j * BANK + c * P
                nc.tensor.matmul(m_ps[u % MB][:, :], qh[0:QK, par, at:at + P], kh[0:QK, par, cols(kb)],
                                 start=True, stop=True).then_inc(unit_ready, 1)

            def turn_maxima():
                for c in range(CB):
                    mm = nc.tensor.transpose(x_ps[0:1, c * P:(c + 1) * P], nmx[:, c:c + 1], keep["ident"][:, :])
                mm.then_inc(nmx_turned, 1)

            pe.wait_ge(wkv_in, 16)
            for t in range(NT):
                if t % (NT // 2) == 0:
                    pe.wait_ge(ct_in[t // (NT // 2)], 16)
                if t >= MB:
                    if (t - MB) % 2 == 0:
                        pe.wait_ge(v_even_copied, (t - MB) // 2 + 1)
                    else:
                        pe.wait_ge(v_odd_copied, (t - MB) // 2 + 1)
                for k in range(KKV):
                    rhs = wkv[:, k, :].rearrange("p (h c) -> p h c", h=HEADS)[:, :, NOPE:]
                    mm = nc.tensor.matmul(m_ps[t % MB][:, :], ct[:, t, (KQ + k) * P:(KQ + k + 1) * P], rhs,
                                          start=(k == 0), stop=(k == KKV - 1))
                mm.then_inc(v_ready, 1)
            pe.wait_ge(wq_in[0], WQ_IN)
            for j in range(NQB):
                if j >= 2:
                    pe.wait_ge(k_lo_done, j - 1)
                project_k(o_ps[j % 2], j, 0)
                if j >= 1:
                    pe.wait_ge(q_nope_copied, j)
                    pe.wait_ge(q_prod_done, 2 * j)
                project_q(0, j)
            pe.wait_ge(v_even_copied, NT // 2)
            pe.wait_ge(v_odd_copied, NT // 2)
            pe.wait_ge(q_hi_done, 1)
            pe.wait_ge(k_hi_done, NQB)
            pe.wait_ge(kpe_hi_done, 2)
            for u in range(NT):
                if u >= MB:
                    pe.wait_ge(max_part, u - MB + 1)
                unit(0, 0, u)
            pe.wait_ge(q_nope_copied, NQB)
            pe.wait_ge(q_prod_done, 2 * NQB)
            pe.wait_ge(nmx_ready, 1)
            turn_maxima()
            pe.wait_ge(rows_set, 4)
            pe.wait_ge(kpe_lo_done, 2)

            def body(hp, last):
                def scores(s):
                    b, kt = s // NT, s % NT
                    h, j = b // NQB, b % NQB
                    if kt == 0:
                        pe.wait_ge(row_done, hp * NG + b + 1)
                        if j == 0:
                            pe.wait_ge(k_lo_done, hp * NG + (h + 1) * NQB)
                            pe.wait_ge(q_lo_done, hp * NG + (h + 1) * NQB)
                    if s >= 2:
                        pe.wait_ge(exp_done, hp * PER + s - 1)
                    out = s_ps[s % 2][:, :]
                    k_hi, k_lo = (x[0:QK + 1, h, kt * P:(kt + 1) * P] for x in (kh, kl))
                    q_hi, q_lo = (x[0:QK + 1, h, cols(j)] for x in (qh, ql))
                    nc.tensor.matmul(out, k_hi, q_hi, start=True, stop=False)
                    nc.tensor.matmul(out, k_hi, q_lo, start=False, stop=False)
                    nc.tensor.matmul(out, k_lo, q_hi, start=False, stop=True).then_inc(scores_ready, 1)

                def values(s):
                    b, kt = s // NT, s % NT
                    h, j = b // NQB, b % NQB
                    if kt == 0:
                        if j == 0:
                            pe.wait_ge(v_lo_done, hp * 2 + h + 1)
                        if b >= 2 or not is_first(hp):
                            pe.wait_ge(att_done, hp * NG + max(b - 1, 0))
                    pe.wait_ge(lo_done, hp * PER + s + 1)
                    for a in range(2):
                        mm = nc.tensor.matmul(o_ps[b % 2][:, :], v[:, h, kt, :], pr[:, s % RING, a, :],
                                              start=(kt == 0 and a == 0), stop=(kt == NT - 1 and a == 1))
                    mm.then_inc(values_done, 1)

                def denominators(b):
                    pe.wait_ge(sum_done, (hp * NG + b + 1) * (NT - 1))
                    nc.tensor.matmul(x_ps[0:VD, :], ones[:, :], acc[:, b % 2, :], start=True, stop=True
                                     ).then_inc(den_ready, 1)

                for s in range(PER + LAG):
                    if s < PER:
                        b, kt = s // NT, s % NT
                        h, j = b // NQB, b % NQB
                        project = not (last and h == 1)
                        if kt == NT - 1 and not (last and b == NG - 1):
                            pe.wait_ge(nmx_ready, hp * NG + b + 2)
                            if project:
                                pe.wait_ge(q_nope_copied, hp * NG + NQB + b + 1)
                                pe.wait_ge(q_prod_done, 2 * (hp * NG + NQB + b + 1))
                            else:
                                pe.wait_ge(rden_done, hp * NG + b)
                            turn_maxima()
                        scores(s)
                        if kt == 0 and project:
                            if j == 0:
                                pe.wait_ge(wq_in[1 - h], WQ_IN * (hp + 1 + h))
                                pe.wait_ge(wk_done, hp * 2 + h + 2)
                            if b == 0 and not is_first(hp):
                                pe.wait_ge(rden_done, hp * NG)
                            project_k(x_ps, j, 1 - h)
                        if not (last and b == NG - 1):
                            par, nj = after(b)
                            for u in UNITS[kt]:
                                if nj == 0 and u % CB == 0:
                                    pe.wait_ge(k_hi_done, hp * NG + (h + 1) * NQB + u // CB + 1)
                                    if u == 0:
                                        pe.wait_ge(q_hi_done, hp * NG + (h + 1) * NQB + 1)
                                pe.wait_ge(max_part, (hp * NG + b + 1) * NT + max(u - MB + 1, 0))
                                unit(par, nj, u)
                    if s >= LAG:
                        values(s - LAG)
                    if s < PER and kt == LAG and b >= 1:
                        if project:
                            pe.wait_ge(k_lo_done, hp * NG + NQB + b + 1)
                        else:
                            pe.wait_ge(row_done, hp * NG + b + 1)
                        denominators(b - 1)
                    if s < PER and kt == QSTEP and project:
                        if b >= 1:
                            pe.wait_ge(rden_done, hp * NG + b)
                        else:
                            pe.wait_ge(k_lo_done, hp * NG + NQB + b + 1)
                        project_q(1 - h, j)
                if not last:
                    pe.wait_ge(row_done, (hp + 1) * NG + 1)
                else:
                    pe.wait_ge(rden_done, (hp + 1) * NG - 1)
                denominators(NG - 1)

            over_pairs(pe, body)

        @block.scalar
        def _(act):
            def k_high(src, par, j):
                nc.scalar.activation(kh[0:NOPE, par, cols(j)], src[0:NOPE, :], ACT.Copy).then_inc(k_hi_done, 1)

            def q_nope():
                nc.scalar.activation(qf[0:NOPE, :], x_ps[0:NOPE, :], ACT.Copy).then_inc(q_nope_copied, 1)

            def q_high(par, j):
                nc.scalar.activation(qh[0:QK, par, cols(j)], qf[0:QK, :], ACT.Copy).then_inc(q_hi_done, 1)

            def v_high(n, par):
                nc.scalar.activation(v[:, par, :, 0:VD], v_all[:, :, bass.ds(n * VD, VD)],
                                     ACT.Copy).then_inc(v_hi_done, 1)

            def max_row(par, j):
                nc.scalar.activation(qh[QK:QK + 1, par, cols(j)], x_ps[0:1, :], ACT.Copy).then_inc(row_done, 1)

            act.wait_ge(kpe_in, 16)
            for par in range(2):
                nc.scalar.activation(kh[NOPE:QK, par, :], e[NOPE:QK].rearrange("p r n -> p (r n)")[:, 0:S],
                                     ACT.Copy).then_inc(kpe_hi_done, 1)
            for t in range(0, NT, 2):
                act.wait_ge(v_ready, t + 1)
                nc.scalar.activation(v_all[:, t, :], m_ps[t % MB][:, :], ACT.Copy).then_inc(v_even_copied, 1)
            for j in range(NQB):
                act.wait_ge(k_ready, j + 1)
                k_high(o_ps[j % 2], 0, j)
                act.wait_ge(q_ready, j + 1)
                if j >= 1:
                    act.wait_ge(q_lo_done, j)
                q_nope()
                act.wait_ge(q_nope_copied, j + 1)
                act.wait_ge(q_added, j + 1)
                q_high(0, j)
            act.wait_ge(v_even_copied, NT // 2)
            act.wait_ge(v_odd_copied, NT // 2)
            v_high(0, 0)
            act.wait_ge(nmx_turned, 1)
            max_row(0, 0)
            act.wait_ge(kpe_lo_done, 2)

            def body(hp, last):
                def exps(s):
                    act.wait_ge(scores_ready, hp * PER + s + 1)
                    if s >= RING:
                        old = s - RING
                        act.wait_ge(lo_done, hp * PER + old + 1)
                        act.wait_ge(sum_done, (hp * NG + old // NT) * (NT - 1) + max(old % NT, 1))
                    elif s == 0 and not is_first(hp):
                        act.wait_ge(lo_done, hp * PER)
                        act.wait_ge(sum_done, hp * NG * (NT - 1))
                    nc.scalar.activation(e[:, s % RING, :], s_ps[s % 2][:, :], ACT.Exp, scale=SCALE).then_inc(exp_done, 1)

                def high(s):
                    act.wait_ge(exp_done, hp * PER + s + 1)
                    if s >= RING or not is_first(hp):
                        act.wait_ge(values_done, hp * PER + max(s - RING + 1, 0))
                    nc.scalar.activation(pr[:, s % RING, 0, :], e[:, s % RING, :], ACT.Copy).then_inc(hi_done, 1)

                def output_low(b):
                    act.wait_ge(values_done, hp * PER + (b + 1) * NT)
                    if b >= 1 or not is_first(hp):
                        act.wait_ge(osum_done, hp * NG + b)
                    nc.scalar.activation(olo, o_ps[b % 2][VD:P, :], ACT.Copy).then_inc(olo_done, 1)

                for s in range(PER):
                    b, kt = s // NT, s % NT
                    h, j = b // NQB, b % NQB
                    project = not (last and h == 1)
                    if kt == NT - 1 and not (last and b == NG - 1):
                        act.wait_ge(nmx_turned, hp * NG + b + 2)
                        max_row(*after(b))
                    exps(s)
                    if s >= 1:
                        high(s - 1)
                    if kt == 1 and project:
                        act.wait_ge(k_ready, hp * NG + NQB + b + 1)
                        k_high(x_ps, 1 - h, j)
                    if kt == LAG + 1 and b >= 1:
                        output_low(b - 1)
                    if project and kt == QSTEP + 1:
                        act.wait_ge(q_ready, hp * NG + NQB + b + 1)
                        act.wait_ge(q_lo_done, hp * NG + NQB + b)
                        q_nope()
                    if project and kt == NT - 1:
                        act.wait_ge(q_nope_copied, hp * NG + NQB + b + 1)
                        act.wait_ge(q_added, hp * NG + NQB + b + 1)
                        q_high(1 - h, j)
                    if project and j == 1 and kt == 0:
                        if h == 1 or not is_first(hp):
                            act.wait_ge(values_done, hp * PER + h * (PER // 2))
                        v_high(hp * 2 + h + 1, 1 - h)
                high(PER - 1)
                output_low(NG - 1)

            over_pairs(act, body)

        @block.vector
        def _(dve):
            def k_low(src, par, j):
                nc.vector.tensor_tensor(kl[0:NOPE, par, cols(j)], src[0:NOPE, :],
                                        kh[0:NOPE, par, cols(j)].bitcast(F32), ALU.subtract).then_inc(k_lo_done, 1)

            def q_products(j):
                for a in range(2):
                    rows = slice(NOPE + a * ROPE, NOPE + (a + 1) * ROPE)
                    nc.vector.tensor_tensor(prod[:, a, :], x_ps[rows, :], rope[rows, cols(j)],
                                            ALU.mult).then_inc(q_prod_done, 1)

            def v_low(n, par):
                nc.vector.tensor_tensor(v[:, par, :, VD:2 * VD], v_all[:, :, bass.ds(n * VD, VD)],
                                        v[:, par, :, 0:VD].bitcast(F32), ALU.subtract).then_inc(v_lo_done, 1)

            def reduce_unit(u):
                nc.vector.tensor_reduce(mx[:, u % CB, u // CB:u // CB + 1], m_ps[u % MB][:, :], AX,
                                        ALU.max).then_inc(max_part, 1)

            def combine():
                nc.vector.tensor_reduce(nmx[:, :], mx[:], AX, ALU.max, negate=True).then_inc(nmx_ready, 1)

            def k_weights(n, par):
                nc.vector.tensor_copy(wk[:, par], wkv[:, :, bass.ds(n * (NOPE + VD), NOPE)]).then_inc(wk_done, 1)

            nc.vector.memset(ones[:, :], 1.0).then_inc(rows_set, 1)
            dve.wait_ge(wkv_in, 16)
            k_weights(0, 0)
            k_weights(1, 1)
            for t in range(1, NT, 2):
                dve.wait_ge(v_ready, t + 1)
                nc.vector.tensor_copy(v_all[:, t, :], m_ps[t % MB][:, :]).then_inc(v_odd_copied, 1)
            dve.wait_ge(tabs_in, 16)
            for j in range(NQB):
                dve.wait_ge(k_hi_done, j + 1)
                k_low(o_ps[j % 2], 0, j)
                dve.wait_ge(q_ready, j + 1)
                if j >= 1:
                    dve.wait_ge(q_added, j)
                q_products(j)
            for u in range(NT):
                dve.wait_ge(unit_ready, u + 1)
                reduce_unit(u)
            dve.wait_ge(max_part, NT)
            combine()
            for par in range(2):
                dve.wait_ge(kpe_hi_done, par + 1)
                nc.vector.tensor_tensor(kl[NOPE:QK, par, :], e[NOPE:QK].rearrange("p r n -> p (r n)")[:, 0:S],
                                        kh[NOPE:QK, par, :].bitcast(F32), ALU.subtract).then_inc(kpe_lo_done, 1)
            dve.wait_ge(v_hi_done, 1)
            v_low(0, 0)

            def body(hp, last):
                def low(s):
                    dve.wait_ge(hi_done, hp * PER + s + 1)
                    nc.vector.tensor_tensor(pr[:, s % RING, 1, :], e[:, s % RING, :],
                                            pr[:, s % RING, 0, :].bitcast(F32), ALU.subtract).then_inc(lo_done, 1)

                def inverse(b):
                    dve.wait_ge(den_ready, hp * NG + b + 1)
                    if b >= 1 or not is_first(hp):
                        dve.wait_ge(att_done, hp * NG + b)
                    nc.vector.reciprocal(rden, x_ps[0:VD, :]).then_inc(rden_done, 1)

                def output_sum(b):
                    dve.wait_ge(olo_done, hp * NG + b + 1)
                    nc.vector.tensor_tensor(osum, o_ps[b % 2][0:VD, :], olo, ALU.add).then_inc(osum_done, 1)

                def output(b):
                    dve.wait_ge(osum_done, hp * NG + b + 1)
                    dve.wait_ge(rden_done, hp * NG + b + 1)
                    if b >= 2 or not is_first(hp):
                        dve.wait_ge(att_stored[b % 2], 16 * (hp * NQB + b // 2))
                    nc.vector.tensor_tensor(att[:, b % 2, :], osum, rden, ALU.mult).then_inc(att_done, 1)

                for s in range(PER):
                    b, kt = s // NT, s % NT
                    h, j = b // NQB, b % NQB
                    project = not (last and h == 1)
                    if s >= 1:
                        low(s - 1)
                    if kt == 1 and project:
                        dve.wait_ge(k_hi_done, hp * NG + NQB + b + 1)
                        k_low(x_ps, 1 - h, j)
                    if kt == 2 and project and j == NQB - 1 and not (last and h == 0):
                        k_weights(hp * 2 + h + 2, h)
                    if b >= 1 and kt == LAG + 1:
                        inverse(b - 1)
                    if b >= 1 and kt == LAG + 2:
                        output_sum(b - 1)
                    if b >= 1 and kt == LAG + 3:
                        output(b - 1)
                    if project and kt == QSTEP + 1:
                        dve.wait_ge(q_ready, hp * NG + NQB + b + 1)
                        dve.wait_ge(q_added, hp * NG + NQB + b)
                        q_products(j)
                    if project and j == 1 and kt == 1:
                        dve.wait_ge(v_hi_done, hp * 2 + h + 2)
                        v_low(hp * 2 + h + 1, 1 - h)
                    if not (last and b == NG - 1):
                        for u in UNITS[kt]:
                            dve.wait_ge(unit_ready, (hp * NG + b + 1) * NT + u + 1)
                            reduce_unit(u)
                        if kt == NT - 2:
                            dve.wait_ge(max_part, (hp * NG + b + 2) * NT)
                            dve.wait_ge(nmx_turned, hp * NG + b + 1)
                            combine()
                low(PER - 1)
                output_sum(NG - 1)
                inverse(NG - 1)
                output(NG - 1)

            over_pairs(dve, body)

        @block.gpsimd
        def _(pool):
            def q_sum():
                nc.gpsimd.tensor_tensor(qf[NOPE:QK, :], prod[:, 0, :], prod[:, 1, :],
                                        ALU.add).then_inc(q_added, 1)

            def q_low(par, j):
                nc.gpsimd.tensor_tensor(ql[0:QK, par, cols(j)], qf[0:QK, :], qh[0:QK, par, cols(j)].bitcast(F32),
                                        ALU.subtract).then_inc(q_lo_done, 1)

            m.clear_last(pool)
            for rows, value in ((kh, 1.0), (kl, 0.0), (ql, 0.0)):
                nc.gpsimd.memset(rows[QK:QK + 1].bitcast(F32), value).then_inc(rows_set, 1)
            for j in range(NQB):
                pool.wait_ge(q_prod_done, 2 * (j + 1))
                if j >= 1:
                    pool.wait_ge(q_lo_done, j)
                q_sum()
                pool.wait_ge(q_hi_done, j + 1)
                q_low(0, j)

            def body(hp, last):
                for s in range(PER):
                    b, kt = s // NT, s % NT
                    h, j = b // NQB, b % NQB
                    project = not (last and h == 1)
                    if kt == 1:
                        pool.wait_ge(exp_done, hp * PER + s + 1)
                        pool.wait_ge(q_lo_done, hp * NG + NQB + min(b, NG // 2 if last else b))
                        if b >= 2 or not is_first(hp):
                            pool.wait_ge(den_ready, hp * NG + max(b - 1, 0))
                        nc.gpsimd.tensor_tensor(acc[:, b % 2, :], e[:, (s - 1) % RING, :], e[:, s % RING, :],
                                                ALU.add).then_inc(sum_done, 1)
                    elif kt > 1:
                        pool.wait_ge(exp_done, hp * PER + s + 1)
                        if project and kt == NT - 1:
                            pool.wait_ge(q_added, hp * NG + NQB + b + 1)
                        pool.wait_ge(sum_done, (hp * NG + b) * (NT - 1) + kt - 1)
                        nc.gpsimd.tensor_tensor(acc[:, b % 2, :], acc[:, b % 2, :], e[:, s % RING, :],
                                                ALU.add).then_inc(sum_done, 1)
                    if project and kt == NT - 2:
                        pool.wait_ge(q_prod_done, 2 * (hp * NG + NQB + b + 1))
                        pool.wait_ge(sum_done, (hp * NG + b) * (NT - 1) + kt)
                        q_sum()
                    if project and kt == NT - 1:
                        pool.wait_ge(q_hi_done, hp * NG + NQB + b + 1)
                        pool.wait_ge(sum_done, (hp * NG + b) * (NT - 1) + kt)
                        q_low(1 - h, j)

            over_pairs(pool, body)


def pooling(nc, w, keep):
    W = len(WINDOWS)
    PAD = max(WINDOWS) // 2
    WIDTH = max(SEQS) + 2 * PAD
    jobs = [(g, c) for g in (1, 0) for c in range(W)]
    with ExitStack() as ctx:
        m = Pools(nc, ctx, "mix")
        u = m.sb("u", [P, 2, WIDTH])
        sums = m.sb("sums", [P, 2, WIDTH])
        diff = m.sb("diff", [P, 2, max(SEQS)])
        edge = m.sb("edge", [P, W, 2 * PAD])
        ends = m.sb("ends", [P, 2 * PAD])
        out = m.sb("out", [P, 2, max(SEQS)])
        wp = m.sb("wp", [P, W, P])
        scale = m.sb("scale", [P, W])
        y_ps = [m.ps(f"y_ps{i}") for i in range(2)]
        tabs_in = m.sem("tabs_in")
        pads_set = m.sem("pads_set")
        u_in = [m.sem(f"u_in{i}") for i in range(2)]
        summed = m.sem("summed")
        diff_ready = m.sem("diff_ready")
        y_ready = m.sem("y_ready")
        y_copied = m.sem("y_copied")
        stored = [m.sem(f"stored{i}") for i in range(2)]
        block = ctx.enter_context(nc.Block())
        banks = [SEQS[g] // BANK for g, _ in jobs]

        @block.gpsimd
        def _(pool):
            m.clear_last(pool)

        @block.sync
        def _(sp):
            sp.dma_start(wp[:], w["w_pool"][0].rearrange("g c d -> c g d")).then_inc(tabs_in, 16)
            sp.dma_start(edge[:].rearrange("p a b -> p (a b)"), w["k_edge"].partition_broadcast(P)).then_inc(tabs_in, 16)
            sp.dma_start(scale[:, :], w["pool_scale"][0].rearrange("(g p) -> p g", p=P),
                         allow_slow_non_contiguous=True).then_inc(tabs_in, 16)
            sp.wait_ge(pads_set, 2)
            for n, (g, c) in enumerate(jobs):
                if n >= 2:
                    sp.wait_ge(diff_ready, n - 1)
                S = SEQS[g]
                if n in (W, W + 1):
                    sp.wait_ge(pads_set, 3 + n - W)
                sp.dma_start(u[:, n % 2, PAD:PAD + S], w["s_ut"][c, :, STARTS[g]:STARTS[g] + S]).then_inc(u_in[n % 2], 16)

        @block.vector
        def _(dve):
            step = sequence(summed)
            for i in range(2):
                nc.vector.memset(u[:, i, :], 0.0).then_inc(pads_set, 1)
            dve.wait_ge(tabs_in, 48)
            for n, (g, c) in enumerate(jobs):
                S = SEQS[g]
                x, a = u[:, n % 2], sums
                dve.wait_ge(u_in[n % 2], 16 * (n // 2 + 1))
                done = step(nc.vector.tensor_tensor(a[:, 0, 1:S + 2 * PAD], x[:, 0:S + 2 * PAD - 1],
                                                    x[:, 1:S + 2 * PAD], ALU.add))
                for lev in range(1, c + 1):
                    r = 1 << (lev - 1)
                    lo, hi = 2 * r, S + 2 * PAD - 2 * r + 1
                    src, dst = a[:, (lev - 1) % 2], a[:, lev % 2]
                    dve.wait_ge(summed, done)
                    done = step(nc.vector.tensor_tensor(dst[:, lo:hi], src[:, lo - r:hi - r], src[:, lo + r:hi + r],
                                                        ALU.add))
                total = a[:, c % 2]
                dve.wait_ge(summed, done)
                if n >= 2:
                    dve.wait_ge(y_ready, sum(banks[:n - 1]))
                step(nc.vector.scalar_tensor_tensor(diff[:, n % 2, PAD:S - PAD], total[:, 2 * PAD:S],
                                                    1.0 / WINDOWS[c], x[:, 2 * PAD:S], ALU.mult, ALU.subtract))
                for k, at in enumerate((0, S - PAD)):
                    done = step(nc.vector.tensor_tensor(ends[:, k * PAD:(k + 1) * PAD],
                                                        total[:, PAD + at:2 * PAD + at],
                                                        edge[:, c, k * PAD:(k + 1) * PAD], ALU.mult))
                dve.wait_ge(summed, done)
                for k, at in enumerate((0, S - PAD)):
                    last = nc.vector.tensor_tensor(diff[:, n % 2, at:at + PAD], ends[:, k * PAD:(k + 1) * PAD],
                                                   x[:, PAD + at:2 * PAD + at], ALU.subtract)
                last.then_inc(diff_ready, 1)
                dve.wait_ge(diff_ready, n + 1)
                if n in (W - 2, W - 1):
                    nc.vector.memset(x[:, PAD + SEQS[0]:], 0.0).then_inc(pads_set, 1)

        @block.tensor
        def _(pe):
            pe.wait_ge(tabs_in, 48)
            q = 0
            for n, (g, c) in enumerate(jobs):
                pe.wait_ge(diff_ready, n + 1)
                for b in range(banks[n]):
                    if q >= 2:
                        pe.wait_ge(y_copied, q - 1)
                    nc.tensor.matmul(y_ps[q % 2][:, :], wp[:, c, :], diff[:, n % 2, b * BANK:(b + 1) * BANK],
                                     start=True, stop=True).then_inc(y_ready, 1)
                    q += 1

        @block.scalar
        def _(act):
            act.wait_ge(tabs_in, 48)
            q = 0
            for n, (g, c) in enumerate(jobs):
                if n >= 2:
                    act.wait_ge(stored[n % 2], 16 * (n // 2))
                for b in range(banks[n]):
                    act.wait_ge(y_ready, q + 1)
                    nc.scalar.activation(out[:, n % 2, b * BANK:(b + 1) * BANK], y_ps[q % 2][:, :], ACT.Copy,
                                         scale=scale[:, c:c + 1]).then_inc(y_copied, 1)
                    q += 1
                act.wait_ge(y_copied, q)
                act.dma_start(w["s_pool"][c, :, STARTS[g]:STARTS[g] + SEQS[g]],
                              out[:, n % 2, 0:SEQS[g]]).then_inc(stored[n % 2], 16)
            for i in range(2):
                act.wait_ge(stored[i], 16 * len(jobs) // 2)


def out_proj(nc, w, keep):
    BLOCKS = TILES // 2
    SPLIT = TILE0[1] // 2
    KA = HEADS * VD // P
    with ExitStack() as ctx:
        m = Pools(nc, ctx, "outp")
        wraw = m.sb("wraw", [P, 2, D])
        wh = m.sb("wh", [P, KD, D], F32R)
        wl = m.sb("wl", [P, KD, D], F32R)
        wr = m.sb("wr", [P, KD, E])
        g1 = m.sb("g1", [P, 2, D])
        mix = m.sb("mix", [P, 2, KD, P])
        mh = m.sb("mh", [P, 2, KD, P], F32R)
        ml = m.sb("ml", [P, 2, KD, P], F32R)
        x = m.sb("x", [P, 2, D])
        gated = m.sb("gated", [P, 2, D])
        x1 = m.sb("x1", [P, 2, D])
        xn = m.sb("xn", [P, 2, D])
        junk = m.sb("junk", [P, 2, D])
        ms = m.sb("ms", [P, 2])
        eps = m.sb("eps", [P, 1])
        h2 = m.sb("h2", [P, KD, 2 * P])
        o_ps = m.ps("o_ps", [P, 2, 2, BANK])
        x_ps = m.ps("x_ps", [P, 2, BANK])
        l_ps = m.ps("l_ps")
        eps_set = m.sem("eps_set")
        w_in = [m.sem(f"w_in{i}") for i in range(2)]
        w_hi_done = m.sem("w_hi_done")
        w_lo_done = m.sem("w_lo_done")
        tabs_in = m.sem("tabs_in")
        mix_in = [m.sem(f"mix_in{i}") for i in range(2)]
        x_in = [m.sem(f"x_in{i}") for i in range(2)]
        mix_hi_done = m.sem("mix_hi_done")
        mix_lo_done = m.sem("mix_lo_done")
        o_ready = m.sem("o_ready")
        gate_done = m.sem("gate_done")
        x1_done = m.sem("x1_done")
        squared = m.sem("squared")
        std_done = m.sem("std_done")
        rstd_done = m.sem("rstd_done")
        xn_done = m.sem("xn_done")
        x1_stored = [m.sem(f"x1_stored{i}") for i in range(2)]
        xn_stored = [m.sem(f"xn_stored{i}") for i in range(2)]
        xn_turned = m.sem("xn_turned")
        h2_done = m.sem("h2_done")
        logits_ready = m.sem("logits_ready")
        logits_copied = m.sem("logits_copied")
        block = ctx.enter_context(nc.Block())

        def over_blocks(eng, body):
            body(0, 0, None)
            body(1, 0, 0)
            with eng.Fori(2, SPLIT) as r:
                body(r, 0, 0)
            body(SPLIT, 1, 0)
            with eng.Fori(SPLIT + 1, BLOCKS) as r:
                body(r, 1, 1)

        @block.sync
        def _(sp):
            def body(r, g, before):
                for u in range(2):
                    if before is not None:
                        sp.wait_ge(mix_lo_done, 2 * r - (1 - u))
                    sp.dma_start(mix[:, u, 0:KA], w["s_att"][:, bass.ds(r * 2 * P + u * P, P)]
                                 .rearrange("(c p) t -> p c t", p=P)).then_inc(mix_in[u], 16)
                    sp.dma_start(mix[:, u, KA:KD], w["s_pool"][:, :, bass.ds(r * 2 * P + u * P, P)]
                                 .rearrange("c p t -> p c t")).then_inc(mix_in[u], 16)
                for u in range(2):
                    if before is not None:
                        sp.wait_ge(x1_done, 2 * r - (1 - u))
                    src = w[("x_prompt", "x_sample")[g]][0]
                    sp.dma_start(x[:, u, :], src[bass.ds(r * 2 * P + u * P - STARTS[g], P), :]).then_inc(x_in[u], 16)

            for k in range(2):
                sp.dma_start(wraw[:, k], w["w_out"][0][k * P:(k + 1) * P, :]).then_inc(w_in[k], 16)
            sp.dma_start(wr[:], w["w_router"][0].rearrange("(k p) e -> p k e", p=P)).then_inc(tabs_in, 16)
            for g in range(2):
                sp.dma_start(g1[:, g, :], w["s_gates"][0, g * D:(g + 1) * D].partition_broadcast(P)).then_inc(tabs_in, 16)
            for k in range(2, KD):
                sp.wait_ge(w_lo_done, k - 1)
                sp.dma_start(wraw[:, k % 2], w["w_out"][0][k * P:(k + 1) * P, :]).then_inc(w_in[k % 2], 16)
            over_blocks(sp, body)

        @block.gpsimd
        def _(pool):
            m.clear_last(pool)
            def body(r, g, before):
                for u in range(2):
                    pool.wait_ge(gate_done, 2 * r + u + 1)
                    pool.wait_ge(x_in[u], 16 * r + 16)
                    if before is not None:
                        pool.wait_ge(xn_done, 2 * r)
                        pool.wait_ge(x1_stored[u], 16 * r)
                    nc.gpsimd.tensor_tensor(x1[:, u, :], gated[:, u, :], x[:, u, :], ALU.add).then_inc(x1_done, 1)

            over_blocks(pool, body)

        @block.tensor
        def _(pe):
            def turn_xn(r):
                pe.wait_ge(xn_done, 2 * r + 2)
                for c in range(KD // 2):
                    if c >= 2:
                        pe.wait_ge(h2_done, KD * r + 2 * (c - 1))
                    for k in (2 * c, 2 * c + 1):
                        for u in range(2):
                            mm = nc.tensor.transpose(x_ps[:, c % 2, (k % 2 * 2 + u) * P:(k % 2 * 2 + u + 1) * P],
                                                     xn[:, u, k * P:(k + 1) * P], keep["ident"][:, :])
                    mm.then_inc(xn_turned, 1)

            def route(r):
                pe.wait_ge(h2_done, KD * r + KD)
                for k in range(KD):
                    mm = nc.tensor.matmul(l_ps[0:E, 0:2 * P], wr[:, k, :], h2[:, k, :],
                                          start=(k == 0), stop=(k == KD - 1))
                mm.then_inc(logits_ready, 1)

            def body(r, g, before):
                if before is not None:
                    turn_xn(r - 1)
                if before is not None:
                    if not isinstance(r, int) or r >= 2:
                        pe.wait_ge(logits_copied, r - 1)
                    route(r - 1)
                for u in range(2):
                    pe.wait_ge(mix_lo_done, 2 * r + u + 1)
                    if before is not None:
                        pe.wait_ge(gate_done, 2 * r - (1 - u))
                    for c in range(2):
                        out = o_ps[:, u, c, :]
                        for k in range(KD):
                            if before is None and u == 0 and c == 0:
                                pe.wait_ge(w_lo_done, k + 1)
                            hi, lo = wh[:, k, c * BANK:(c + 1) * BANK], wl[:, k, c * BANK:(c + 1) * BANK]
                            nc.tensor.matmul(out, mh[:, u, k, :], hi, start=(k == 0), stop=False)
                            nc.tensor.matmul(out, mh[:, u, k, :], lo, start=False, stop=False)
                            mm = nc.tensor.matmul(out, ml[:, u, k, :], hi, start=False, stop=(k == KD - 1))
                    mm.then_inc(o_ready, 1)

            pe.wait_ge(tabs_in, 48)
            over_blocks(pe, body)
            turn_xn(BLOCKS - 1)
            pe.wait_ge(logits_copied, BLOCKS - 1)
            route(BLOCKS - 1)

        @block.scalar
        def _(act):
            def modulate(r, g):
                for u in range(2):
                    act.wait_ge(xn_done, 2 * r + u + 1)
                    act.dma_start(w["s_xn"][bass.ds(r * 2 * P + u * P, P), :], xn[:, u, :]).then_inc(xn_stored[u], 16)
                for k in range(KD):
                    act.wait_ge(xn_turned, KD // 2 * r + k // 2 + 1)
                    if k == 0 and (not isinstance(r, int) or r >= 1):
                        act.wait_ge(logits_ready, r)
                    nc.scalar.activation(h2[:, k, :], x_ps[:, k // 2 % 2, k % 2 * 2 * P:(k % 2 + 1) * 2 * P],
                                         ACT.Identity, bias=keep["modc"][:, g, 3 * KD + k:3 * KD + k + 1],
                                         scale=keep["modc"][:, g, 4 * KD + k:4 * KD + k + 1]).then_inc(h2_done, 1)

            def body(r, g, before):
                if before is not None:
                    modulate(r - 1, before)
                for u in range(2):
                    act.wait_ge(mix_in[u], 32 * r + 32)
                    if before is not None:
                        act.wait_ge(o_ready, 2 * r - (1 - u))
                    nc.scalar.activation(mh[:, u], mix[:, u], ACT.Copy).then_inc(mix_hi_done, 1)
                for u in range(2):
                    act.wait_ge(x1_done, 2 * r + u + 1)
                    if before is not None:
                        act.wait_ge(squared, 2 * r - (1 - u))
                        act.wait_ge(xn_done, 2 * r)
                    nc.scalar.activation(junk[:, u, :], x1[:, u, :], ACT.Square, scale=float(D) ** -0.5,
                                         accum_out=ms[:, u:u + 1]).then_inc(squared, 1)
                for u in range(2):
                    act.dma_start(w["s_x"][bass.ds(r * 2 * P + u * P, P), :], x1[:, u, :]).then_inc(x1_stored[u], 16)
                act.wait_ge(squared, 2 * r + 2)
                nc.scalar.activation(ms[:, :], ms[:, :], ACT.Sqrt, bias=eps[:, 0:1]).then_inc(std_done, 1)

            act.wait_ge(eps_set, 1)
            for k in range(KD):
                act.wait_ge(w_in[k % 2], 16 * (k // 2 + 1))
                nc.scalar.activation(wh[:, k, :], wraw[:, k % 2, :], ACT.Copy).then_inc(w_hi_done, 1)
            over_blocks(act, body)
            modulate(BLOCKS - 1, 1)
            for u in range(2):
                act.wait_ge(x1_stored[u], 16 * BLOCKS)
                act.wait_ge(xn_stored[u], 16 * BLOCKS)

        @block.vector
        def _(dve):
            def copy_logits(r):
                dve.wait_ge(logits_ready, r + 1)
                nc.vector.tensor_copy(keep["logits"][:, bass.ds(r * 2 * P, 2 * P)],
                                      l_ps[0:E, 0:2 * P]).then_inc(logits_copied, 1)

            def body(r, g, before):
                for u in range(2):
                    dve.wait_ge(mix_hi_done, 2 * r + u + 1)
                    nc.vector.tensor_tensor(ml[:, u], mix[:, u], mh[:, u].bitcast(F32),
                                            ALU.subtract).then_inc(mix_lo_done, 1)
                if before is not None:
                    copy_logits(r - 1)
                for u in range(2):
                    dve.wait_ge(o_ready, 2 * r + u + 1)
                    if before is not None:
                        dve.wait_ge(x1_done, 2 * r - (1 - u))
                    nc.vector.tensor_tensor(gated[:, u, :], o_ps[:, u].rearrange("p c n -> p (c n)"), g1[:, g, :],
                                            ALU.mult).then_inc(gate_done, 1)
                dve.wait_ge(std_done, r + 1)
                nc.vector.reciprocal(ms[:, :], ms[:, :]).then_inc(rstd_done, 1)
                dve.wait_ge(rstd_done, r + 1)
                for u in range(2):
                    if before is not None:
                        dve.wait_ge(xn_stored[u], 16 * r)
                        dve.wait_ge(xn_turned, KD // 2 * r)
                    nc.vector.tensor_scalar(xn[:, u, :], x1[:, u, :], ms[:, u:u + 1], None,
                                            ALU.mult).then_inc(xn_done, 1)

            nc.vector.memset(eps[:], EPS).then_inc(eps_set, 1)
            dve.wait_ge(tabs_in, 48)
            for k in range(KD):
                dve.wait_ge(w_hi_done, k + 1)
                nc.vector.tensor_tensor(wl[:, k, :], wraw[:, k % 2, :], wh[:, k, :].bitcast(F32),
                                        ALU.subtract).then_inc(w_lo_done, 1)
            over_blocks(dve, body)
            copy_logits(BLOCKS - 1)


def selection(nc, w, keep):
    BITS = 30
    N = TILES * E
    NP = TILE0[1]
    SLOTS = sum(CT)
    V = 5
    groups = ((0, NP), (NP, TILES))
    with ExitStack() as ctx:
        m = Pools(nc, ctx, "sel")
        aff = m.sb("aff", [P, TILES, E])
        red = m.sb("red", [P, TILES])
        one = m.sb("one", [P, P], BF16)
        two = m.sb("two", [P, P], BF16)
        below = m.sb("below", [P, P], BF16)
        iota = m.sb("iota", [P, max(CAPS)], BF16)
        first = m.sb("first", [P, E, TILES])
        ids = m.sb("ids", [P, TILES, 2], BF16)
        bit = m.sb("bit", [P, 2, E], I32)
        thr = m.sb("thr", [P, 2, E])
        cand = m.sb("cand", [P, 2, E])
        count = m.sb("count", [P, 2, E])
        need = m.sb("need", [P, 2, E])
        mark = m.sb("mark", [P, TILES, E], BF16)
        more = m.sb("more", [P, TILES, E], BF16)
        total = m.sb("total", [P, E, TILES])
        scan = m.sb("scan", [P, E, TILES])
        rank = m.sb("rank", [P, TILES, E])
        slot = m.sb("slot", [P, TILES, E])
        rest = m.sb("rest", [P, 2, TILES, E])
        vals = m.sb("vals", [P, TILES, E, V], BF16)
        hot = m.sb("hot", [P, 2, TILES, max(CAPS)], BF16)
        got = m.sb("got", [P, E, SLOTS, V])
        l_ps = m.ps("l_ps")
        c_ps = m.ps("c_ps")
        r_ps = m.ps("r_ps")
        g_ps = [m.ps(f"g_ps{i}") for i in range(2)]
        tabs_in = m.sem("tabs_in")
        turned = m.sem("turned")
        step_done = m.sem("step_done")
        exp_done = m.sem("exp_done")
        bit_step = m.sem("bit_step")
        marked = m.sem("marked")
        counted = m.sem("counted")
        ranked = m.sem("ranked")
        summed = m.sem("summed")
        hot_done = m.sem("hot_done")
        moved = m.sem("moved")
        got_done = m.sem("got_done")
        block = ctx.enter_context(nc.Block())

        @block.gpsimd
        def _(pool):
            m.clear_last(pool)

        @block.sync
        def _(sp):
            for dst, src in ((one[:, :], w["k_one"]), (two[:, :], w["k_two"]), (below[:, :], w["k_below"]),
                             (iota[:, :], w["k_iota"].partition_broadcast(P)),
                             (first[:].rearrange("p e t -> p (e t)"), w["k_first"].partition_broadcast(P)),
                             (ids[:].rearrange("p t v -> p (t v)"), w["k_ids"])):
                sp.dma_start(dst, src).then_inc(tabs_in, 16)

        def tiles_last(x):
            return x.rearrange("p t e -> p e t")

        @block.vector
        def _(dve):
            step = sequence(step_done)

            def then(instruction):
                dve.wait_ge(step_done, step(instruction))

            dve.wait_ge(turned, 1)
            then(nc.vector.tensor_copy(aff[:].rearrange("p t e -> p (t e)"), l_ps[:, 0:N]))
            then(nc.vector.tensor_reduce(red[:, :], aff[:], AX, ALU.max))
            wide = red[:, :].unsqueeze(2).broadcast_to([P, TILES, E])
            step(nc.vector.tensor_tensor(aff[:], aff[:], wide, ALU.subtract))
            dve.wait_ge(exp_done, 1)
            then(nc.vector.tensor_reduce(red[:, :], aff[:], AX, ALU.add))
            then(nc.vector.reciprocal(red[:, :], red[:, :]))
            then(nc.vector.tensor_tensor(aff[:], aff[:], wide, ALU.mult))
            dve.wait_ge(tabs_in, 96)
            then(nc.vector.tensor_copy(vals[:, :, :, 2], aff[:]))
            then(nc.vector.tensor_tensor(rest[:, 0], aff[:], vals[:, :, :, 2], ALU.subtract))
            then(nc.vector.tensor_copy(vals[:, :, :, 3], rest[:, 0]))
            then(nc.vector.tensor_tensor(rest[:, 1], rest[:, 0], vals[:, :, :, 3], ALU.subtract))
            then(nc.vector.tensor_copy(vals[:, :, :, 4], rest[:, 1]))
            for v in range(2):
                then(nc.vector.tensor_copy(vals[:, :, :, v], ids[:, :, v].unsqueeze(2).broadcast_to([P, TILES, E])))
            then(nc.vector.memset(bit[:], 1 << (BITS - 1)))
            then(nc.vector.memset(thr[:], 0.0))
            with dve.Fori(0, BITS) as i:
                nc.vector.tensor_tensor(cand[:].bitcast(I32), thr[:].bitcast(I32), bit[:],
                                        ALU.bitwise_or).then_inc(bit_step, 1)
                dve.wait_ge(bit_step, i * 5 + 1)
                for a, b in groups:
                    c = cand[:, int(a > 0)].unsqueeze(1).broadcast_to([P, b - a, E])
                    nc.vector.tensor_tensor(mark[:, a:b], aff[:, a:b], c, ALU.is_ge).then_inc(marked, 1)
                nc.vector.tensor_scalar(bit[:], bit[:], 1, None, ALU.logical_shift_right).then_inc(bit_step, 1)
                dve.wait_ge(counted, i + 1)
                for g, (a, b) in enumerate(groups):
                    nc.vector.tensor_reduce(count[:, g], c_ps[:, a * E:b * E].rearrange("p (t e) -> p e t", e=E),
                                            AX, ALU.add).then_inc(bit_step, 1)
                dve.wait_ge(bit_step, i * 5 + 4)
                nc.vector.scalar_tensor_tensor(cand[:], count[:], float(CAPS[1]), cand[:], ALU.is_ge,
                                               ALU.mult).then_inc(bit_step, 1)
                dve.wait_ge(bit_step, i * 5 + 5)
                nc.vector.tensor_tensor(thr[:], thr[:], cand[:], ALU.max).then_inc(summed, 1)
                dve.wait_ge(summed, i + 1)
            for g, (a, b) in enumerate(groups):
                t = thr[:, g].unsqueeze(1).broadcast_to([P, b - a, E])
                nc.vector.tensor_tensor(mark[:, a:b], aff[:, a:b], t, ALU.is_equal).then_inc(marked, 1)
                nc.vector.tensor_tensor(more[:, a:b], aff[:, a:b], t, ALU.is_gt).then_inc(marked, 1)

            def ranks(n):
                dve.wait_ge(ranked, n)
                then(nc.vector.tensor_copy(total[:], c_ps[:, 0:N].rearrange("p (t e) -> p e t", e=E)))
                then(nc.vector.tensor_tensor_scan(scan[:].rearrange("p e t -> p (e t)"),
                                                  first[:].rearrange("p e t -> p (e t)"),
                                                  total[:].rearrange("p e t -> p (e t)"), 0.0, ALU.mult, ALU.add))
                then(nc.vector.tensor_tensor(scan[:], scan[:], total[:], ALU.subtract))
                then(nc.vector.tensor_tensor(rank[:], r_ps[:, 0:N].rearrange("p (t e) -> p t e", e=E),
                                             scan[:].rearrange("p e t -> p t e"), ALU.add))

            ranks(1)
            dve.wait_ge(ranked, 2)
            for g, (a, b) in enumerate(groups):
                then(nc.vector.tensor_reduce(count[:, g], g_ps[0][:, a * E:b * E].rearrange("p (t e) -> p e t", e=E),
                                             AX, ALU.add))
                then(nc.vector.tensor_scalar(need[:, g], count[:, g], -1.0, float(CAPS[g]), ALU.mult, ALU.add))
                left = need[:, g].unsqueeze(1).broadcast_to([P, b - a, E])
                then(nc.vector.tensor_tensor(rank[:, a:b], rank[:, a:b], left, ALU.is_lt))
            then(nc.vector.tensor_tensor(rank[:], rank[:], mark[:], ALU.mult))
            nc.vector.tensor_tensor(more[:], more[:], rank[:], ALU.add).then_inc(marked, 1)
            dve.wait_ge(marked, 2 * BITS + 5)
            ranks(3)
            then(nc.vector.tensor_scalar(rank[:], rank[:], 1.0, None, ALU.add))
            then(nc.vector.tensor_tensor(rank[:], rank[:], more[:], ALU.mult))
            then(nc.vector.tensor_scalar(slot[:], rank[:], -1.0, None, ALU.add))
            for e in range(E):
                if e >= 2:
                    dve.wait_ge(moved, e - 1)
                for t in range(TILES):
                    cap = CAPS[int(t >= NP)]
                    mk = nc.vector.tensor_scalar(hot[:, e % 2, t, 0:cap], iota[:, 0:cap], slot[:, t, e:e + 1], None,
                                                 ALU.is_equal)
                mk.then_inc(hot_done, 1)
                if e >= 1:
                    dve.wait_ge(moved, e)
                    nc.vector.tensor_copy(got[:, e - 1].rearrange("p s v -> p (s v)"),
                                          g_ps[(e - 1) % 2][:, 0:SLOTS * V]).then_inc(got_done, 1)
            dve.wait_ge(moved, E)
            nc.vector.tensor_copy(got[:, E - 1].rearrange("p s v -> p (s v)"),
                                  g_ps[(E - 1) % 2][:, 0:SLOTS * V]).then_inc(got_done, 1)
            dve.wait_ge(got_done, E)
            then(nc.vector.tensor_tensor(keep["index"][:], got[:, :, :, 0], got[:, :, :, 1], ALU.add))
            then(nc.vector.tensor_tensor(got[:, :, :, 0], got[:, :, :, 2], got[:, :, :, 3], ALU.add))
            then(nc.vector.tensor_tensor(keep["gate"][:], got[:, :, :, 0], got[:, :, :, 4], ALU.add))

        @block.scalar
        def _(act):
            act.wait_ge(step_done, 3)
            nc.scalar.activation(aff[:], aff[:], ACT.Exp).then_inc(exp_done, 1)

        @block.tensor
        def _(pe):
            for n in range(TILES):
                mm = nc.tensor.transpose(l_ps[:, n * E:(n + 1) * E], keep["logits"][:, n * P:(n + 1) * P],
                                         keep["ident"][0:E, 0:E])
            mm.then_inc(turned, 1)
            pe.wait_ge(tabs_in, 96)
            with pe.Fori(0, BITS) as i:
                for g, ((a, b), weight) in enumerate(zip(groups, (two, one))):
                    pe.wait_ge(marked, 2 * i + g + 1)
                    if g == 0:
                        pe.wait_ge(bit_step, 5 * i + 1)
                    mm = nc.tensor.matmul(c_ps[:, a * E:b * E], weight[:, :],
                                          mark[:, a:b].rearrange("p t e -> p (t e)"), start=True, stop=True)
                mm.then_inc(counted, 1)

            def ranks(x):
                flat = x[:].rearrange("p t e -> p (t e)")
                nc.tensor.matmul(c_ps[:, 0:N], one[:, :], flat, start=True, stop=True)
                nc.tensor.matmul(r_ps[:, 0:N], below[:, :], flat, start=True, stop=True).then_inc(ranked, 1)

            pe.wait_ge(marked, 2 * BITS + 4)
            ranks(mark)
            nc.tensor.matmul(g_ps[0][:, 0:N], one[:, :], more[:].rearrange("p t e -> p (t e)"),
                             start=True, stop=True).then_inc(ranked, 1)
            pe.wait_ge(marked, 2 * BITS + 5)
            ranks(more)
            for e in range(E):
                pe.wait_ge(hot_done, e + 1)
                if e >= 2:
                    pe.wait_ge(got_done, e - 1)
                for s in range(SLOTS):
                    g = int(s >= CT[0])
                    a, b = groups[g]
                    c = s - g * CT[0]
                    for t in range(a, b):
                        mm = nc.tensor.matmul(g_ps[e % 2][:, s * V:(s + 1) * V], hot[:, e % 2, t, c * P:(c + 1) * P],
                                              vals[:, t, e, :], start=(t == a), stop=(t == b - 1))
                mm.then_inc(moved, 1)


def experts(nc, w, keep):
    CHUNKS = 6
    GU = 4
    PIECES = 4
    SLOTS = sum(CT)
    C = SLOTS * P
    NP = CT[0] * P
    KP = KD // PIECES
    TURNS = ((0, 1), (2,), (3,), (4,), (5, 6), (7,))
    with ExitStack() as ctx:
        m = Pools(nc, ctx, "moe")
        raw = m.sb("raw", [P, 2, KD, BANK])
        wh = m.sb("wh", [P, 2, KD, BANK], F32R)
        wl = m.sb("wl", [P, 2, KD, BANK], F32R)
        rows = m.sb("rows", [P, SLOTS, D])
        xf = m.sb("xf", [P, 2, C])
        xh = m.sb("xh", [P, KD, C], F32R)
        xl = m.sb("xl", [P, KD, C], F32R)
        silu = m.sb("silu", [P, 2, C])
        hf = m.sb("hf", [P, 2, C])
        hh = m.sb("hh", [P, KF, C], F32R)
        hl = m.sb("hl", [P, KF, C], F32R)
        ye = m.sb("ye", [P, SLOTS, D])
        g2 = m.sb("g2", [P, 2, D])
        to_gather = m.sb("to_gather", [P, SLOTS], I32)
        to_add = m.sb("to_add", [P, SLOTS], I32)
        a_ps = [m.ps(f"a_ps{i}") for i in range(2)]
        u_ps = [m.ps(f"u_ps{i}") for i in range(2)]
        t_ps = [m.ps(f"t_ps{i}") for i in range(2)]
        d_ps = [m.ps(f"d_ps{i}") for i in range(2)]
        g2_in = m.sem("g2_in")
        raw_in = [m.sem(f"raw_in{i}") for i in range(2)]
        w_hi_done = m.sem("w_hi_done")
        w_lo_done = m.sem("w_lo_done")
        gather_index = m.sem("gather_index")
        add_index = m.sem("add_index")
        gathered = [m.sem(f"gathered{i}") for i in range(SLOTS)]
        pool_waited = m.sem("pool_waited")
        sp_waited = m.sem("sp_waited")
        turned = m.sem("turned")
        x_full = m.sem("x_full")
        x_hi_done = m.sem("x_hi_done")
        x_lo_done = m.sem("x_lo_done")
        gu_ready = m.sem("gu_ready")
        silu_done = m.sem("silu_done")
        h_full = m.sem("h_full")
        h_hi_done = m.sem("h_hi_done")
        h_lo_done = m.sem("h_lo_done")
        d_ready = m.sem("d_ready")
        ye_done = m.sem("ye_done")
        added = [m.sem(f"added{i}") for i in range(SLOTS)]
        block = ctx.enter_context(nc.Block())
        DOWNS = 2 * SLOTS

        def over_experts(eng, body):
            body(0, False)
            with eng.Fori(1, E - 1) as e:
                body(e, False)
            body(E - 1, True)

        def is_first(e):
            return isinstance(e, int) and e == 0

        @block.sync
        def _(sp):
            def load(e, c):
                s = c % 2
                if c < GU:
                    for i, name in enumerate(("w_gate", "w_up")):
                        src = w[name][0][bass.ds(e, 1), :, c * 256:(c + 1) * 256]
                        sp.dma_start(raw[:, s, :, i * 256:(i + 1) * 256],
                                     src.rearrange("o (k p) n -> p (o k) n", p=P)).then_inc(raw_in[s], 16)
                else:
                    src = w["w_down"][0][bass.ds(e, 1), :, (c - GU) * BANK:(c - GU + 1) * BANK]
                    src = src.rearrange("o (k p) n -> p (o k) n", p=P)
                    for i in range(2):
                        half = slice(i * KD // 2, (i + 1) * KD // 2)
                        sp.dma_start(raw[:, s, half, :], src[:, half, :]).then_inc(raw_in[s], 16)

            def body(e, last):
                after = e + 1
                for c in range(CHUNKS - 1 if last else CHUNKS):
                    if c >= 1 or not is_first(e):
                        sp.wait_ge(w_lo_done, (e * CHUNKS + c) * PIECES)
                        sp.sem_inc(sp_waited, 1)
                    load(*((e, c + 1) if c + 1 < CHUNKS else (after, 0)))

            for g in range(2):
                at = (2 + g) * D
                sp.dma_start(g2[:, g, :], w["s_gates"][0, at:at + D].partition_broadcast(P)).then_inc(g2_in, 16)
            load(0, 0)
            over_experts(sp, body)

        @block.gpsimd
        def _(pool):
            m.clear_last(pool)

            def gather(e):
                pool.wait_ge(gather_index, e + 1)
                pool.sem_inc(pool_waited, 1)
                for s in range(SLOTS):
                    pool.indirect_dma_start(out=rows[:, s, :], out_offset=None, in_=w["s_xn"],
                                            in_offset=bass.IndirectOffsetOnAxis(ap=to_gather[:, s:s + 1], axis=0)
                                            ).then_inc(gathered[s], 16)

            def body(e, last):
                if not last:
                    pool.wait_ge(turned, (e + 1) * KD)
                    gather(e + 1)
                pool.wait_ge(ye_done, (e + 1) * DOWNS)
                pool.wait_ge(add_index, e + 1)
                for s in range(SLOTS):
                    if not is_first(e):
                        pool.wait_ge(added[s], e * 16)
                pool.sem_inc(pool_waited, 1)
                for s in range(SLOTS):
                    pool.indirect_dma_start(out=w["s_x"],
                                            out_offset=bass.IndirectOffsetOnAxis(ap=to_add[:, s:s + 1], axis=0),
                                            in_=ye[:, s, :], in_offset=None, compute_op=ALU.add).then_inc(added[s], 16)

            gather(0)
            over_experts(pool, body)
            for s in range(SLOTS):
                pool.wait_ge(added[s], E * 16)

        @block.tensor
        def _(pe):
            def turn(e, k):
                if k == 0:
                    for s in range(SLOTS):
                        pe.wait_ge(gathered[s], (e + 1) * 16)
                if not (isinstance(e, int) and e == 0 and k < 2):
                    pe.wait_ge(x_full, (e * KD + k - 1) * 2)
                for s in range(SLOTS):
                    mm = nc.tensor.transpose(t_ps[k % 2][:, s * P:(s + 1) * P], rows[:, s, k * P:(k + 1) * P],
                                             keep["ident"][:, :])
                mm.then_inc(turned, 1)

            def body(e, last):
                for c in range(GU):
                    pe.wait_ge(w_lo_done, (e * CHUNKS + c + 1) * PIECES)
                    for i in range(2):
                        f = 2 * c + i
                        if c == 0 and i == 0:
                            pe.wait_ge(x_lo_done, (e + 1) * KD)
                        if c > 0:
                            pe.wait_ge(h_full, e * KF + f - 1)
                        for ps, col in ((a_ps, i * P), (u_ps, 256 + i * P)):
                            for k in range(KD):
                                hi, lo = wh[:, c % 2, k, col:col + P], wl[:, c % 2, k, col:col + P]
                                out = ps[i][:, 0:C]
                                nc.tensor.matmul(out, hi, xh[:, k, :], start=(k == 0), stop=False)
                                nc.tensor.matmul(out, hi, xl[:, k, :], start=False, stop=False)
                                mm = nc.tensor.matmul(out, lo, xh[:, k, :], start=False, stop=(k == KD - 1))
                        mm.then_inc(gu_ready, 1)
                for n in range(2):
                    c = GU + n
                    pe.wait_ge(w_lo_done, (e * CHUNKS + c + 1) * PIECES)
                    for s in range(SLOTS):
                        j = n * SLOTS + s
                        if not last:
                            for k in TURNS[j]:
                                turn(e + 1, k)
                        if j == 0:
                            pe.wait_ge(h_lo_done, (e + 1) * KF)
                        if j >= 2:
                            pe.wait_ge(ye_done, e * DOWNS + j - 1)
                        out = d_ps[j % 2][:, :]
                        for k in range(KF):
                            h_hi, h_lo = hh[:, k, s * P:(s + 1) * P], hl[:, k, s * P:(s + 1) * P]
                            nc.tensor.matmul(out, h_hi, wh[:, c % 2, k, :], start=(k == 0), stop=False)
                            nc.tensor.matmul(out, h_hi, wl[:, c % 2, k, :], start=False, stop=False)
                            mm = nc.tensor.matmul(out, h_lo, wh[:, c % 2, k, :], start=False, stop=(k == KF - 1))
                        mm.then_inc(d_ready, 1)

            for k in range(KD):
                turn(0, k)
            over_experts(pe, body)

        def chunk_is_used(eng, e, c):
            if c < GU:
                eng.wait_ge(gu_ready, e * KF + 2 * (c + 1))
            else:
                eng.wait_ge(d_ready, e * DOWNS + (c - GU + 1) * SLOTS)

        @block.scalar
        def _(act):
            def split(e, c):
                s = c % 2
                act.wait_ge(raw_in[s], (e * (CHUNKS // 2) + c // 2 + 1) * 32)
                for i in range(PIECES):
                    part = slice(i * KP, (i + 1) * KP)
                    nc.scalar.activation(wh[:, s, part, :], raw[:, s, part, :], ACT.Copy).then_inc(w_hi_done, 1)

            def modulate(e, k):
                act.wait_ge(turned, e * KD + k + 1)
                if not (isinstance(e, int) and e == 0 and k < 2):
                    act.wait_ge(x_lo_done, e * KD + k - 1)
                for g, cols in enumerate((slice(0, NP), slice(NP, C))):
                    nc.scalar.activation(xf[:, k % 2, cols], t_ps[k % 2][:, cols], ACT.Identity,
                                         bias=keep["modc"][:, g, 3 * KD + k:3 * KD + k + 1],
                                         scale=keep["modc"][:, g, 4 * KD + k:4 * KD + k + 1]).then_inc(x_full, 1)
                act.wait_ge(x_full, (e * KD + k + 1) * 2)
                nc.scalar.activation(xh[:, k, :], xf[:, k % 2, :], ACT.Copy).then_inc(x_hi_done, 1)

            def body(e, last):
                for c in range(CHUNKS):
                    nxt = (e, c + 1) if c + 1 < CHUNKS else (e + 1, 0)
                    if c + 1 < CHUNKS or not last:
                        if c >= 1:
                            chunk_is_used(act, e, c - 1)
                        elif not is_first(e):
                            act.wait_ge(d_ready, e * DOWNS)
                        split(*nxt)
                    if c < GU:
                        for i in range(2):
                            f = 2 * c + i
                            act.wait_ge(gu_ready, e * KF + f + 1)
                            nc.scalar.activation(silu[:, i, :], a_ps[i][:, 0:C], ACT.Silu).then_inc(silu_done, 1)
                            act.wait_ge(h_full, e * KF + f + 1)
                            nc.scalar.activation(hh[:, f, :], hf[:, i, :], ACT.Copy).then_inc(h_hi_done, 1)
                    elif not last:
                        for j in range((c - GU) * SLOTS, (c - GU + 1) * SLOTS):
                            for k in TURNS[j]:
                                modulate(e + 1, k)

            split(0, 0)
            for k in range(KD):
                modulate(0, k)
            over_experts(act, body)

        @block.vector
        def _(dve):
            def split(e, c):
                s = c % 2
                for i in range(PIECES):
                    part = slice(i * KP, (i + 1) * KP)
                    dve.wait_ge(w_hi_done, (e * CHUNKS + c) * PIECES + i + 1)
                    nc.vector.tensor_tensor(wl[:, s, part, :], raw[:, s, part, :], wh[:, s, part, :].bitcast(F32),
                                            ALU.subtract).then_inc(w_lo_done, 1)

            def x_low(e, k):
                dve.wait_ge(x_hi_done, e * KD + k + 1)
                nc.vector.tensor_tensor(xl[:, k, :], xf[:, k % 2, :], xh[:, k, :].bitcast(F32),
                                        ALU.subtract).then_inc(x_lo_done, 1)

            def index(e, dst, sem):
                nc.vector.tensor_copy(dst[:, :].unsqueeze(1), keep["index"][:, bass.ds(e, 1), :]).then_inc(sem, 1)

            def body(e, last):
                for s in range(SLOTS):
                    if not is_first(e):
                        dve.wait_ge(added[s], e * 16)
                index(e, to_add, add_index)
                if not last:
                    for s in range(SLOTS):
                        dve.wait_ge(gathered[s], (e + 1) * 16)
                    index(e + 1, to_gather, gather_index)
                for c in range(CHUNKS):
                    if c + 1 < CHUNKS or not last:
                        split(*((e, c + 1) if c + 1 < CHUNKS else (e + 1, 0)))
                    if c < GU:
                        for i in range(2):
                            f = 2 * c + i
                            dve.wait_ge(silu_done, e * KF + f + 1)
                            nc.vector.tensor_tensor(hf[:, i, :], u_ps[i][:, 0:C], silu[:, i, :],
                                                    ALU.mult).then_inc(h_full, 1)
                            dve.wait_ge(h_hi_done, e * KF + f + 1)
                            nc.vector.tensor_tensor(hl[:, f, :], hf[:, i, :], hh[:, f, :].bitcast(F32),
                                                    ALU.subtract).then_inc(h_lo_done, 1)
                    else:
                        for s in range(SLOTS):
                            n = c - GU
                            j = n * SLOTS + s
                            if not last:
                                for k in TURNS[j]:
                                    x_low(e + 1, k)
                            dve.wait_ge(d_ready, e * DOWNS + j + 1)
                            nc.vector.scalar_tensor_tensor(ye[:, s, n * BANK:(n + 1) * BANK], d_ps[j % 2][:, :],
                                                           keep["gate"][:, bass.ds(e, 1), s:s + 1].rearrange("p o s -> p (o s)"),
                                                           g2[:, int(s >= CT[0]), n * BANK:(n + 1) * BANK],
                                                           ALU.mult, ALU.mult).then_inc(ye_done, 1)

            index(0, to_gather, gather_index)
            dve.wait_ge(g2_in, 32)
            split(0, 0)
            for k in range(KD):
                x_low(0, k)
            over_experts(dve, body)


def final_norm(nc, w, keep):
    with ExitStack() as ctx:
        m = Pools(nc, ctx, "fin")
        R = 4
        BLOCKS = TILES // 2
        gain = m.sb("gain", [P, D])
        x = m.sb("x", [P, R, 2, D])
        y = m.sb("y", [P, R, 2, D])
        ms = m.sb("ms", [P, TILES])
        eps = m.sb("eps", [P, 1])
        gain_in = m.sem("gain_in")
        eps_set = m.sem("eps_set")
        x_in = [m.sem(f"x_in{i}") for i in range(R)]
        squared = m.sem("squared")
        std_done = m.sem("std_done")
        rstd_done = m.sem("rstd_done")
        y_done = m.sem("y_done")
        stored = [m.sem(f"stored{i}") for i in range(R)]
        block = ctx.enter_context(nc.Block())

        @block.gpsimd
        def _(pool):
            m.clear_last(pool)

        @block.sync
        def _(sp):
            sp.dma_start(gain[:, :], w["final_norm_g"].partition_broadcast(P)).then_inc(gain_in, 16)
            for b in range(BLOCKS):
                if b >= R:
                    sp.wait_ge(y_done, 2 * (b - R + 1))
                src = w["s_x"][b * 2 * P:(b + 1) * 2 * P, :].rearrange("(j p) d -> p j d", p=P)
                sp.dma_start(x[:, b % R], src).then_inc(x_in[b % R], 16)

        def store(act, b):
            act.wait_ge(y_done, 2 * b + 2)
            g = int(2 * b >= TILE0[1])
            row = b * 2 * P - STARTS[g]
            dst = w[("y_prompt", "y_sample")[g]][0][row:row + 2 * P, :].rearrange("(j p) d -> p j d", p=P)
            act.dma_start(dst, y[:, b % R]).then_inc(stored[b % R], 16)

        @block.scalar
        def _(act):
            act.wait_ge(eps_set, 1)
            for b in range(BLOCKS):
                act.wait_ge(x_in[b % R], 16 * (b // R + 1))
                if b >= R:
                    act.wait_ge(stored[b % R], 16 * (b // R))
                for j in range(2):
                    nc.scalar.activation(y[:, b % R, j, :], x[:, b % R, j, :], ACT.Square, scale=float(D) ** -0.5,
                                         accum_out=ms[:, 2 * b + j:2 * b + j + 1]).then_inc(squared, 1)
                act.wait_ge(squared, 2 * b + 2)
                nc.scalar.activation(ms[:, 2 * b:2 * b + 2], ms[:, 2 * b:2 * b + 2], ACT.Sqrt,
                                     bias=eps[:, 0:1]).then_inc(std_done, 1)
                if b >= 1:
                    store(act, b - 1)
            store(act, BLOCKS - 1)
            for i in range(R):
                act.wait_ge(stored[i], 16 * (BLOCKS // R))

        @block.vector
        def _(dve):
            nc.vector.memset(eps[:], EPS).then_inc(eps_set, 1)
            dve.wait_ge(gain_in, 16)
            for b in range(BLOCKS):
                dve.wait_ge(std_done, b + 1)
                nc.vector.reciprocal(ms[:, 2 * b:2 * b + 2], ms[:, 2 * b:2 * b + 2]).then_inc(rstd_done, 1)
                dve.wait_ge(rstd_done, b + 1)
                for j in range(2):
                    nc.vector.scalar_tensor_tensor(y[:, b % R, j, :], x[:, b % R, j, :], ms[:, 2 * b + j:2 * b + j + 1],
                                                   gain[:, :], ALU.mult, ALU.mult).then_inc(y_done, 1)


def build(nc, w):
    keep = {}

    def tile(ctx, name, shape, dt=F32):
        keep[name] = ctx.enter_context(nc.sbuf_tensor(f"keep_{name}", shape, dt))

    with ExitStack() as ctx:
        tile(ctx, "ident", [P, P])
        tile(ctx, "modc", [P, 3, 6 * KD])
        tile(ctx, "index", [P, E, sum(CT)], I32)
        tile(ctx, "gate", [P, E, sum(CT)])
        modulation(nc, w, keep)
        in_proj(nc, w, keep)
        for g in (1, 0):
            attention(nc, w, keep, g)
        pooling(nc, w, keep)
        with ExitStack() as route_ctx:
            tile(route_ctx, "logits", [E, TOKENS])
            out_proj(nc, w, keep)
            selection(nc, w, keep)
        experts(nc, w, keep)
        final_norm(nc, w, keep)


SCRATCH = {
    "s_gates": [1, 4 * D],
    "s_ct": [TILES, P, KC * P],
    "s_krt": [ROPE, TOKENS],
    "s_ut": [DP // P, P, TOKENS],
    "s_att": [HEADS * VD, TOKENS],
    "s_pool": [DP // P, P, TOKENS],
    "s_x": [TOKENS, D],
    "s_xn": [TOKENS, D],
}


def constants():
    inv = np.float32(10000.0) ** (-np.arange(0, ROPE, 2, dtype=np.float32) / np.float32(ROPE))
    out = {"k_ident": np.eye(P, dtype=np.float32)}
    rope = np.zeros((TILES, P, 2, ROPE), np.float32)
    for g in range(2):
        ang = np.arange(SEQS[g], dtype=np.float32)[:, None] * inv[None, :]
        for a, f in enumerate((np.cos, np.sin)):
            t = f(ang).astype(np.float32).reshape(-1, P, ROPE // 2)
            rope[TILE0[g]:TILE0[g] + SEQS[g] // P, :, a] = np.concatenate([t, t], -1)
    out["k_rope"] = rope
    turned = rope[TILE0[1]:].reshape(SEQS[1], 2, ROPE).transpose(1, 2, 0).copy()
    turned[1, :ROPE // 2] *= -1
    out["k_rope_t"] = np.ascontiguousarray(turned.reshape(2 * ROPE, SEQS[1]))
    t = np.arange(SEQS[0])
    edge = []
    for size in WINDOWS:
        count = np.minimum(t + size // 2, SEQS[0]) - np.maximum(t - size // 2, 0)
        inverse = np.float32(1) / count.astype(np.float32)
        edge.append(np.concatenate([inverse[:8], inverse[-8:]]))
    out["k_edge"] = np.concatenate(edge).astype(np.float32)
    bf16 = mybir.dt.np(BF16)
    out["k_one"] = np.ones((P, P), bf16)
    out["k_two"] = np.full((P, P), 2, bf16)
    out["k_below"] = np.triu(np.ones((P, P)), 1).astype(bf16)
    out["k_iota"] = np.arange(max(CAPS)).astype(bf16)
    first = np.ones((E, TILES), np.float32)
    first[:, list(TILE0)] = 0
    out["k_first"] = first.reshape(-1)
    out["k_ids"] = np.stack(np.broadcast_arrays(np.arange(TILES)[None, :] * P, np.arange(P)[:, None]),
                            -1).reshape(P, -1).astype(bf16)
    return out


INPUTS = ["x_prompt", "x_sample", "c_prompt", "c_sample", "w_ada", "b_ada", "w_in", "q_norm_g", "kv_norm_g",
          "w_uq", "w_ukv", "w_pool", "pool_scale", "w_out", "w_router", "w_gate", "w_up", "w_down",
          "final_norm_g"]


def kernel(**inputs):
    import concourse.bacc as bacc
    from concourse.bass_utils import run_bass_kernel_spmd

    nc = bacc.Bacc("TRN2", target_bir_lowering=False, num_devices=1)
    arrays, w = {}, {}
    given = {name: np.ascontiguousarray(inputs[name]) for name in INPUTS}
    for name, a in (*given.items(), *constants().items()):
        arrays[name] = a
        w[name] = nc.dram_tensor(name, list(a.shape), mybir.dt.from_np(a.dtype), kind="ExternalInput").ap()
    for name, shape in SCRATCH.items():
        w[name] = nc.dram_tensor(name, shape, F32, kind="Internal").ap()
    for g, name in enumerate(("y_prompt", "y_sample")):
        w[name] = nc.dram_tensor(name, [1, SEQS[g], D], F32, kind="ExternalOutput").ap()
    build(nc, w)
    r = run_bass_kernel_spmd(nc, [arrays], core_ids=[0])
    return r.results[0]["y_prompt"], r.results[0]["y_sample"]
```

```python
from contextlib import ExitStack

import numpy as np

import concourse.bass as bass
from concourse import mybir

F32 = mybir.dt.float32
F32R = mybir.dt.float32r
BF16 = mybir.dt.bfloat16
I32 = mybir.dt.int32
ALU = mybir.AluOpType
ACT = mybir.ActivationFunctionType
AX = mybir.AxisListType.X

P = 128
BANK = 512
D = 1024
KD = D // P
SEQS = (1024, 2048)
STARTS = (0, 1024)
TOKENS = sum(SEQS)
TILES = TOKENS // P
TILE0 = (0, SEQS[0] // P)
QL, KVL, ROPE, DP = 384, 256, 32, 512
D_IN = QL + KVL + ROPE + DP
HEADS, NOPE, VD = 8, 64, 64
QK = NOPE + ROPE
KQ, KKV = QL // P, KVL // P
KC = KQ + KKV
E = 16
FF = 1024
KF = FF // P
CAPS = tuple(2 * s // E for s in SEQS)
CT = tuple(c // P for c in CAPS)
EPS = 1e-6
WINDOWS = (2, 4, 8, 16)


def sequence(sem, start=0):
    count = [start]

    def step(instruction):
        count[0] += 1
        instruction.then_inc(sem, 1)
        return count[0]

    return step


class Pools:

    before, used = [], []

    def __init__(self, nc, ctx, stage):
        self.nc, self.ctx, self.stage = nc, ctx, stage
        Pools.before, Pools.used = Pools.used, []

    def sb(self, name, shape, dt=F32):
        return self.ctx.enter_context(self.nc.sbuf_tensor(f"{self.stage}_{name}", shape, dt))

    def ps(self, name, shape=(P, BANK), dt=F32):
        return self.ctx.enter_context(self.nc.psum_tensor(f"{self.stage}_{name}", list(shape), dt))

    def sem(self, name):
        s = self.ctx.enter_context(self.nc.semaphore(f"{self.stage}_{name}"))
        Pools.used.append(s.num)
        return s

    def clear_last(self, pool):
        nums = sorted(Pools.before)
        while nums:
            n = 1
            while n < len(nums) and nums[n] == nums[0] + n:
                n += 1
            pool.sem_clear(range(nums[0], nums[0] + n))
            nums = nums[n:]


def modulation(nc, w, keep):
    RING = 3
    NCH = 6 * D // BANK
    COLS = [part * KD + k for part in (0, 1, 3, 4) for k in range(KD)]
    with ExitStack() as ctx:
        m = Pools(nc, ctx, "ada")
        ct = m.sb("ct", [P, 2, KD])
        cs = m.sb("cs", [P, 2, KD])
        wa = m.sb("wa", [P, RING, KD, BANK])
        bias = m.sb("bias", [2, 6 * D])
        rows = m.sb("rows", [2, 6 * D])
        r_ps = [m.ps(f"r_ps{i}") for i in range(2)]
        c_ps = [m.ps(f"c_ps{i}") for i in range(2)]
        small_in = m.sem("small_in")
        bias_in = m.sem("bias_in")
        w_in = [m.sem(f"w_in{i}") for i in range(RING)]
        silu_done = m.sem("silu_done")
        chunk_done = m.sem("chunk_done")
        rows_done = m.sem("rows_done")
        turned = m.sem("turned")
        cols_done = m.sem("cols_done")
        gates_stored = m.sem("gates_stored")
        block = ctx.enter_context(nc.Block())
        w_ada = w["w_ada"][0].rearrange("(p k) n -> p k n", k=KD)

        @block.sync
        def _(sp):
            for g, name in enumerate(("c_prompt", "c_sample")):
                sp.dma_start(ct[:, g, :], w[name][0].rearrange("(p k) -> p k", k=KD)).then_inc(small_in, 16)
            for n in range(NCH):
                if n == 1:
                    sp.dma_start(bias[:, :], w["b_ada"][0].partition_broadcast(2)).then_inc(bias_in, 16)
                    sp.dma_start(keep["ident"][:, :], w["k_ident"]).then_inc(bias_in, 16)
                if n >= RING:
                    sp.wait_ge(chunk_done, n - RING + 1)
                sp.dma_start(wa[:, n % RING], w_ada[:, :, n * BANK:(n + 1) * BANK]).then_inc(w_in[n % RING], 16)
            sp.wait_ge(rows_done, NCH)
            for a, part in enumerate((2, 5)):
                for g in range(2):
                    at = (2 * a + g) * D
                    sp.dma_start(w["s_gates"][0:1, at:at + D],
                                 rows[g:g + 1, part * D:(part + 1) * D]).then_inc(gates_stored, 16)
            sp.wait_ge(gates_stored, 64)

        @block.gpsimd
        def _(pool):
            m.clear_last(pool)

        @block.scalar
        def _(act):
            act.wait_ge(small_in, 32)
            nc.scalar.activation(cs[:], ct[:], ACT.Silu).then_inc(silu_done, 1)

        @block.tensor
        def _(pe):
            pe.wait_ge(silu_done, 1)
            for n in range(NCH):
                pe.wait_ge(w_in[n % RING], 16 * (n // RING + 1))
                if n >= 2:
                    pe.wait_ge(rows_done, n - 1)
                for k in range(KD):
                    mm = nc.tensor.matmul(r_ps[n % 2][0:2, :], cs[:, :, k], wa[:, n % RING, k, :],
                                          start=(k == 0), stop=(k == KD - 1))
                mm.then_inc(chunk_done, 1)
            pe.wait_ge(bias_in, 32)
            pe.wait_ge(rows_done, NCH)
            for i, j in enumerate(COLS):
                half = i // (2 * KD)
                c = 2 * (i % (2 * KD))
                mm = nc.tensor.transpose(c_ps[half][:, c:c + 2], rows[:, j * P:(j + 1) * P], keep["ident"][0:2, 0:2])
                mm.then_inc(turned, 1)

        @block.vector
        def _(dve):
            dve.wait_ge(bias_in, 32)
            for n in range(NCH):
                dve.wait_ge(chunk_done, n + 1)
                part = slice(n * BANK, (n + 1) * BANK)
                nc.vector.tensor_tensor(rows[:, part], r_ps[n % 2][0:2, :], bias[:, part], ALU.add).then_inc(rows_done, 1)
            for half, first in enumerate((0, 3 * KD)):
                dve.wait_ge(turned, 2 * KD * (half + 1))
                for g in range(2):
                    cols = c_ps[half][:, 0:4 * KD].rearrange("p (k g) -> p g k", g=2)[:, g, :]
                    nc.vector.tensor_copy(keep["modc"][:, g, first:first + KD], cols[:, 0:KD]).then_inc(cols_done, 1)
                    nc.vector.tensor_scalar(keep["modc"][:, g, first + KD:first + 2 * KD], cols[:, KD:2 * KD], 1.0,
                                            None, ALU.add).then_inc(cols_done, 1)


def in_proj(nc, w, keep):
    TB = 2
    UG = DP // P // TB
    NB = TILES // TB
    T = TB * P
    with ExitStack() as ctx:
        m = Pools(nc, ctx, "inp")
        wraw = m.sb("wraw", [P, 2, D_IN])
        wh = m.sb("wh", [P, KD, D_IN], F32R)
        wl = m.sb("wl", [P, KD, D_IN], F32R)
        x = m.sb("x", [P, 2, TB, D])
        junk = m.sb("junk", [P, 2, D])
        zjunk = m.sb("zjunk", [P, QL + KVL])
        hf = m.sb("hf", [P, 2, 2, T])
        hh = m.sb("hh", [P, 2, KD, T], F32R)
        hl = m.sb("hl", [P, 2, KD, T], F32R)
        rope = m.sb("rope", [P, TILES, 2, ROPE])
        ms = m.sb("ms", [P, NB, TB])
        zr = m.sb("zr", [P, 2, QL + KVL])
        zms = m.sb("zms", [P, TILES, 2])
        kr = m.sb("kr", [P, TILES, ROPE])
        tmp = m.sb("tmp", [P, 2, ROPE])
        ut = m.sb("ut", [P, 2, UG, T])
        ct = m.sb("ct", [P, 2, KC * P])
        krt = m.sb("krt", [ROPE, TOKENS])
        gain = m.sb("gain", [P, KC])
        eps = m.sb("eps", [P, 1])
        t_ps = [m.ps(f"t_ps{i}") for i in range(2)]
        q_ps, kv_ps = m.ps("q_ps"), m.ps("kv_ps")
        u_ps = [m.ps(f"u_ps{i}") for i in range(2)]
        c_ps = [m.ps(f"c_ps{i}") for i in range(2)]
        w_loaded = [m.sem(f"w_loaded{k}") for k in range(2)]
        w_hi_done = m.sem("w_hi_done")
        w_lo_done = m.sem("w_lo_done")
        x_loaded = [m.sem(f"x_loaded{i}") for i in range(2)]
        rope_loaded = m.sem("rope_loaded")
        eps_set = m.sem("eps_set")
        x_squared = m.sem("x_squared")
        x_std = m.sem("x_std")
        x_rstd = m.sem("x_rstd")
        x_normed = m.sem("x_normed")
        xt_ready = m.sem("xt_ready")
        h_full = m.sem("h_full")
        h_hi_done = m.sem("h_hi_done")
        h_lo_done = m.sem("h_lo_done")
        z_ready = m.sem("z_ready")
        z_squared = m.sem("z_squared")
        z_std = m.sem("z_std")
        z_rstd = m.sem("z_rstd")
        z_normed = m.sem("z_normed")
        roped = m.sem("roped")
        u_ready = m.sem("u_ready")
        u_copied = m.sem("u_copied")
        u_stored = [m.sem(f"u_stored{i}") for i in range(2)]
        ct_ready = m.sem("ct_ready")
        ct_copied = m.sem("ct_copied")
        ct_stored = [m.sem(f"ct_stored{i}") for i in range(2)]
        kr_stored = m.sem("kr_stored")
        block = ctx.enter_context(nc.Block())

        def group(b):
            return 0 if b * TB < TILE0[1] else 1

        @block.sync
        def _(sp):
            def load(b):
                g = group(b)
                row = b * T - STARTS[g]
                src = w[("x_prompt", "x_sample")[g]][0][row:row + T, :]
                sp.dma_start(x[:, b % 2], src.rearrange("(j p) d -> p j d", p=P)).then_inc(x_loaded[b % 2], 16)

            load(0)
            for name, k0, ks in (("q_norm_g", 0, KQ), ("kv_norm_g", KQ, KKV)):
                sp.dma_start(gain[:, k0:k0 + ks], w[name][0].rearrange("(k p) -> p k", p=P),
                             allow_slow_non_contiguous=True).then_inc(rope_loaded, 16)
            sp.dma_start(rope[:], w["k_rope"].rearrange("t p a c -> p t a c")).then_inc(rope_loaded, 16)
            for k in range(KD):
                if k == 2:
                    load(1)
                if k >= 2:
                    sp.wait_ge(w_lo_done, k - 1)
                sp.dma_start(wraw[:, k % 2, :], w["w_in"][0][k * P:(k + 1) * P, :]).then_inc(w_loaded[k % 2], 16)
            for n in range(TILES):
                b = n // TB
                if n % TB == 0 and b + 2 < NB:
                    sp.wait_ge(xt_ready, KD // 2 * (b + 1))
                    load(b + 2)
                sp.wait_ge(u_copied, n + 1)
                sp.dma_start(w["s_ut"][n % TB * UG:(n % TB + 1) * UG, :, b * T:(b + 1) * T].rearrange("g p t -> p g t"),
                             ut[:, n % 2]).then_inc(u_stored[n % 2], 16)
                sp.wait_ge(ct_copied, n + 1)
                sp.dma_start(w["s_ct"][n], ct[:, n % 2]).then_inc(ct_stored[n % 2], 16)
            sp.dma_start(w["s_krt"], krt[:, :]).then_inc(kr_stored, 16)
            for i in range(2):
                sp.wait_ge(u_stored[i], 16 * TILES // 2)
                sp.wait_ge(ct_stored[i], 16 * TILES // 2)
            sp.wait_ge(kr_stored, 16)

        @block.gpsimd
        def _(pool):
            m.clear_last(pool)

        @block.scalar
        def _(act):
            def w_high(k):
                act.wait_ge(w_loaded[k % 2], 16 * (k // 2 + 1))
                nc.scalar.activation(wh[:, k, :], wraw[:, k % 2, :], ACT.Copy).then_inc(w_hi_done, 1)

            def stats(b):
                act.wait_ge(x_loaded[b % 2], 16 * (b // 2 + 1))
                for j in range(TB):
                    if TB * b + j >= 2:
                        act.wait_ge(x_squared, TB * b + j - 1)
                    sq = nc.scalar.activation(junk[:, j % 2], x[:, b % 2, j, :], ACT.Square, scale=float(D) ** -0.5,
                                              accum_out=ms[:, b, j:j + 1])
                    sq.then_inc(x_squared, 1)
                act.wait_ge(x_squared, TB * (b + 1))
                nc.scalar.activation(ms[:, b, :], ms[:, b, :], ACT.Sqrt, bias=eps[:, 0:1]).then_inc(x_std, 1)

            def modulate(b, c):
                i = KD // 2 * b + c
                act.wait_ge(xt_ready, i + 1)
                if i >= 2:
                    act.wait_ge(h_lo_done, i - 1)
                if c == 0 and b >= 2:
                    act.wait_ge(u_ready, TB * (b - 1))
                g = group(b)
                for a in range(2):
                    k = 2 * c + a
                    nc.scalar.activation(hf[:, c % 2, a, :], t_ps[c % 2][:, a * T:(a + 1) * T], ACT.Identity,
                                         bias=keep["modc"][:, g, k:k + 1],
                                         scale=keep["modc"][:, g, KD + k:KD + k + 1]).then_inc(h_full, 1)
                act.wait_ge(h_full, 2 * (i + 1))
                nc.scalar.activation(hh[:, b % 2, 2 * c:2 * c + 2, :], hf[:, c % 2], ACT.Copy).then_inc(h_hi_done, 1)

            def latent_stats(n):
                act.wait_ge(z_ready, n + 1)
                if n:
                    act.wait_ge(z_squared, 2 * n)
                sq = nc.scalar.activation(zjunk[:, 0:QL], q_ps[:, 0:QL], ACT.Square, scale=float(QL) ** -0.5,
                                          accum_out=zms[:, n, 0:1])
                sq.then_inc(z_squared, 1)
                sq = nc.scalar.activation(zjunk[:, QL:QL + KVL], kv_ps[:, 0:KVL], ACT.Square,
                                          scale=float(KVL) ** -0.5, accum_out=zms[:, n, 1:2])
                sq.then_inc(z_squared, 1)
                act.wait_ge(z_squared, 2 * (n + 1))
                nc.scalar.activation(zms[:, n, :], zms[:, n, :], ACT.Sqrt, bias=eps[:, 0:1]).then_inc(z_std, 1)

            def latent_copy(n):
                act.wait_ge(ct_ready, n + 1)
                if n >= 2:
                    act.wait_ge(ct_stored[n % 2], 16 * (n // 2))
                for k in range(KC):
                    nc.scalar.activation(ct[:, n % 2, k * P:(k + 1) * P], c_ps[k // 4][:, k % 4 * P:(k % 4 + 1) * P],
                                         ACT.Copy, scale=gain[:, k:k + 1])
                nc.scalar.activation(krt[:, n * P:(n + 1) * P], c_ps[1][0:ROPE, P:2 * P],
                                     ACT.Copy).then_inc(ct_copied, 1)

            act.wait_ge(eps_set, 1)
            act.wait_ge(rope_loaded, 48)
            stats(0)
            for k in range(2):
                w_high(k)
            for c in range(KD // 2):
                modulate(0, c)
                w_high(2 + c)
            for k in range(2 + KD // 2, KD):
                w_high(k)
            stats(1)
            for b in range(NB):
                for j in range(TB):
                    if j == 1 and b + 2 < NB:
                        stats(b + 2)
                    if b + 1 < NB:
                        modulate(b + 1, 2 * j)
                    latent_stats(TB * b + j)
                    if b + 1 < NB:
                        modulate(b + 1, 2 * j + 1)
                    latent_copy(TB * b + j)

        @block.vector
        def _(dve):
            nc.vector.memset(eps[:], EPS).then_inc(eps_set, 1)
            dve.wait_ge(rope_loaded, 48)

            def norm(b):
                dve.wait_ge(x_std, b + 1)
                nc.vector.reciprocal(ms[:, b, :], ms[:, b, :]).then_inc(x_rstd, 1)
                dve.wait_ge(x_rstd, b + 1)
                for j in range(TB):
                    nc.vector.tensor_scalar(x[:, b % 2, j, :], x[:, b % 2, j, :], ms[:, b, j:j + 1], None,
                                            ALU.mult).then_inc(x_normed, 1)

            def h_low(b, c):
                dve.wait_ge(h_hi_done, KD // 2 * b + c + 1)
                nc.vector.tensor_tensor(hl[:, b % 2, 2 * c:2 * c + 2, :], hf[:, c % 2],
                                        hh[:, b % 2, 2 * c:2 * c + 2, :].bitcast(F32),
                                        ALU.subtract).then_inc(h_lo_done, 1)

            def w_low(k):
                dve.wait_ge(w_hi_done, k + 1)
                nc.vector.tensor_tensor(wl[:, k, :], wraw[:, k % 2, :], wh[:, k, :].bitcast(F32),
                                        ALU.subtract).then_inc(w_lo_done, 1)

            norm(0)
            for k in range(2):
                w_low(k)
            for c in range(KD // 2):
                h_low(0, c)
                w_low(2 + c)
            for k in range(2 + KD // 2, KD):
                w_low(k)
            norm(1)
            for b in range(NB):
                for j in range(TB):
                    n = TB * b + j
                    if b + 1 < NB:
                        h_low(b + 1, 2 * j)
                    dve.wait_ge(z_squared, 2 * (n + 1))
                    if n:
                        dve.wait_ge(roped, 2 * n)
                    for a in range(2):
                        nc.vector.tensor_tensor(tmp[:, a, :], kv_ps[:, KVL:KVL + ROPE], rope[:, n, a, :],
                                                ALU.mult).then_inc(z_rstd, 1)
                    dve.wait_ge(z_rstd, 3 * n + 2)
                    H = ROPE // 2
                    nc.vector.tensor_tensor(kr[:, n, 0:H], tmp[:, 0, 0:H], tmp[:, 1, H:ROPE],
                                            ALU.subtract).then_inc(roped, 1)
                    nc.vector.tensor_tensor(kr[:, n, H:ROPE], tmp[:, 0, H:ROPE], tmp[:, 1, 0:H],
                                            ALU.add).then_inc(roped, 1)
                    dve.wait_ge(z_std, n + 1)
                    nc.vector.reciprocal(zms[:, n, :], zms[:, n, :]).then_inc(z_rstd, 1)
                    dve.wait_ge(z_rstd, 3 * n + 3)
                    if n >= 2:
                        dve.wait_ge(ct_ready, n - 1)
                    nc.vector.tensor_scalar(zr[:, n % 2, 0:QL], q_ps[:, 0:QL], zms[:, n, 0:1], None,
                                            ALU.mult).then_inc(z_normed, 1)
                    nc.vector.tensor_scalar(zr[:, n % 2, QL:QL + KVL], kv_ps[:, 0:KVL], zms[:, n, 1:2], None,
                                            ALU.mult).then_inc(z_normed, 1)
                    if b + 1 < NB:
                        h_low(b + 1, 2 * j + 1)
                    dve.wait_ge(u_ready, n + 1)
                    if n >= 2:
                        dve.wait_ge(u_stored[n % 2], 16 * (n // 2))
                    nc.vector.tensor_copy(ut[:, n % 2].rearrange("p g t -> p (g t)"), u_ps[n % 2][:, :]
                                          ).then_inc(u_copied, 1)
                    if j == 1 and b + 2 < NB:
                        norm(b + 2)

        @block.tensor
        def _(pe):
            def turn(b, c):
                i = KD // 2 * b + c
                if c == 0:
                    pe.wait_ge(x_normed, TB * (b + 1))
                if i >= 2:
                    pe.wait_ge(h_full, 2 * (i - 1))
                for a in range(2):
                    k = 2 * c + a
                    for j in range(TB):
                        mm = nc.tensor.transpose(t_ps[c % 2][:, (a * TB + j) * P:(a * TB + j + 1) * P],
                                                 x[:, b % 2, j, k * P:(k + 1) * P], keep["ident"][:, :])
                mm.then_inc(xt_ready, 1)

            def product(out, a_hi, a_lo, b_hi, b_lo, k):
                nc.tensor.matmul(out, a_hi, b_hi, start=(k == 0), stop=False)
                nc.tensor.matmul(out, a_hi, b_lo, start=False, stop=False)
                return nc.tensor.matmul(out, a_lo, b_hi, start=False, stop=(k == KD - 1))

            for c in range(KD // 2):
                turn(0, c)
            for b in range(NB):
                for j in range(TB):
                    n = TB * b + j
                    if n:
                        pe.wait_ge(z_normed, 2 * n)
                        pe.wait_ge(roped, 2 * n)
                        pe.wait_ge(z_squared, 2 * n)
                    token = slice(j * P, (j + 1) * P)
                    if b + 1 < NB:
                        turn(b + 1, 2 * j)
                    for ps, c0, size in ((q_ps, 0, QL), (kv_ps, QL, KVL + ROPE)):
                        for k in range(KD):
                            if j == 0 and c0 == 0 and k % 2 == 0:
                                pe.wait_ge(h_lo_done, KD // 2 * b + k // 2 + 1)
                            if n == 0 and c0 == 0:
                                pe.wait_ge(w_lo_done, k + 1)
                            mm = product(ps[:, 0:size], hh[:, b % 2, k, token], hl[:, b % 2, k, token],
                                         wh[:, k, c0:c0 + size], wl[:, k, c0:c0 + size], k)
                    mm.then_inc(z_ready, 1)
                    if b + 1 < NB:
                        turn(b + 1, 2 * j + 1)
                    if n >= 2:
                        pe.wait_ge(u_copied, n - 1)
                    for i in range(UG):
                        c0 = QL + KVL + ROPE + (j * UG + i) * P
                        for k in range(KD):
                            mm = product(u_ps[n % 2][:, i * T:(i + 1) * T], wh[:, k, c0:c0 + P], wl[:, k, c0:c0 + P],
                                         hh[:, b % 2, k, :], hl[:, b % 2, k, :], k)
                    mm.then_inc(u_ready, 1)
                    pe.wait_ge(z_normed, 2 * (n + 1))
                    if n:
                        pe.wait_ge(ct_copied, n)
                    for c in range(KC):
                        mm = nc.tensor.transpose(c_ps[c // 4][:, c % 4 * P:(c % 4 + 1) * P],
                                                 zr[:, n % 2, c * P:(c + 1) * P], keep["ident"][:, :])
                    pe.wait_ge(roped, 2 * (n + 1))
                    mm = nc.tensor.transpose(c_ps[1][0:ROPE, P:2 * P], kr[:, n, :], keep["ident"][:, :])
                    mm.then_inc(ct_ready, 1)


def attention(nc, w, keep, g):
    S = SEQS[g]
    NT = S // P
    NQB = S // BANK
    CB = BANK // P
    NG = 2 * NQB
    PER = NG * NT
    PAIRS = HEADS // 2
    RING = 4
    MB = 3
    LAG = 3
    KSTEP = 1 if NT == 8 else 2
    DEN = LAG + 2 if NT == 8 else LAG + 4
    SPREAD = DEN + 1 if NT == 8 else DEN + 3
    UNITS = [[u for u in range(NT) if 1 + u * (NT - 3) // NT == kt] for kt in range(NT)]
    V_PIECES = 4
    VP = NT // V_PIECES
    SUMS = NT - 2
    WQ_IN = 3 * 16
    SCALE = float(QK) ** -0.5
    t0 = TILE0[g]
    with ExitStack() as ctx:
        m = Pools(nc, ctx, f"att{g}")
        ct = m.sb("ct", [P, NT, KC * P])
        wk_all = m.sb("wk_all", [P, KKV, HEADS, NOPE])
        v_all = m.sb("v_all", [P, NT, HEADS * VD])
        v = m.sb("v", [P, 2, NT, 2 * VD], F32R)
        wq = m.sb("wq", [P, 2, KQ, P])
        wk = m.sb("wk", [P, 2, KKV, NOPE])
        lower = m.sb("lower", [P, max(SEQS) // BANK, BANK])
        rope = lower[:].rearrange("p r n -> p (r n)")
        olo, osum = (lower[0:VD, i, :] for i in range(2))
        qh = m.sb("qh", [P, 2, S], F32R)
        ql = m.sb("ql", [P, 2, S], F32R)
        kh = m.sb("kh", [P, 2, S], F32R)
        kl = m.sb("kl", [P, 2, S], F32R)
        qf = m.sb("qf", [P, BANK])
        upper = m.sb("upper", [P, 2, BANK])
        att, prod = upper[0:VD], upper[NOPE:QK]
        e = m.sb("e", [P, RING, BANK])
        pr = m.sb("pr", [P, RING, 2, BANK], F32R)
        acc = m.sb("acc", [P, 2, 2, BANK])
        wv = acc[:, 0]
        ones = m.sb("ones", [P, 1])
        mx = m.sb("mx", [P, CB, NQB])
        nmx = m.sb("nmx", [P, CB])
        rden = m.sb("rden", [P, CB])
        s_ps = [m.ps(f"s_ps{i}") for i in range(2)]
        m_ps = [m.ps(f"m_ps{i}") for i in range(MB)]
        o_ps = [m.ps(f"o_ps{i}") for i in range(2)]
        x_ps = m.ps("x_ps")
        ct_in = [m.sem(f"ct_in{i}") for i in range(2)]
        wkv_in = m.sem("wkv_in")
        wk_in = m.sem("wk_in")
        tabs_in = m.sem("tabs_in")
        kpe_in = m.sem("kpe_in")
        wq_in = [m.sem(f"wq_in{i}") for i in range(2)]
        wk_done = m.sem("wk_done")
        rows_set = m.sem("rows_set")
        v_ready = m.sem("v_ready")
        v_even_copied = m.sem("v_even_copied")
        v_odd_copied = m.sem("v_odd_copied")
        v_hi_done = m.sem("v_hi_done")
        v_lo_done = m.sem("v_lo_done")
        kpe_hi_done = m.sem("kpe_hi_done")
        kpe_lo_done = m.sem("kpe_lo_done")
        k_ready = m.sem("k_ready")
        k_hi_done = m.sem("k_hi_done")
        k_lo_done = m.sem("k_lo_done")
        q_ready = m.sem("q_ready")
        q_nope_copied = m.sem("q_nope_copied")
        q_prod_done = m.sem("q_prod_done")
        q_added = m.sem("q_added")
        q_hi_done = m.sem("q_hi_done")
        q_lo_done = m.sem("q_lo_done")
        unit_ready = m.sem("unit_ready")
        max_part = m.sem("max_part")
        nmx_ready = m.sem("nmx_ready")
        nmx_turned = m.sem("nmx_turned")
        row_done = m.sem("row_done")
        scores_ready = m.sem("scores_ready")
        exp_done = m.sem("exp_done")
        hi_done = m.sem("hi_done")
        lo_done = m.sem("lo_done")
        sum_done = m.sem("sum_done")
        values_done = m.sem("values_done")
        olo_done = m.sem("olo_done")
        den_ready = m.sem("den_ready")
        rden_done = m.sem("rden_done")
        rden_spread = m.sem("rden_spread")
        osum_done = m.sem("osum_done")
        att_done = m.sem("att_done")
        att_stored = [m.sem(f"att_stored{i}") for i in range(2)]
        block = ctx.enter_context(nc.Block())

        def over_pairs(eng, body):
            body(0, False)
            with eng.Fori(1, PAIRS - 1) as hp:
                body(hp, False)
            body(PAIRS - 1, True)

        def from_start(hp, i):
            return i >= 0 or not (isinstance(hp, int) and hp == 0)

        def at(s):
            b = s // NT
            return b, s % NT, b // NQB % 2, b % NQB

        def summed(s):
            return (1, 1, 2, 2)[s % NT] if s % NT < 4 else s % NT - 1

        def projects(hp, b, last):
            return from_start(hp, b) and not (last and b >= NQB)

        def after(b):
            return (b + 1) // NQB % 2, (b + 1) % NQB

        def cols(j):
            return slice(j * BANK, (j + 1) * BANK)

        @block.sync
        def _(sp):
            def load_weights(n, par):
                H = ROPE // 2
                src = w["w_uq"][0].rearrange("(k p) n -> p k n", p=P)
                for dst, at, width in ((0, 0, QK), (QK, QK - H, H), (QK + H, NOPE, H)):
                    sp.dma_start(wq[:, par, :, dst:dst + width], src[:, :, bass.ds(n * QK + at, width)],
                                 ).then_inc(wq_in[par], 16)

            src = w["w_ukv"][0].rearrange("(k p) (h c) -> k p h c", p=P, h=HEADS)
            for k in range(KKV):
                sp.dma_start(wv[:, k].rearrange("p (h c) -> p h c", h=HEADS), src[k][:, :, NOPE:]).then_inc(wkv_in, 16)
            for i in range(2):
                half = slice(i * NT // 2, (i + 1) * NT // 2)
                sp.dma_start(ct[:, half], w["s_ct"][t0:t0 + NT][half].rearrange("t p c -> p t c")).then_inc(ct_in[i], 16)
            load_weights(0, 0)
            for k in range(KKV):
                sp.dma_start(wk_all[:, k], src[k][:, :, 0:NOPE]).then_inc(wk_in, 16)
            sp.dma_start(rope[NOPE:P, 0:S], w["k_rope_t"][:, 0:S]).then_inc(tabs_in, 16)
            sp.dma_start(e[NOPE:QK].rearrange("p r n -> p (r n)")[:, 0:S],
                         w["s_krt"][:, STARTS[g]:STARTS[g] + S]).then_inc(kpe_in, 16)
            load_weights(1, 1)

            def body(hp, last):
                for b in range(NG):
                    h, j = b // NQB, b % NQB
                    if j == 0 and not last:
                        sp.wait_ge(q_ready, hp * NG + (h + 1) * NQB)
                        load_weights(hp * 2 + h + 2, h)
                    sp.wait_ge(att_done, hp * NG + b + 1)
                    sp.dma_start(w["s_att"][bass.ds(hp * 2 * VD + h * VD, VD),
                                            STARTS[g] + j * BANK:STARTS[g] + (j + 1) * BANK],
                                 att[:, b % 2, :]).then_inc(att_stored[b % 2], 16)

            over_pairs(sp, body)
            for i in range(2):
                sp.wait_ge(att_stored[i], 16 * PAIRS * NQB)

        @block.tensor
        def _(pe):
            def project_k(out, j, k0):
                for k in range(KKV):
                    mm = nc.tensor.matmul(out[0:NOPE, :], wk[:, k0, k, :], ct_cols(KQ + k, j),
                                          start=(k == 0), stop=(k == KKV - 1))
                mm.then_inc(k_ready, 1)

            def ct_cols(k, j):
                return ct[:, j * CB:(j + 1) * CB, k * P:(k + 1) * P]

            def project_q(par, j):
                for k in range(KQ):
                    mm = nc.tensor.matmul(x_ps[:, :], wq[:, par, k, :], ct_cols(k, j),
                                          start=(k == 0), stop=(k == KQ - 1))
                mm.then_inc(q_ready, 1)

            def unit(par, j, u):
                kb, c = u // CB, u % CB
                at = j * BANK + c * P
                nc.tensor.matmul(m_ps[u % MB][:, :], qh[0:QK, par, at:at + P], kh[0:QK, par, cols(kb)],
                                 start=True, stop=True).then_inc(unit_ready, 1)

            def turn_maxima(bank):
                for c in range(CB):
                    mm = nc.tensor.transpose(o_ps[bank][0:1, c * P:(c + 1) * P], nmx[:, c:c + 1], keep["ident"][:, :])
                mm.then_inc(nmx_turned, 1)

            pe.wait_ge(wkv_in, 16 * KKV)
            for t in range(NT):
                if t % (NT // 2) == 0:
                    pe.wait_ge(ct_in[t // (NT // 2)], 16)
                if t >= MB:
                    if (t - MB) % 2 == 0:
                        pe.wait_ge(v_even_copied, (t - MB) // 2 + 1)
                    else:
                        pe.wait_ge(v_odd_copied, (t - MB) // 2 + 1)
                for k in range(KKV):
                    mm = nc.tensor.matmul(m_ps[t % MB][:, :], ct[:, t, (KQ + k) * P:(KQ + k + 1) * P], wv[:, k, :],
                                          start=(k == 0), stop=(k == KKV - 1))
                mm.then_inc(v_ready, 1)
            pe.wait_ge(wq_in[0], WQ_IN)
            pe.wait_ge(wk_done, 1)
            for j in range(NQB):
                if j >= 2:
                    pe.wait_ge(k_lo_done, j - 1)
                project_k(o_ps[j % 2], j, 0)
                if j >= 1:
                    pe.wait_ge(q_nope_copied, j)
                    pe.wait_ge(q_prod_done, 2 * j)
                project_q(0, j)
            pe.wait_ge(v_even_copied, NT // 2)
            pe.wait_ge(v_odd_copied, NT // 2)
            pe.wait_ge(q_hi_done, 1)
            pe.wait_ge(k_hi_done, NQB)
            pe.wait_ge(kpe_hi_done, 2)
            for u in range(NT):
                if u >= MB:
                    pe.wait_ge(max_part, u - MB + 1)
                unit(0, 0, u)
            pe.wait_ge(q_nope_copied, NQB)
            pe.wait_ge(q_prod_done, 2 * NQB)
            pe.wait_ge(nmx_ready, 1)
            turn_maxima(1)
            pe.wait_ge(rows_set, 4)
            pe.wait_ge(kpe_lo_done, 2)

            def scores(hp, s):
                b, kt, h, j = at(s)
                if kt == 0:
                    pe.wait_ge(row_done, hp * NG + b + 1)
                    pe.wait_ge(q_lo_done, hp * NG + b + 1)
                    if j == 0:
                        pe.wait_ge(k_lo_done, hp * NG + (h + 1) * NQB)
                if from_start(hp, s - 2):
                    pe.wait_ge(exp_done, hp * PER + s - 1)
                out = s_ps[s % 2][:, :]
                k_hi, k_lo = (x[0:QK + 1, h, kt * P:(kt + 1) * P] for x in (kh, kl))
                q_hi, q_lo = (x[0:QK + 1, h, cols(j)] for x in (qh, ql))
                nc.tensor.matmul(out, k_hi, q_hi, start=True, stop=False)
                nc.tensor.matmul(out, k_hi, q_lo, start=False, stop=False)
                nc.tensor.matmul(out, k_lo, q_hi, start=False, stop=True).then_inc(scores_ready, 1)

            def values(hp, s):
                b, kt, h, j = at(s)
                if kt == 0:
                    if j == 0:
                        pe.wait_ge(v_lo_done, (hp * 2 + h + 1) * V_PIECES)
                    if from_start(hp, b - 2):
                        pe.wait_ge(att_done, hp * NG + b - 1)
                pe.wait_ge(lo_done, hp * PER + s + 1)
                for a in range(2):
                    mm = nc.tensor.matmul(o_ps[b % 2][:, :], v[:, h, kt, :], pr[:, s % RING, a, :],
                                          start=(kt == 0 and a == 0), stop=(kt == NT - 1 and a == 1))
                mm.then_inc(values_done, 1)

            def denominators(hp, b):
                pe.wait_ge(sum_done, (hp * NG + b + 1) * SUMS)
                pe.wait_ge(osum_done, hp * NG + b + 1)
                for c in range(CB):
                    for i in range(2):
                        mm = nc.tensor.matmul(o_ps[b % 2][:, c:c + 1], acc[:, b % 2, i, c * P:(c + 1) * P],
                                              ones[:, :], start=(i == 0), stop=(i == 1))
                mm.then_inc(den_ready, 1)

            def spread_inverses(hp, b):
                pe.wait_ge(rden_done, hp * NG + b + 1)
                for c in range(CB):
                    mm = nc.tensor.matmul(o_ps[b % 2][0:VD, c * P:(c + 1) * P],
                                          rden[:, c:c + 1].broadcast_to([P, VD]), keep["ident"][:, :],
                                          start=True, stop=True)
                mm.then_inc(rden_spread, 1)

            def body(hp, last):
                for s in range(PER):
                    b, kt, h, j = at(s)
                    project = not (last and h == 1)
                    if kt == NT - 1 and not (last and b == NG - 1):
                        pe.wait_ge(nmx_ready, hp * NG + b + 2)
                        if from_start(hp, b - 1):
                            pe.wait_ge(att_done, hp * NG + b)
                        turn_maxima((b - 1) % 2)
                    scores(hp, s)
                    if kt == KSTEP and project:
                        if j == 0:
                            pe.wait_ge(wq_in[1 - h], WQ_IN * (hp + 1 + h))
                            pe.wait_ge(wk_done, hp * 2 + h + 2)
                        pe.wait_ge(q_nope_copied, hp * NG + NQB + b)
                        pe.wait_ge(q_prod_done, 2 * (hp * NG + NQB + b))
                        project_k(x_ps, j, 1 - h)
                    if not (last and b == NG - 1):
                        par, nj = after(b)
                        for u in UNITS[kt]:
                            if u == 0:
                                pe.wait_ge(q_hi_done, hp * NG + b + 2)
                            if nj == 0 and u % CB == 0:
                                pe.wait_ge(k_hi_done, hp * NG + (h + 1) * NQB + u // CB + 1)
                            pe.wait_ge(max_part, (hp * NG + b + 1) * NT + max(u - MB + 1, 0))
                            unit(par, nj, u)
                    if from_start(hp, s - LAG):
                        values(hp, s - LAG)
                    if kt == NT - 2 and project:
                        pe.wait_ge(k_lo_done, hp * NG + NQB + b + 1)
                        project_q(1 - h, j)
                    if kt == DEN and from_start(hp, b - 1):
                        denominators(hp, b - 1)
                    if kt == SPREAD and from_start(hp, b - 1):
                        spread_inverses(hp, b - 1)

            over_pairs(pe, body)
            for s in range(-LAG, 0):
                values(PAIRS, s)
            denominators(PAIRS, -1)
            spread_inverses(PAIRS, -1)

        @block.scalar
        def _(act):
            def k_high(src, par, j):
                nc.scalar.activation(kh[0:NOPE, par, cols(j)], src[0:NOPE, :], ACT.Copy).then_inc(k_hi_done, 1)

            def q_nope():
                nc.scalar.activation(qf[0:NOPE, :], x_ps[0:NOPE, :], ACT.Copy).then_inc(q_nope_copied, 1)

            def q_high(par, j):
                nc.scalar.activation(qh[0:QK, par, cols(j)], qf[0:QK, :], ACT.Copy).then_inc(q_hi_done, 1)

            def v_high(n, par, i):
                tiles = slice(i * VP, (i + 1) * VP)
                nc.scalar.activation(v[:, par, tiles, 0:VD], v_all[:, tiles, bass.ds(n * VD, VD)],
                                     ACT.Copy).then_inc(v_hi_done, 1)

            def max_row(bank, par, j):
                nc.scalar.activation(qh[QK:QK + 1, par, cols(j)], o_ps[bank][0:1, :], ACT.Copy).then_inc(row_done, 1)

            act.wait_ge(kpe_in, 16)
            for par in range(2):
                nc.scalar.activation(kh[NOPE:QK, par, :], e[NOPE:QK].rearrange("p r n -> p (r n)")[:, 0:S],
                                     ACT.Copy).then_inc(kpe_hi_done, 1)
            for t in range(0, NT, 2):
                act.wait_ge(v_ready, t + 1)
                nc.scalar.activation(v_all[:, t, :], m_ps[t % MB][:, :], ACT.Copy).then_inc(v_even_copied, 1)
            for j in range(NQB):
                act.wait_ge(k_ready, j + 1)
                k_high(o_ps[j % 2], 0, j)
                act.wait_ge(q_ready, j + 1)
                if j >= 1:
                    act.wait_ge(q_lo_done, j)
                q_nope()
                act.wait_ge(q_nope_copied, j + 1)
                act.wait_ge(q_added, j + 1)
                q_high(0, j)
            act.wait_ge(v_even_copied, NT // 2)
            act.wait_ge(v_odd_copied, NT // 2)
            for i in range(V_PIECES):
                v_high(0, 0, i)
            act.wait_ge(nmx_turned, 1)
            max_row(1, 0, 0)
            act.wait_ge(kpe_lo_done, 2)

            def exps(hp, s):
                act.wait_ge(scores_ready, hp * PER + s + 1)
                if from_start(hp, s - RING):
                    old = s - RING
                    act.wait_ge(lo_done, hp * PER + old + 1)
                    act.wait_ge(sum_done, (hp * NG + old // NT) * SUMS + summed(old))
                nc.scalar.activation(e[:, s % RING, :], s_ps[s % 2][:, :], ACT.Exp, scale=SCALE).then_inc(exp_done, 1)

            def high(hp, s):
                act.wait_ge(exp_done, hp * PER + s + 1)
                if from_start(hp, s - RING):
                    act.wait_ge(values_done, hp * PER + s - RING + 1)
                nc.scalar.activation(pr[:, s % RING, 0, :], e[:, s % RING, :], ACT.Copy).then_inc(hi_done, 1)

            def output_low(hp, b):
                act.wait_ge(values_done, hp * PER + (b + 1) * NT)
                if from_start(hp, b - 1):
                    act.wait_ge(osum_done, hp * NG + b)
                nc.scalar.activation(olo, o_ps[b % 2][VD:P, :], ACT.Copy).then_inc(olo_done, 1)

            def body(hp, last):
                for s in range(PER):
                    b, kt, h, j = at(s)
                    project = not (last and h == 1)
                    if kt == NT - 1 and not (last and b == NG - 1):
                        act.wait_ge(nmx_turned, hp * NG + b + 2)
                        max_row((b - 1) % 2, *after(b))
                    exps(hp, s)
                    if from_start(hp, s - 1):
                        high(hp, s - 1)
                    if kt == KSTEP + 1 and project:
                        act.wait_ge(k_ready, hp * NG + NQB + b + 1)
                        k_high(x_ps, 1 - h, j)
                    if kt == LAG and from_start(hp, b - 1):
                        output_low(hp, b - 1)
                    if project and kt == NT - 1:
                        act.wait_ge(q_ready, hp * NG + NQB + b + 1)
                        act.wait_ge(q_lo_done, hp * NG + NQB + b)
                        q_nope()
                    if kt == 0 and projects(hp, b - 1, last):
                        act.wait_ge(q_nope_copied, hp * NG + NQB + b)
                        act.wait_ge(q_added, hp * NG + NQB + b)
                        pb = b - 1
                        q_high(1 - pb // NQB % 2, pb % NQB)
                    if project and j == 1 and kt < V_PIECES:
                        if kt == 0 and from_start(hp, h - 1):
                            act.wait_ge(values_done, hp * PER + h * (PER // 2))
                        v_high(hp * 2 + h + 1, 1 - h, kt)

            over_pairs(act, body)
            high(PAIRS, -1)
            output_low(PAIRS, -1)

        @block.vector
        def _(dve):
            def k_low(src, par, j):
                nc.vector.tensor_tensor(kl[0:NOPE, par, cols(j)], src[0:NOPE, :],
                                        kh[0:NOPE, par, cols(j)].bitcast(F32), ALU.subtract).then_inc(k_lo_done, 1)

            def q_products(j):
                for a in range(2):
                    rows = slice(NOPE + a * ROPE, NOPE + (a + 1) * ROPE)
                    nc.vector.tensor_tensor(prod[:, a, :], x_ps[rows, :], rope[rows, cols(j)],
                                            ALU.mult).then_inc(q_prod_done, 1)

            def v_low(n, par, i):
                tiles = slice(i * VP, (i + 1) * VP)
                nc.vector.tensor_tensor(v[:, par, tiles, VD:2 * VD], v_all[:, tiles, bass.ds(n * VD, VD)],
                                        v[:, par, tiles, 0:VD].bitcast(F32), ALU.subtract).then_inc(v_lo_done, 1)

            def reduce_unit(u):
                nc.vector.tensor_reduce(mx[:, u % CB, u // CB:u // CB + 1], m_ps[u % MB][:, :], AX,
                                        ALU.max).then_inc(max_part, 1)

            def combine():
                nc.vector.tensor_reduce(nmx[:, :], mx[:], AX, ALU.max, negate=True).then_inc(nmx_ready, 1)

            def k_weights(n, par):
                nc.vector.tensor_copy(wk[:, par], wk_all[:, :, bass.ds(n, 1), :].rearrange("p k o c -> p k (o c)")).then_inc(wk_done, 1)

            nc.vector.memset(ones[:, :], 1.0).then_inc(rows_set, 1)
            dve.wait_ge(wk_in, 16 * KKV)
            k_weights(0, 0)
            k_weights(1, 1)
            for t in range(1, NT, 2):
                dve.wait_ge(v_ready, t + 1)
                nc.vector.tensor_copy(v_all[:, t, :], m_ps[t % MB][:, :]).then_inc(v_odd_copied, 1)
            dve.wait_ge(tabs_in, 16)
            for j in range(NQB):
                dve.wait_ge(k_hi_done, j + 1)
                k_low(o_ps[j % 2], 0, j)
                dve.wait_ge(q_ready, j + 1)
                if j >= 1:
                    dve.wait_ge(q_added, j)
                q_products(j)
            for u in range(NT):
                dve.wait_ge(unit_ready, u + 1)
                reduce_unit(u)
            dve.wait_ge(max_part, NT)
            combine()
            for par in range(2):
                dve.wait_ge(kpe_hi_done, par + 1)
                nc.vector.tensor_tensor(kl[NOPE:QK, par, :], e[NOPE:QK].rearrange("p r n -> p (r n)")[:, 0:S],
                                        kh[NOPE:QK, par, :].bitcast(F32), ALU.subtract).then_inc(kpe_lo_done, 1)
            for i in range(V_PIECES):
                dve.wait_ge(v_hi_done, i + 1)
                v_low(0, 0, i)

            def low(hp, s):
                dve.wait_ge(hi_done, hp * PER + s + 1)
                nc.vector.tensor_tensor(pr[:, s % RING, 1, :], e[:, s % RING, :],
                                        pr[:, s % RING, 0, :].bitcast(F32), ALU.subtract).then_inc(lo_done, 1)

            def output_sum(hp, b):
                dve.wait_ge(olo_done, hp * NG + b + 1)
                nc.vector.tensor_tensor(osum, o_ps[b % 2][0:VD, :], olo, ALU.add).then_inc(osum_done, 1)

            def inverse(hp, b):
                dve.wait_ge(den_ready, hp * NG + b + 1)
                nc.vector.reciprocal(rden[:, :], o_ps[b % 2][:, 0:CB]).then_inc(rden_done, 1)

            def output(hp, b):
                dve.wait_ge(osum_done, hp * NG + b + 1)
                dve.wait_ge(rden_spread, hp * NG + b + 1)
                if from_start(hp, b - 2):
                    dve.wait_ge(att_stored[b % 2], 16 * (hp * NQB + b // 2))
                nc.vector.tensor_tensor(att[:, b % 2, :], osum, o_ps[b % 2][0:VD, :], ALU.mult).then_inc(att_done, 1)

            def body(hp, last):
                for s in range(PER):
                    b, kt, h, j = at(s)
                    project = not (last and h == 1)
                    if not (last and b == NG - 1):
                        for u in UNITS[kt]:
                            dve.wait_ge(unit_ready, (hp * NG + b + 1) * NT + u + 1)
                            reduce_unit(u)
                    if from_start(hp, s - 1):
                        low(hp, s - 1)
                    if kt == KSTEP + 1 and project:
                        dve.wait_ge(k_hi_done, hp * NG + NQB + b + 1)
                        k_low(x_ps, 1 - h, j)
                    if kt == 2 and project and j == NQB - 1 and not (last and h == 0):
                        k_weights(hp * 2 + h + 2, h)
                    if from_start(hp, b - 1):
                        if kt == LAG + 1:
                            output_sum(hp, b - 1)
                        if kt == DEN + 1:
                            inverse(hp, b - 1)
                        if kt == SPREAD + (0 if NT == 8 else 1):
                            output(hp, b - 1)
                    if project and kt == NT - 1:
                        dve.wait_ge(q_ready, hp * NG + NQB + b + 1)
                        dve.wait_ge(q_added, hp * NG + NQB + b)
                        q_products(j)
                    if project and j == 1 and kt < V_PIECES:
                        dve.wait_ge(v_hi_done, (hp * 2 + h + 1) * V_PIECES + kt + 1)
                        v_low(hp * 2 + h + 1, 1 - h, kt)
                    if not (last and b == NG - 1):
                        if kt == NT - 2:
                            dve.wait_ge(max_part, (hp * NG + b + 2) * NT)
                            dve.wait_ge(nmx_turned, hp * NG + b + 1)
                            combine()

            over_pairs(dve, body)
            low(PAIRS, -1)
            output_sum(PAIRS, -1)
            inverse(PAIRS, -1)
            output(PAIRS, -1)

        @block.gpsimd
        def _(pool):
            def q_sum():
                nc.gpsimd.tensor_tensor(qf[NOPE:QK, :], prod[:, 0, :], prod[:, 1, :],
                                        ALU.add).then_inc(q_added, 1)

            def q_low(par, j):
                nc.gpsimd.tensor_tensor(ql[0:QK, par, cols(j)], qf[0:QK, :], qh[0:QK, par, cols(j)].bitcast(F32),
                                        ALU.subtract).then_inc(q_lo_done, 1)

            m.clear_last(pool)
            for rows, value in ((kh, 1.0), (kl, 0.0), (ql, 0.0)):
                nc.gpsimd.memset(rows[QK:QK + 1].bitcast(F32), value).then_inc(rows_set, 1)
            for j in range(NQB):
                pool.wait_ge(q_prod_done, 2 * (j + 1))
                if j >= 1:
                    pool.wait_ge(q_lo_done, j)
                q_sum()
                pool.wait_ge(q_hi_done, j + 1)
                q_low(0, j)

            def body(hp, last):
                for s in range(PER):
                    b, kt, h, j = at(s)
                    project = not (last and h == 1)
                    if kt == 0 and projects(hp, b - 1, last):
                        pb = b - 1
                        pool.wait_ge(q_prod_done, 2 * (hp * NG + NQB + b))
                        pool.wait_ge(sum_done, (hp * NG + b) * SUMS)
                        q_sum()
                        pool.wait_ge(q_hi_done, hp * NG + NQB + b)
                        q_low(1 - pb // NQB % 2, pb % NQB)
                    if kt in (1, 3):
                        pool.wait_ge(exp_done, hp * PER + s + 1)
                        if kt == 1:
                            pool.wait_ge(q_lo_done, hp * NG + NQB + (min(b, NQB) if last else b))
                            if from_start(hp, b - 2):
                                pool.wait_ge(den_ready, hp * NG + b - 1)
                        nc.gpsimd.tensor_tensor(acc[:, b % 2, kt // 2, :], e[:, (s - 1) % RING, :],
                                                e[:, s % RING, :], ALU.add).then_inc(sum_done, 1)
                    elif kt >= 4:
                        pool.wait_ge(exp_done, hp * PER + s + 1)
                        pool.wait_ge(sum_done, (hp * NG + b) * SUMS + kt - 3)
                        nc.gpsimd.tensor_tensor(acc[:, b % 2, kt % 2, :], acc[:, b % 2, kt % 2, :],
                                                e[:, s % RING, :], ALU.add).then_inc(sum_done, 1)

            over_pairs(pool, body)


def pooling(nc, w, keep):
    W = len(WINDOWS)
    PAD = max(WINDOWS) // 2
    WIDTH = max(SEQS) + 2 * PAD
    jobs = [(g, c) for g in (1, 0) for c in range(W)]
    with ExitStack() as ctx:
        m = Pools(nc, ctx, "mix")
        u = m.sb("u", [P, 2, WIDTH])
        sums = m.sb("sums", [P, 2, WIDTH])
        diff = m.sb("diff", [P, 2, max(SEQS)])
        edge = m.sb("edge", [P, W, 2 * PAD])
        ends = m.sb("ends", [P, 2 * PAD])
        out = m.sb("out", [P, 2, max(SEQS)])
        wp = m.sb("wp", [P, W, P])
        scale = m.sb("scale", [P, W])
        y_ps = [m.ps(f"y_ps{i}") for i in range(2)]
        tabs_in = m.sem("tabs_in")
        pads_set = m.sem("pads_set")
        u_in = [m.sem(f"u_in{i}") for i in range(2)]
        summed = m.sem("summed")
        diff_ready = m.sem("diff_ready")
        y_ready = m.sem("y_ready")
        y_copied = m.sem("y_copied")
        stored = [m.sem(f"stored{i}") for i in range(2)]
        block = ctx.enter_context(nc.Block())
        banks = [SEQS[g] // BANK for g, _ in jobs]

        @block.gpsimd
        def _(pool):
            m.clear_last(pool)

        @block.sync
        def _(sp):
            sp.dma_start(wp[:], w["w_pool"][0].rearrange("g c d -> c g d")).then_inc(tabs_in, 16)
            sp.dma_start(edge[:].rearrange("p a b -> p (a b)"), w["k_edge"].partition_broadcast(P)).then_inc(tabs_in, 16)
            sp.dma_start(scale[:, :], w["pool_scale"][0].rearrange("(g p) -> p g", p=P),
                         allow_slow_non_contiguous=True).then_inc(tabs_in, 16)
            sp.wait_ge(pads_set, 2)
            for n, (g, c) in enumerate(jobs):
                if n >= 2:
                    sp.wait_ge(diff_ready, n - 1)
                S = SEQS[g]
                if n in (W, W + 1):
                    sp.wait_ge(pads_set, 3 + n - W)
                sp.dma_start(u[:, n % 2, PAD:PAD + S], w["s_ut"][c, :, STARTS[g]:STARTS[g] + S]).then_inc(u_in[n % 2], 16)

        @block.vector
        def _(dve):
            step = sequence(summed)
            for i in range(2):
                nc.vector.memset(u[:, i, :], 0.0).then_inc(pads_set, 1)
            dve.wait_ge(tabs_in, 48)
            for n, (g, c) in enumerate(jobs):
                S = SEQS[g]
                x, a = u[:, n % 2], sums
                dve.wait_ge(u_in[n % 2], 16 * (n // 2 + 1))
                done = step(nc.vector.tensor_tensor(a[:, 0, 1:S + 2 * PAD], x[:, 0:S + 2 * PAD - 1],
                                                    x[:, 1:S + 2 * PAD], ALU.add))
                for lev in range(1, c + 1):
                    r = 1 << (lev - 1)
                    lo, hi = 2 * r, S + 2 * PAD - 2 * r + 1
                    src, dst = a[:, (lev - 1) % 2], a[:, lev % 2]
                    dve.wait_ge(summed, done)
                    done = step(nc.vector.tensor_tensor(dst[:, lo:hi], src[:, lo - r:hi - r], src[:, lo + r:hi + r],
                                                        ALU.add))
                total = a[:, c % 2]
                dve.wait_ge(summed, done)
                if n >= 2:
                    dve.wait_ge(y_ready, sum(banks[:n - 1]))
                step(nc.vector.scalar_tensor_tensor(diff[:, n % 2, PAD:S - PAD], total[:, 2 * PAD:S],
                                                    1.0 / WINDOWS[c], x[:, 2 * PAD:S], ALU.mult, ALU.subtract))
                for k, at in enumerate((0, S - PAD)):
                    done = step(nc.vector.tensor_tensor(ends[:, k * PAD:(k + 1) * PAD],
                                                        total[:, PAD + at:2 * PAD + at],
                                                        edge[:, c, k * PAD:(k + 1) * PAD], ALU.mult))
                dve.wait_ge(summed, done)
                for k, at in enumerate((0, S - PAD)):
                    last = nc.vector.tensor_tensor(diff[:, n % 2, at:at + PAD], ends[:, k * PAD:(k + 1) * PAD],
                                                   x[:, PAD + at:2 * PAD + at], ALU.subtract)
                last.then_inc(diff_ready, 1)
                dve.wait_ge(diff_ready, n + 1)
                if n in (W - 2, W - 1):
                    nc.vector.memset(x[:, PAD + SEQS[0]:], 0.0).then_inc(pads_set, 1)

        @block.tensor
        def _(pe):
            pe.wait_ge(tabs_in, 48)
            q = 0
            for n, (g, c) in enumerate(jobs):
                pe.wait_ge(diff_ready, n + 1)
                for b in range(banks[n]):
                    if q >= 2:
                        pe.wait_ge(y_copied, q - 1)
                    nc.tensor.matmul(y_ps[q % 2][:, :], wp[:, c, :], diff[:, n % 2, b * BANK:(b + 1) * BANK],
                                     start=True, stop=True).then_inc(y_ready, 1)
                    q += 1

        @block.scalar
        def _(act):
            act.wait_ge(tabs_in, 48)
            q = 0
            for n, (g, c) in enumerate(jobs):
                if n >= 2:
                    act.wait_ge(stored[n % 2], 16 * (n // 2))
                for b in range(banks[n]):
                    act.wait_ge(y_ready, q + 1)
                    nc.scalar.activation(out[:, n % 2, b * BANK:(b + 1) * BANK], y_ps[q % 2][:, :], ACT.Copy,
                                         scale=scale[:, c:c + 1]).then_inc(y_copied, 1)
                    q += 1
                act.wait_ge(y_copied, q)
                act.dma_start(w["s_pool"][c, :, STARTS[g]:STARTS[g] + SEQS[g]],
                              out[:, n % 2, 0:SEQS[g]]).then_inc(stored[n % 2], 16)
            for i in range(2):
                act.wait_ge(stored[i], 16 * len(jobs) // 2)


def out_proj(nc, w, keep):
    BLOCKS = TILES // 2
    SPLIT = TILE0[1] // 2
    WR = 4
    KA = HEADS * VD // P
    with ExitStack() as ctx:
        m = Pools(nc, ctx, "outp")
        wraw = m.sb("wraw", [P, WR, D])
        wh = m.sb("wh", [P, KD, D], F32R)
        wl = m.sb("wl", [P, KD, D], F32R)
        wr = m.sb("wr", [P, KD, E])
        g1 = m.sb("g1", [P, 2, D])
        mix = m.sb("mix", [P, 2, KD, P])
        mh = m.sb("mh", [P, 2, KD, P], F32R)
        ml = m.sb("ml", [P, 2, KD, P], F32R)
        x = m.sb("x", [P, 2, D])
        gated = m.sb("gated", [P, 2, D])
        x1 = m.sb("x1", [P, 2, D])
        xn = m.sb("xn", [P, 2, D])
        junk = m.sb("junk", [P, 2, D])
        ms = m.sb("ms", [P, 2])
        eps = m.sb("eps", [P, 1])
        h2 = m.sb("h2", [P, KD, 2 * P])
        o_ps = m.ps("o_ps", [P, 2, 2, BANK])
        x_ps = m.ps("x_ps", [P, 2, BANK])
        l_ps = m.ps("l_ps")
        eps_set = m.sem("eps_set")
        w_in = [m.sem(f"w_in{i}") for i in range(WR)]
        w_hi_done = m.sem("w_hi_done")
        w_lo_done = m.sem("w_lo_done")
        tabs_in = m.sem("tabs_in")
        mix_in = [m.sem(f"mix_in{i}") for i in range(2)]
        x_in = [m.sem(f"x_in{i}") for i in range(2)]
        mix_hi_done = m.sem("mix_hi_done")
        mix_lo_done = m.sem("mix_lo_done")
        o_ready = m.sem("o_ready")
        gate_done = m.sem("gate_done")
        x1_done = m.sem("x1_done")
        squared = m.sem("squared")
        std_done = m.sem("std_done")
        rstd_done = m.sem("rstd_done")
        xn_done = m.sem("xn_done")
        x1_stored = [m.sem(f"x1_stored{i}") for i in range(2)]
        xn_stored = [m.sem(f"xn_stored{i}") for i in range(2)]
        xn_turned = m.sem("xn_turned")
        h2_done = m.sem("h2_done")
        logits_ready = m.sem("logits_ready")
        logits_copied = m.sem("logits_copied")
        block = ctx.enter_context(nc.Block())

        def over_blocks(eng, body):
            body(0, 0, None)
            body(1, 0, 0)
            with eng.Fori(2, SPLIT) as r:
                body(r, 0, 0)
            body(SPLIT, 1, 0)
            with eng.Fori(SPLIT + 1, BLOCKS - 1) as r:
                body(r, 1, 1)
            body(BLOCKS - 1, 1, 1, last=True)

        @block.sync
        def _(sp):
            def body(r, g, before, last=False):
                for u in range(2):
                    if before is not None:
                        sp.wait_ge(mix_lo_done, 2 * r - (1 - u))
                    sp.dma_start(mix[:, u, 0:KA], w["s_att"][:, bass.ds(r * 2 * P + u * P, P)]
                                 .rearrange("(c p) t -> p c t", p=P)).then_inc(mix_in[u], 16)
                    sp.dma_start(mix[:, u, KA:KD], w["s_pool"][:, :, bass.ds(r * 2 * P + u * P, P)]
                                 .rearrange("c p t -> p c t")).then_inc(mix_in[u], 16)
                for u in range(2):
                    if before is not None:
                        sp.wait_ge(x1_done, 2 * r - (1 - u))
                    src = w[("x_prompt", "x_sample")[g]][0]
                    sp.dma_start(x[:, u, :], src[bass.ds(r * 2 * P + u * P - STARTS[g], P), :]).then_inc(x_in[u], 16)

            for k in range(WR):
                sp.dma_start(wraw[:, k], w["w_out"][0][k * P:(k + 1) * P, :]).then_inc(w_in[k], 16)
            sp.dma_start(wr[:], w["w_router"][0].rearrange("(k p) e -> p k e", p=P)).then_inc(tabs_in, 16)
            for g in range(2):
                sp.dma_start(g1[:, g, :], w["s_gates"][0, g * D:(g + 1) * D].partition_broadcast(P)).then_inc(tabs_in, 16)
            for k in range(WR, KD):
                sp.wait_ge(w_lo_done, k - WR + 1)
                sp.dma_start(wraw[:, k % WR], w["w_out"][0][k * P:(k + 1) * P, :]).then_inc(w_in[k % WR], 16)
            over_blocks(sp, body)

        @block.gpsimd
        def _(pool):
            m.clear_last(pool)
            def body(r, g, before, last=False):
                for u in range(2):
                    pool.wait_ge(gate_done, 2 * r + u + 1)
                    pool.wait_ge(x_in[u], 16 * r + 16)
                    if before is not None:
                        pool.wait_ge(xn_done, 2 * r)
                        pool.wait_ge(x1_stored[u], 16 * r)
                    nc.gpsimd.tensor_tensor(x1[:, u, :], gated[:, u, :], x[:, u, :], ALU.add).then_inc(x1_done, 1)

            over_blocks(pool, body)

        @block.tensor
        def _(pe):
            def turn_xn(r):
                pe.wait_ge(xn_done, 2 * r + 2)
                for c in range(KD // 2):
                    if c >= 2:
                        pe.wait_ge(h2_done, KD * r + 2 * (c - 1))
                    for k in (2 * c, 2 * c + 1):
                        for u in range(2):
                            mm = nc.tensor.transpose(x_ps[:, c % 2, (k % 2 * 2 + u) * P:(k % 2 * 2 + u + 1) * P],
                                                     xn[:, u, k * P:(k + 1) * P], keep["ident"][:, :])
                    mm.then_inc(xn_turned, 1)

            def route(r):
                if isinstance(r, int) and r == 0:
                    pe.wait_ge(tabs_in, 48)
                pe.wait_ge(h2_done, KD * r + KD)
                for k in range(KD):
                    mm = nc.tensor.matmul(l_ps[0:E, 0:2 * P], wr[:, k, :], h2[:, k, :],
                                          start=(k == 0), stop=(k == KD - 1))
                mm.then_inc(logits_ready, 1)

            def body(r, g, before, last=False):
                for u in range(2):
                    pe.wait_ge(mix_lo_done, 2 * r + u + 1)
                    if before is not None:
                        pe.wait_ge(gate_done, 2 * r - (1 - u))
                    for c in range(2):
                        out = o_ps[:, u, c, :]
                        for k in range(KD):
                            if before is None and u == 0 and c == 0:
                                pe.wait_ge(w_lo_done, k + 1)
                            hi, lo = wh[:, k, c * BANK:(c + 1) * BANK], wl[:, k, c * BANK:(c + 1) * BANK]
                            nc.tensor.matmul(out, mh[:, u, k, :], hi, start=(k == 0), stop=False)
                            nc.tensor.matmul(out, mh[:, u, k, :], lo, start=False, stop=False)
                            mm = nc.tensor.matmul(out, ml[:, u, k, :], hi, start=False, stop=(k == KD - 1))
                    mm.then_inc(o_ready, 1)
                    if before is not None:
                        if u == 0:
                            turn_xn(r - 1)
                        else:
                            if not isinstance(r, int) or r >= 2:
                                pe.wait_ge(logits_copied, r - 1)
                            route(r - 1)

            over_blocks(pe, body)
            turn_xn(BLOCKS - 1)
            pe.wait_ge(logits_copied, BLOCKS - 1)
            route(BLOCKS - 1)

        @block.scalar
        def _(act):
            def mix_high(r, u, first):
                act.wait_ge(mix_in[u], 32 * r + 32)
                if not first:
                    act.wait_ge(o_ready, 2 * r - (1 - u))
                nc.scalar.activation(mh[:, u], mix[:, u], ACT.Copy).then_inc(mix_hi_done, 1)

            def modulate(r, g):
                for u in range(2):
                    act.wait_ge(xn_done, 2 * r + u + 1)
                    act.dma_start(w["s_xn"][bass.ds(r * 2 * P + u * P, P), :], xn[:, u, :]).then_inc(xn_stored[u], 16)
                for k in range(KD):
                    act.wait_ge(xn_turned, KD // 2 * r + k // 2 + 1)
                    if k == 0 and (not isinstance(r, int) or r >= 1):
                        act.wait_ge(logits_ready, r)
                    nc.scalar.activation(h2[:, k, :], x_ps[:, k // 2 % 2, k % 2 * 2 * P:(k % 2 + 1) * 2 * P],
                                         ACT.Identity, bias=keep["modc"][:, g, 3 * KD + k:3 * KD + k + 1],
                                         scale=keep["modc"][:, g, 4 * KD + k:4 * KD + k + 1]).then_inc(h2_done, 1)

            def body(r, g, before, last=False):
                mix_high(r, 1, before is None)
                if before is not None:
                    modulate(r - 1, before)
                for u in range(2):
                    act.wait_ge(x1_done, 2 * r + u + 1)
                    if before is not None:
                        act.wait_ge(squared, 2 * r - (1 - u))
                        act.wait_ge(xn_done, 2 * r)
                    nc.scalar.activation(junk[:, u, :], x1[:, u, :], ACT.Square, scale=float(D) ** -0.5,
                                         accum_out=ms[:, u:u + 1]).then_inc(squared, 1)
                    if u == 0 and not last:
                        mix_high(r + 1, 0, False)
                for u in range(2):
                    act.dma_start(w["s_x"][bass.ds(r * 2 * P + u * P, P), :], x1[:, u, :]).then_inc(x1_stored[u], 16)
                act.wait_ge(squared, 2 * r + 2)
                nc.scalar.activation(ms[:, :], ms[:, :], ACT.Sqrt, bias=eps[:, 0:1]).then_inc(std_done, 1)

            act.wait_ge(eps_set, 1)
            for k in range(KD):
                act.wait_ge(w_in[k % WR], 16 * (k // WR + 1))
                nc.scalar.activation(wh[:, k, :], wraw[:, k % WR, :], ACT.Copy).then_inc(w_hi_done, 1)
            mix_high(0, 0, True)
            over_blocks(act, body)
            modulate(BLOCKS - 1, 1)
            for u in range(2):
                act.wait_ge(x1_stored[u], 16 * BLOCKS)
                act.wait_ge(xn_stored[u], 16 * BLOCKS)

        @block.vector
        def _(dve):
            def copy_logits(r):
                dve.wait_ge(logits_ready, r + 1)
                nc.vector.tensor_copy(keep["logits"][:, bass.ds(r * 2 * P, 2 * P)],
                                      l_ps[0:E, 0:2 * P]).then_inc(logits_copied, 1)

            def body(r, g, before, last=False):
                mix_low(r, 1, before is None)
                for u in range(2):
                    dve.wait_ge(o_ready, 2 * r + u + 1)
                    if before is not None:
                        dve.wait_ge(x1_done, 2 * r - (1 - u))
                    nc.vector.tensor_tensor(gated[:, u, :], o_ps[:, u].rearrange("p c n -> p (c n)"), g1[:, g, :],
                                            ALU.mult).then_inc(gate_done, 1)
                    if u == 0:
                        if not last:
                            mix_low(r + 1, 0, False)
                if before is not None:
                    copy_logits(r - 1)
                dve.wait_ge(std_done, r + 1)
                nc.vector.reciprocal(ms[:, :], ms[:, :]).then_inc(rstd_done, 1)
                dve.wait_ge(rstd_done, r + 1)
                for u in range(2):
                    if before is not None:
                        dve.wait_ge(xn_stored[u], 16 * r)
                        dve.wait_ge(xn_turned, KD // 2 * r)
                    nc.vector.tensor_scalar(xn[:, u, :], x1[:, u, :], ms[:, u:u + 1], None,
                                            ALU.mult).then_inc(xn_done, 1)

            def mix_low(r, u, first):
                dve.wait_ge(mix_hi_done, 2 * r + u + 1)
                if not first:
                    dve.wait_ge(o_ready, 2 * r - (1 - u))
                nc.vector.tensor_tensor(ml[:, u], mix[:, u], mh[:, u].bitcast(F32),
                                        ALU.subtract).then_inc(mix_lo_done, 1)

            nc.vector.memset(eps[:], EPS).then_inc(eps_set, 1)
            for k in range(KD):
                dve.wait_ge(w_hi_done, k + 1)
                nc.vector.tensor_tensor(wl[:, k, :], wraw[:, k % WR, :], wh[:, k, :].bitcast(F32),
                                        ALU.subtract).then_inc(w_lo_done, 1)
            mix_low(0, 0, True)
            dve.wait_ge(tabs_in, 48)
            over_blocks(dve, body)
            copy_logits(BLOCKS - 1)


def selection(nc, w, keep):
    BITS = 30
    N = TILES * E
    NP = TILE0[1]
    SLOTS = sum(CT)
    V = 5
    groups = ((0, NP), (NP, TILES))
    with ExitStack() as ctx:
        m = Pools(nc, ctx, "sel")
        aff = m.sb("aff", [P, TILES, E])
        red = m.sb("red", [P, TILES])
        one = m.sb("one", [P, P], BF16)
        two = m.sb("two", [P, P], BF16)
        below = m.sb("below", [P, P], BF16)
        iota = m.sb("iota", [P, max(CAPS)], BF16)
        first = m.sb("first", [P, E, TILES])
        ids = m.sb("ids", [P, TILES, 2], BF16)
        bit = m.sb("bit", [P, 2, E], I32)
        thr = m.sb("thr", [P, 2, E])
        cand = m.sb("cand", [P, 2, E])
        count = m.sb("count", [P, 2, E])
        need = m.sb("need", [P, 2, E])
        mark = m.sb("mark", [P, TILES, E], BF16)
        more = m.sb("more", [P, TILES, E], BF16)
        total = m.sb("total", [P, E, TILES])
        scan = m.sb("scan", [P, E, TILES])
        rank = m.sb("rank", [P, TILES, E])
        slot = m.sb("slot", [P, TILES, E])
        rest = m.sb("rest", [P, 2, TILES, E])
        vals = m.sb("vals", [P, TILES, E, V], BF16)
        hot = m.sb("hot", [P, 2, TILES, max(CAPS)], BF16)
        got = m.sb("got", [P, E, SLOTS, V])
        l_ps = m.ps("l_ps")
        c_ps = m.ps("c_ps")
        r_ps = m.ps("r_ps")
        g_ps = [m.ps(f"g_ps{i}") for i in range(2)]
        tabs_in = m.sem("tabs_in")
        turned = m.sem("turned")
        step_done = m.sem("step_done")
        exp_done = m.sem("exp_done")
        bit_step = m.sem("bit_step")
        marked = m.sem("marked")
        counted = m.sem("counted")
        ranked = m.sem("ranked")
        summed = m.sem("summed")
        hot_done = m.sem("hot_done")
        moved = m.sem("moved")
        got_done = m.sem("got_done")
        block = ctx.enter_context(nc.Block())

        @block.gpsimd
        def _(pool):
            m.clear_last(pool)

        @block.sync
        def _(sp):
            for dst, src in ((one[:, :], w["k_one"]), (two[:, :], w["k_two"]), (below[:, :], w["k_below"]),
                             (iota[:, :], w["k_iota"].partition_broadcast(P)),
                             (first[:].rearrange("p e t -> p (e t)"), w["k_first"].partition_broadcast(P)),
                             (ids[:].rearrange("p t v -> p (t v)"), w["k_ids"])):
                sp.dma_start(dst, src).then_inc(tabs_in, 16)

        def tiles_last(x):
            return x.rearrange("p t e -> p e t")

        @block.vector
        def _(dve):
            step = sequence(step_done)

            def then(instruction):
                dve.wait_ge(step_done, step(instruction))

            dve.wait_ge(turned, 1)
            then(nc.vector.tensor_copy(aff[:].rearrange("p t e -> p (t e)"), l_ps[:, 0:N]))
            then(nc.vector.tensor_reduce(red[:, :], aff[:], AX, ALU.max))
            wide = red[:, :].unsqueeze(2).broadcast_to([P, TILES, E])
            step(nc.vector.tensor_tensor(aff[:], aff[:], wide, ALU.subtract))
            dve.wait_ge(exp_done, 1)
            then(nc.vector.tensor_reduce(red[:, :], aff[:], AX, ALU.add))
            then(nc.vector.reciprocal(red[:, :], red[:, :]))
            then(nc.vector.tensor_tensor(aff[:], aff[:], wide, ALU.mult))
            dve.wait_ge(tabs_in, 96)
            then(nc.vector.tensor_copy(vals[:, :, :, 2], aff[:]))
            then(nc.vector.tensor_tensor(rest[:, 0], aff[:], vals[:, :, :, 2], ALU.subtract))
            then(nc.vector.tensor_copy(vals[:, :, :, 3], rest[:, 0]))
            then(nc.vector.tensor_tensor(rest[:, 1], rest[:, 0], vals[:, :, :, 3], ALU.subtract))
            then(nc.vector.tensor_copy(vals[:, :, :, 4], rest[:, 1]))
            for v in range(2):
                then(nc.vector.tensor_copy(vals[:, :, :, v], ids[:, :, v].unsqueeze(2).broadcast_to([P, TILES, E])))
            then(nc.vector.memset(bit[:], 1 << (BITS - 1)))
            then(nc.vector.memset(thr[:], 0.0))
            with dve.Fori(0, BITS) as i:
                nc.vector.tensor_tensor(cand[:].bitcast(I32), thr[:].bitcast(I32), bit[:],
                                        ALU.bitwise_or).then_inc(bit_step, 1)
                dve.wait_ge(bit_step, i * 5 + 1)
                for a, b in groups:
                    c = cand[:, int(a > 0)].unsqueeze(1).broadcast_to([P, b - a, E])
                    nc.vector.tensor_tensor(mark[:, a:b], aff[:, a:b], c, ALU.is_ge).then_inc(marked, 1)
                nc.vector.tensor_scalar(bit[:], bit[:], 1, None, ALU.logical_shift_right).then_inc(bit_step, 1)
                dve.wait_ge(counted, i + 1)
                for g, (a, b) in enumerate(groups):
                    nc.vector.tensor_reduce(count[:, g], c_ps[:, a * E:b * E].rearrange("p (t e) -> p e t", e=E),
                                            AX, ALU.add).then_inc(bit_step, 1)
                dve.wait_ge(bit_step, i * 5 + 4)
                nc.vector.scalar_tensor_tensor(cand[:], count[:], float(CAPS[1]), cand[:], ALU.is_ge,
                                               ALU.mult).then_inc(bit_step, 1)
                dve.wait_ge(bit_step, i * 5 + 5)
                nc.vector.tensor_tensor(thr[:], thr[:], cand[:], ALU.max).then_inc(summed, 1)
                dve.wait_ge(summed, i + 1)
            for g, (a, b) in enumerate(groups):
                t = thr[:, g].unsqueeze(1).broadcast_to([P, b - a, E])
                nc.vector.tensor_tensor(mark[:, a:b], aff[:, a:b], t, ALU.is_equal).then_inc(marked, 1)
                nc.vector.tensor_tensor(more[:, a:b], aff[:, a:b], t, ALU.is_gt).then_inc(marked, 1)

            def ranks(n):
                dve.wait_ge(ranked, n)
                then(nc.vector.tensor_copy(total[:], c_ps[:, 0:N].rearrange("p (t e) -> p e t", e=E)))
                then(nc.vector.tensor_tensor_scan(scan[:].rearrange("p e t -> p (e t)"),
                                                  first[:].rearrange("p e t -> p (e t)"),
                                                  total[:].rearrange("p e t -> p (e t)"), 0.0, ALU.mult, ALU.add))
                then(nc.vector.tensor_tensor(scan[:], scan[:], total[:], ALU.subtract))
                then(nc.vector.tensor_tensor(rank[:], r_ps[:, 0:N].rearrange("p (t e) -> p t e", e=E),
                                             scan[:].rearrange("p e t -> p t e"), ALU.add))

            ranks(1)
            dve.wait_ge(ranked, 2)
            for g, (a, b) in enumerate(groups):
                then(nc.vector.tensor_reduce(count[:, g], g_ps[0][:, a * E:b * E].rearrange("p (t e) -> p e t", e=E),
                                             AX, ALU.add))
                then(nc.vector.tensor_scalar(need[:, g], count[:, g], -1.0, float(CAPS[g]), ALU.mult, ALU.add))
                left = need[:, g].unsqueeze(1).broadcast_to([P, b - a, E])
                then(nc.vector.tensor_tensor(rank[:, a:b], rank[:, a:b], left, ALU.is_lt))
            then(nc.vector.tensor_tensor(rank[:], rank[:], mark[:], ALU.mult))
            nc.vector.tensor_tensor(more[:], more[:], rank[:], ALU.add).then_inc(marked, 1)
            dve.wait_ge(marked, 2 * BITS + 5)
            ranks(3)
            then(nc.vector.tensor_scalar(rank[:], rank[:], 1.0, None, ALU.add))
            then(nc.vector.tensor_tensor(rank[:], rank[:], more[:], ALU.mult))
            then(nc.vector.tensor_scalar(slot[:], rank[:], -1.0, None, ALU.add))
            for e in range(E):
                if e >= 2:
                    dve.wait_ge(moved, e - 1)
                for t in range(TILES):
                    cap = CAPS[int(t >= NP)]
                    mk = nc.vector.tensor_scalar(hot[:, e % 2, t, 0:cap], iota[:, 0:cap], slot[:, t, e:e + 1], None,
                                                 ALU.is_equal)
                mk.then_inc(hot_done, 1)
                if e >= 1:
                    dve.wait_ge(moved, e)
                    nc.vector.tensor_copy(got[:, e - 1].rearrange("p s v -> p (s v)"),
                                          g_ps[(e - 1) % 2][:, 0:SLOTS * V]).then_inc(got_done, 1)
            dve.wait_ge(moved, E)
            nc.vector.tensor_copy(got[:, E - 1].rearrange("p s v -> p (s v)"),
                                  g_ps[(E - 1) % 2][:, 0:SLOTS * V]).then_inc(got_done, 1)
            dve.wait_ge(got_done, E)
            then(nc.vector.tensor_tensor(keep["index"][:], got[:, :, :, 0], got[:, :, :, 1], ALU.add))
            then(nc.vector.tensor_tensor(got[:, :, :, 0], got[:, :, :, 2], got[:, :, :, 3], ALU.add))
            then(nc.vector.tensor_tensor(keep["gate"][:], got[:, :, :, 0], got[:, :, :, 4], ALU.add))

        @block.scalar
        def _(act):
            act.wait_ge(step_done, 3)
            nc.scalar.activation(aff[:], aff[:], ACT.Exp).then_inc(exp_done, 1)

        @block.tensor
        def _(pe):
            for n in range(TILES):
                mm = nc.tensor.transpose(l_ps[:, n * E:(n + 1) * E], keep["logits"][:, n * P:(n + 1) * P],
                                         keep["ident"][0:E, 0:E])
            mm.then_inc(turned, 1)
            pe.wait_ge(tabs_in, 96)
            with pe.Fori(0, BITS) as i:
                for g, ((a, b), weight) in enumerate(zip(groups, (two, one))):
                    pe.wait_ge(marked, 2 * i + g + 1)
                    if g == 0:
                        pe.wait_ge(bit_step, 5 * i + 1)
                    mm = nc.tensor.matmul(c_ps[:, a * E:b * E], weight[:, :],
                                          mark[:, a:b].rearrange("p t e -> p (t e)"), start=True, stop=True)
                mm.then_inc(counted, 1)

            def ranks(x):
                flat = x[:].rearrange("p t e -> p (t e)")
                nc.tensor.matmul(c_ps[:, 0:N], one[:, :], flat, start=True, stop=True)
                nc.tensor.matmul(r_ps[:, 0:N], below[:, :], flat, start=True, stop=True).then_inc(ranked, 1)

            pe.wait_ge(marked, 2 * BITS + 4)
            ranks(mark)
            nc.tensor.matmul(g_ps[0][:, 0:N], one[:, :], more[:].rearrange("p t e -> p (t e)"),
                             start=True, stop=True).then_inc(ranked, 1)
            pe.wait_ge(marked, 2 * BITS + 5)
            ranks(more)
            for e in range(E):
                pe.wait_ge(hot_done, e + 1)
                if e >= 2:
                    pe.wait_ge(got_done, e - 1)
                for s in range(SLOTS):
                    g = int(s >= CT[0])
                    a, b = groups[g]
                    c = s - g * CT[0]
                    for t in range(a, b):
                        mm = nc.tensor.matmul(g_ps[e % 2][:, s * V:(s + 1) * V], hot[:, e % 2, t, c * P:(c + 1) * P],
                                              vals[:, t, e, :], start=(t == a), stop=(t == b - 1))
                mm.then_inc(moved, 1)


def experts(nc, w, keep):
    CHUNKS = 6
    GU = 4
    PIECES = 4
    SLOTS = sum(CT)
    C = SLOTS * P
    NP = CT[0] * P
    KP = KD // PIECES
    TURNS = ((0, 1), (2,), (3,), (4,), (5, 6), (7,))
    with ExitStack() as ctx:
        m = Pools(nc, ctx, "moe")
        raw = m.sb("raw", [P, 2, KD, BANK])
        wh = m.sb("wh", [P, 2, KD, BANK], F32R)
        wl = m.sb("wl", [P, 2, KD, BANK], F32R)
        rows = m.sb("rows", [P, SLOTS, D])
        xf = m.sb("xf", [P, 2, C])
        xh = m.sb("xh", [P, KD, C], F32R)
        xl = m.sb("xl", [P, KD, C], F32R)
        silu = m.sb("silu", [P, 2, C])
        hf = m.sb("hf", [P, 2, C])
        hh = m.sb("hh", [P, KF, C], F32R)
        hl = m.sb("hl", [P, KF, C], F32R)
        ye = m.sb("ye", [P, SLOTS, D])
        g2 = m.sb("g2", [P, 2, D])
        to_gather = m.sb("to_gather", [P, SLOTS], I32)
        to_add = m.sb("to_add", [P, SLOTS], I32)
        a_ps = [m.ps(f"a_ps{i}") for i in range(2)]
        u_ps = [m.ps(f"u_ps{i}") for i in range(2)]
        t_ps = [m.ps(f"t_ps{i}") for i in range(2)]
        d_ps = [m.ps(f"d_ps{i}") for i in range(2)]
        g2_in = m.sem("g2_in")
        raw_in = [m.sem(f"raw_in{i}") for i in range(2)]
        w_hi_done = m.sem("w_hi_done")
        w_lo_done = m.sem("w_lo_done")
        gather_index = m.sem("gather_index")
        add_index = m.sem("add_index")
        gathered = [m.sem(f"gathered{i}") for i in range(SLOTS)]
        pool_waited = m.sem("pool_waited")
        sp_waited = m.sem("sp_waited")
        turned = m.sem("turned")
        x_full = m.sem("x_full")
        x_hi_done = m.sem("x_hi_done")
        x_lo_done = m.sem("x_lo_done")
        gu_ready = m.sem("gu_ready")
        silu_done = m.sem("silu_done")
        h_full = m.sem("h_full")
        h_hi_done = m.sem("h_hi_done")
        h_lo_done = m.sem("h_lo_done")
        d_ready = m.sem("d_ready")
        ye_done = m.sem("ye_done")
        added = [m.sem(f"added{i}") for i in range(SLOTS)]
        block = ctx.enter_context(nc.Block())
        DOWNS = 2 * SLOTS

        def over_experts(eng, body):
            body(0, False)
            with eng.Fori(1, E - 1) as e:
                body(e, False)
            body(E - 1, True)

        def is_first(e):
            return isinstance(e, int) and e == 0

        @block.sync
        def _(sp):
            def load(e, c):
                s = c % 2
                if c < GU:
                    for i, name in enumerate(("w_gate", "w_up")):
                        src = w[name][0][bass.ds(e, 1), :, c * 256:(c + 1) * 256]
                        sp.dma_start(raw[:, s, :, i * 256:(i + 1) * 256],
                                     src.rearrange("o (k p) n -> p (o k) n", p=P)).then_inc(raw_in[s], 16)
                else:
                    src = w["w_down"][0][bass.ds(e, 1), :, (c - GU) * BANK:(c - GU + 1) * BANK]
                    src = src.rearrange("o (k p) n -> p (o k) n", p=P)
                    for i in range(2):
                        half = slice(i * KD // 2, (i + 1) * KD // 2)
                        sp.dma_start(raw[:, s, half, :], src[:, half, :]).then_inc(raw_in[s], 16)

            def body(e, last):
                after = e + 1
                for c in range(CHUNKS - 1 if last else CHUNKS):
                    if c >= 1 or not is_first(e):
                        sp.wait_ge(w_lo_done, (e * CHUNKS + c) * PIECES)
                        sp.sem_inc(sp_waited, 1)
                    load(*((e, c + 1) if c + 1 < CHUNKS else (after, 0)))

            for g in range(2):
                at = (2 + g) * D
                sp.dma_start(g2[:, g, :], w["s_gates"][0, at:at + D].partition_broadcast(P)).then_inc(g2_in, 16)
            load(0, 0)
            over_experts(sp, body)

        @block.gpsimd
        def _(pool):
            m.clear_last(pool)

            def gather(e):
                pool.wait_ge(gather_index, e + 1)
                pool.sem_inc(pool_waited, 1)
                for s in range(SLOTS):
                    pool.indirect_dma_start(out=rows[:, s, :], out_offset=None, in_=w["s_xn"],
                                            in_offset=bass.IndirectOffsetOnAxis(ap=to_gather[:, s:s + 1], axis=0)
                                            ).then_inc(gathered[s], 16)

            def body(e, last):
                if not last:
                    pool.wait_ge(turned, (e + 1) * KD)
                    gather(e + 1)
                pool.wait_ge(ye_done, (e + 1) * DOWNS)
                pool.wait_ge(add_index, e + 1)
                for s in range(SLOTS):
                    if not is_first(e):
                        pool.wait_ge(added[s], e * 16)
                pool.sem_inc(pool_waited, 1)
                for s in range(SLOTS):
                    pool.indirect_dma_start(out=w["s_x"],
                                            out_offset=bass.IndirectOffsetOnAxis(ap=to_add[:, s:s + 1], axis=0),
                                            in_=ye[:, s, :], in_offset=None, compute_op=ALU.add).then_inc(added[s], 16)

            gather(0)
            over_experts(pool, body)
            for s in range(SLOTS):
                pool.wait_ge(added[s], E * 16)

        @block.tensor
        def _(pe):
            def turn(e, k):
                if k == 0:
                    for s in range(SLOTS):
                        pe.wait_ge(gathered[s], (e + 1) * 16)
                if not (isinstance(e, int) and e == 0 and k < 2):
                    pe.wait_ge(x_full, (e * KD + k - 1) * 2)
                for s in range(SLOTS):
                    mm = nc.tensor.transpose(t_ps[k % 2][:, s * P:(s + 1) * P], rows[:, s, k * P:(k + 1) * P],
                                             keep["ident"][:, :])
                mm.then_inc(turned, 1)

            def body(e, last):
                for c in range(GU):
                    pe.wait_ge(w_lo_done, (e * CHUNKS + c + 1) * PIECES)
                    for i in range(2):
                        f = 2 * c + i
                        if c == 0 and i == 0:
                            pe.wait_ge(x_lo_done, (e + 1) * KD)
                        if c > 0:
                            pe.wait_ge(h_full, e * KF + f - 1)
                        for ps, col in ((a_ps, i * P), (u_ps, 256 + i * P)):
                            for k in range(KD):
                                hi, lo = wh[:, c % 2, k, col:col + P], wl[:, c % 2, k, col:col + P]
                                out = ps[i][:, 0:C]
                                nc.tensor.matmul(out, hi, xh[:, k, :], start=(k == 0), stop=False)
                                nc.tensor.matmul(out, hi, xl[:, k, :], start=False, stop=False)
                                mm = nc.tensor.matmul(out, lo, xh[:, k, :], start=False, stop=(k == KD - 1))
                        mm.then_inc(gu_ready, 1)
                for n in range(2):
                    c = GU + n
                    pe.wait_ge(w_lo_done, (e * CHUNKS + c + 1) * PIECES)
                    for s in range(SLOTS):
                        j = n * SLOTS + s
                        if not last:
                            for k in TURNS[j]:
                                turn(e + 1, k)
                        if j == 0:
                            pe.wait_ge(h_lo_done, (e + 1) * KF)
                        if j >= 2:
                            pe.wait_ge(ye_done, e * DOWNS + j - 1)
                        out = d_ps[j % 2][:, :]
                        for k in range(KF):
                            h_hi, h_lo = hh[:, k, s * P:(s + 1) * P], hl[:, k, s * P:(s + 1) * P]
                            nc.tensor.matmul(out, h_hi, wh[:, c % 2, k, :], start=(k == 0), stop=False)
                            nc.tensor.matmul(out, h_hi, wl[:, c % 2, k, :], start=False, stop=False)
                            mm = nc.tensor.matmul(out, h_lo, wh[:, c % 2, k, :], start=False, stop=(k == KF - 1))
                        mm.then_inc(d_ready, 1)

            for k in range(KD):
                turn(0, k)
            over_experts(pe, body)

        def chunk_is_used(eng, e, c):
            if c < GU:
                eng.wait_ge(gu_ready, e * KF + 2 * (c + 1))
            else:
                eng.wait_ge(d_ready, e * DOWNS + (c - GU + 1) * SLOTS)

        @block.scalar
        def _(act):
            def split(e, c):
                s = c % 2
                act.wait_ge(raw_in[s], (e * (CHUNKS // 2) + c // 2 + 1) * 32)
                for i in range(PIECES):
                    part = slice(i * KP, (i + 1) * KP)
                    nc.scalar.activation(wh[:, s, part, :], raw[:, s, part, :], ACT.Copy).then_inc(w_hi_done, 1)

            def modulate(e, k):
                act.wait_ge(turned, e * KD + k + 1)
                if not (isinstance(e, int) and e == 0 and k < 2):
                    act.wait_ge(x_lo_done, e * KD + k - 1)
                for g, cols in enumerate((slice(0, NP), slice(NP, C))):
                    nc.scalar.activation(xf[:, k % 2, cols], t_ps[k % 2][:, cols], ACT.Identity,
                                         bias=keep["modc"][:, g, 3 * KD + k:3 * KD + k + 1],
                                         scale=keep["modc"][:, g, 4 * KD + k:4 * KD + k + 1]).then_inc(x_full, 1)
                act.wait_ge(x_full, (e * KD + k + 1) * 2)
                nc.scalar.activation(xh[:, k, :], xf[:, k % 2, :], ACT.Copy).then_inc(x_hi_done, 1)

            def body(e, last):
                for c in range(CHUNKS):
                    nxt = (e, c + 1) if c + 1 < CHUNKS else (e + 1, 0)
                    if c + 1 < CHUNKS or not last:
                        if c >= 1:
                            chunk_is_used(act, e, c - 1)
                        elif not is_first(e):
                            act.wait_ge(d_ready, e * DOWNS)
                        split(*nxt)
                    if c < GU:
                        for i in range(2):
                            f = 2 * c + i
                            act.wait_ge(gu_ready, e * KF + f + 1)
                            nc.scalar.activation(silu[:, i, :], a_ps[i][:, 0:C], ACT.Silu).then_inc(silu_done, 1)
                            act.wait_ge(h_full, e * KF + f + 1)
                            nc.scalar.activation(hh[:, f, :], hf[:, i, :], ACT.Copy).then_inc(h_hi_done, 1)
                    elif not last:
                        for j in range((c - GU) * SLOTS, (c - GU + 1) * SLOTS):
                            for k in TURNS[j]:
                                modulate(e + 1, k)

            split(0, 0)
            for k in range(KD):
                modulate(0, k)
            over_experts(act, body)

        @block.vector
        def _(dve):
            def split(e, c):
                s = c % 2
                for i in range(PIECES):
                    part = slice(i * KP, (i + 1) * KP)
                    dve.wait_ge(w_hi_done, (e * CHUNKS + c) * PIECES + i + 1)
                    nc.vector.tensor_tensor(wl[:, s, part, :], raw[:, s, part, :], wh[:, s, part, :].bitcast(F32),
                                            ALU.subtract).then_inc(w_lo_done, 1)

            def x_low(e, k):
                dve.wait_ge(x_hi_done, e * KD + k + 1)
                nc.vector.tensor_tensor(xl[:, k, :], xf[:, k % 2, :], xh[:, k, :].bitcast(F32),
                                        ALU.subtract).then_inc(x_lo_done, 1)

            def index(e, dst, sem):
                nc.vector.tensor_copy(dst[:, :].unsqueeze(1), keep["index"][:, bass.ds(e, 1), :]).then_inc(sem, 1)

            def body(e, last):
                for s in range(SLOTS):
                    if not is_first(e):
                        dve.wait_ge(added[s], e * 16)
                index(e, to_add, add_index)
                if not last:
                    for s in range(SLOTS):
                        dve.wait_ge(gathered[s], (e + 1) * 16)
                    index(e + 1, to_gather, gather_index)
                for c in range(CHUNKS):
                    if c + 1 < CHUNKS or not last:
                        split(*((e, c + 1) if c + 1 < CHUNKS else (e + 1, 0)))
                    if c < GU:
                        for i in range(2):
                            f = 2 * c + i
                            dve.wait_ge(silu_done, e * KF + f + 1)
                            nc.vector.tensor_tensor(hf[:, i, :], u_ps[i][:, 0:C], silu[:, i, :],
                                                    ALU.mult).then_inc(h_full, 1)
                            dve.wait_ge(h_hi_done, e * KF + f + 1)
                            nc.vector.tensor_tensor(hl[:, f, :], hf[:, i, :], hh[:, f, :].bitcast(F32),
                                                    ALU.subtract).then_inc(h_lo_done, 1)
                    else:
                        for s in range(SLOTS):
                            n = c - GU
                            j = n * SLOTS + s
                            if not last:
                                for k in TURNS[j]:
                                    x_low(e + 1, k)
                            dve.wait_ge(d_ready, e * DOWNS + j + 1)
                            nc.vector.scalar_tensor_tensor(ye[:, s, n * BANK:(n + 1) * BANK], d_ps[j % 2][:, :],
                                                           keep["gate"][:, bass.ds(e, 1), s:s + 1].rearrange("p o s -> p (o s)"),
                                                           g2[:, int(s >= CT[0]), n * BANK:(n + 1) * BANK],
                                                           ALU.mult, ALU.mult).then_inc(ye_done, 1)

            index(0, to_gather, gather_index)
            dve.wait_ge(g2_in, 32)
            split(0, 0)
            for k in range(KD):
                x_low(0, k)
            over_experts(dve, body)


def final_norm(nc, w, keep):
    with ExitStack() as ctx:
        m = Pools(nc, ctx, "fin")
        R = 4
        BLOCKS = TILES // 2
        gain = m.sb("gain", [P, D])
        x = m.sb("x", [P, R, 2, D])
        y = m.sb("y", [P, R, 2, D])
        ms = m.sb("ms", [P, TILES])
        eps = m.sb("eps", [P, 1])
        gain_in = m.sem("gain_in")
        eps_set = m.sem("eps_set")
        x_in = [m.sem(f"x_in{i}") for i in range(R)]
        squared = m.sem("squared")
        std_done = m.sem("std_done")
        rstd_done = m.sem("rstd_done")
        y_done = m.sem("y_done")
        stored = [m.sem(f"stored{i}") for i in range(R)]
        block = ctx.enter_context(nc.Block())

        @block.gpsimd
        def _(pool):
            m.clear_last(pool)

        @block.sync
        def _(sp):
            sp.dma_start(gain[:, :], w["final_norm_g"].partition_broadcast(P)).then_inc(gain_in, 16)
            for b in range(BLOCKS):
                if b >= R:
                    sp.wait_ge(y_done, 2 * (b - R + 1))
                src = w["s_x"][b * 2 * P:(b + 1) * 2 * P, :].rearrange("(j p) d -> p j d", p=P)
                sp.dma_start(x[:, b % R], src).then_inc(x_in[b % R], 16)

        def store(act, b):
            act.wait_ge(y_done, 2 * b + 2)
            g = int(2 * b >= TILE0[1])
            row = b * 2 * P - STARTS[g]
            dst = w[("y_prompt", "y_sample")[g]][0][row:row + 2 * P, :].rearrange("(j p) d -> p j d", p=P)
            act.dma_start(dst, y[:, b % R]).then_inc(stored[b % R], 16)

        @block.scalar
        def _(act):
            act.wait_ge(eps_set, 1)
            for b in range(BLOCKS):
                act.wait_ge(x_in[b % R], 16 * (b // R + 1))
                if b >= R:
                    act.wait_ge(stored[b % R], 16 * (b // R))
                for j in range(2):
                    nc.scalar.activation(y[:, b % R, j, :], x[:, b % R, j, :], ACT.Square, scale=float(D) ** -0.5,
                                         accum_out=ms[:, 2 * b + j:2 * b + j + 1]).then_inc(squared, 1)
                act.wait_ge(squared, 2 * b + 2)
                nc.scalar.activation(ms[:, 2 * b:2 * b + 2], ms[:, 2 * b:2 * b + 2], ACT.Sqrt,
                                     bias=eps[:, 0:1]).then_inc(std_done, 1)
                if b >= 1:
                    store(act, b - 1)
            store(act, BLOCKS - 1)
            for i in range(R):
                act.wait_ge(stored[i], 16 * (BLOCKS // R))

        @block.vector
        def _(dve):
            nc.vector.memset(eps[:], EPS).then_inc(eps_set, 1)
            dve.wait_ge(gain_in, 16)
            for b in range(BLOCKS):
                dve.wait_ge(std_done, b + 1)
                nc.vector.reciprocal(ms[:, 2 * b:2 * b + 2], ms[:, 2 * b:2 * b + 2]).then_inc(rstd_done, 1)
                dve.wait_ge(rstd_done, b + 1)
                for j in range(2):
                    nc.vector.scalar_tensor_tensor(y[:, b % R, j, :], x[:, b % R, j, :], ms[:, 2 * b + j:2 * b + j + 1],
                                                   gain[:, :], ALU.mult, ALU.mult).then_inc(y_done, 1)


def build(nc, w):
    keep = {}

    def tile(ctx, name, shape, dt=F32):
        keep[name] = ctx.enter_context(nc.sbuf_tensor(f"keep_{name}", shape, dt))

    with ExitStack() as ctx:
        tile(ctx, "ident", [P, P])
        tile(ctx, "modc", [P, 2, 6 * KD])
        tile(ctx, "index", [P, E, sum(CT)], I32)
        tile(ctx, "gate", [P, E, sum(CT)])
        modulation(nc, w, keep)
        in_proj(nc, w, keep)
        for g in (1, 0):
            attention(nc, w, keep, g)
        pooling(nc, w, keep)
        with ExitStack() as route_ctx:
            tile(route_ctx, "logits", [E, TOKENS])
            out_proj(nc, w, keep)
            selection(nc, w, keep)
        experts(nc, w, keep)
        final_norm(nc, w, keep)


SCRATCH = {
    "s_gates": [1, 4 * D],
    "s_ct": [TILES, P, KC * P],
    "s_krt": [ROPE, TOKENS],
    "s_ut": [DP // P, P, TOKENS],
    "s_att": [HEADS * VD, TOKENS],
    "s_pool": [DP // P, P, TOKENS],
    "s_x": [TOKENS, D],
    "s_xn": [TOKENS, D],
}


def constants():
    inv = np.float32(10000.0) ** (-np.arange(0, ROPE, 2, dtype=np.float32) / np.float32(ROPE))
    out = {"k_ident": np.eye(P, dtype=np.float32)}
    rope = np.zeros((TILES, P, 2, ROPE), np.float32)
    for g in range(2):
        ang = np.arange(SEQS[g], dtype=np.float32)[:, None] * inv[None, :]
        for a, f in enumerate((np.cos, np.sin)):
            t = f(ang).astype(np.float32).reshape(-1, P, ROPE // 2)
            rope[TILE0[g]:TILE0[g] + SEQS[g] // P, :, a] = np.concatenate([t, t], -1)
    out["k_rope"] = rope
    turned = rope[TILE0[1]:].reshape(SEQS[1], 2, ROPE).transpose(1, 2, 0).copy()
    turned[1, :ROPE // 2] *= -1
    out["k_rope_t"] = np.ascontiguousarray(turned.reshape(2 * ROPE, SEQS[1]))
    t = np.arange(SEQS[0])
    edge = []
    for size in WINDOWS:
        count = np.minimum(t + size // 2, SEQS[0]) - np.maximum(t - size // 2, 0)
        inverse = np.float32(1) / count.astype(np.float32)
        edge.append(np.concatenate([inverse[:8], inverse[-8:]]))
    out["k_edge"] = np.concatenate(edge).astype(np.float32)
    bf16 = mybir.dt.np(BF16)
    out["k_one"] = np.ones((P, P), bf16)
    out["k_two"] = np.full((P, P), 2, bf16)
    out["k_below"] = np.triu(np.ones((P, P)), 1).astype(bf16)
    out["k_iota"] = np.arange(max(CAPS)).astype(bf16)
    first = np.ones((E, TILES), np.float32)
    first[:, list(TILE0)] = 0
    out["k_first"] = first.reshape(-1)
    out["k_ids"] = np.stack(np.broadcast_arrays(np.arange(TILES)[None, :] * P, np.arange(P)[:, None]),
                            -1).reshape(P, -1).astype(bf16)
    return out


INPUTS = ["x_prompt", "x_sample", "c_prompt", "c_sample", "w_ada", "b_ada", "w_in", "q_norm_g", "kv_norm_g",
          "w_uq", "w_ukv", "w_pool", "pool_scale", "w_out", "w_router", "w_gate", "w_up", "w_down",
          "final_norm_g"]


def kernel(**inputs):
    import concourse.bacc as bacc
    from concourse.bass_utils import run_bass_kernel_spmd

    nc = bacc.Bacc("TRN2", target_bir_lowering=False, num_devices=1)
    arrays, w = {}, {}
    given = {name: np.ascontiguousarray(inputs[name]) for name in INPUTS}
    for name, a in (*given.items(), *constants().items()):
        arrays[name] = a
        w[name] = nc.dram_tensor(name, list(a.shape), mybir.dt.from_np(a.dtype), kind="ExternalInput").ap()
    for name, shape in SCRATCH.items():
        w[name] = nc.dram_tensor(name, shape, F32, kind="Internal").ap()
    for g, name in enumerate(("y_prompt", "y_sample")):
        w[name] = nc.dram_tensor(name, [1, SEQS[g], D], F32, kind="ExternalOutput").ap()
    build(nc, w)
    r = run_bass_kernel_spmd(nc, [arrays], core_ids=[0])
    return r.results[0]["y_prompt"], r.results[0]["y_sample"]
```
